# Optimizing a Trainium2 kernel written in Bass

```python
import jax, jax.numpy as jnp
from jax import lax
import numpy as np

D_MODEL = 1024
BATCH = 1
SEQ = 512
DEPTH = 2

HEAD_DIM = 64
BLOCK = 128
EPS = 1e-6
FOX_HEADS = 4
MLA_HEADS = 4
MLA_Q_RANK = 256
MLA_KV_RANK = 128
MLA_NOPE_DIM = 64
MLA_ROPE_DIM = 32
MLA_V_DIM = 64
ROPE_THETA = 10000.0
SWA_HEADS = 4
SWA_KV_HEADS = 2
WINDOW = 128
DSA_HEADS = 4
DSA_IDX_HEADS = 8
DSA_IDX_DIM = 32
DSA_TOPK_MAX = 256
N_ALIBI = SWA_HEADS + DSA_HEADS
N_EXPERTS = 16
N_GROUPS = 4
EXPERTS_PER_GROUP = N_EXPERTS // N_GROUPS
TOP_K_EXPERTS = 2
D_EXPERT = 256

IN_SIZES = (
    FOX_HEADS * HEAD_DIM, FOX_HEADS * HEAD_DIM, FOX_HEADS * HEAD_DIM, FOX_HEADS,
    MLA_Q_RANK, MLA_KV_RANK, MLA_ROPE_DIM,
    SWA_HEADS * HEAD_DIM, SWA_KV_HEADS * HEAD_DIM, SWA_KV_HEADS * HEAD_DIM,
    DSA_HEADS * HEAD_DIM, HEAD_DIM, HEAD_DIM,
    DSA_IDX_HEADS * DSA_IDX_DIM, DSA_IDX_DIM, DSA_IDX_HEADS,
)
N_IN = sum(IN_SIZES)
D_MIX = FOX_HEADS * HEAD_DIM + MLA_HEADS * MLA_V_DIM + SWA_HEADS * HEAD_DIM + DSA_HEADS * HEAD_DIM

kernel_name = 'hybrid_fox_mla_swa_dsa_moe_block'

def rmsnorm(x, g):
    xf = x.astype(jnp.float32)
    y = xf * lax.rsqrt(jnp.mean(xf * xf, axis=-1, keepdims=True) + EPS)
    return (y * g.astype(jnp.float32)).astype(x.dtype)

def rope(x, pos):
    half = x.shape[-1] // 2
    inv = ROPE_THETA ** (-jnp.arange(half, dtype=jnp.float32) / half)
    ang = pos.astype(jnp.float32)[:, None] * inv[None, :]
    cos = jnp.cos(ang)[None, :, None, :]
    sin = jnp.sin(ang)[None, :, None, :]
    x1 = x[..., :half].astype(jnp.float32)
    x2 = x[..., half:].astype(jnp.float32)
    return jnp.concatenate([x1 * cos - x2 * sin, x2 * cos + x1 * sin], axis=-1).astype(x.dtype)

def causal_block_attention(q, k, v, log_forget=None):
    B, S, H, Dq = q.shape
    nb = S // BLOCK
    scale = Dq ** -0.5
    key_pos = jnp.arange(S)
    cum = None if log_forget is None else jnp.cumsum(log_forget.astype(jnp.float32), axis=1).swapaxes(1, 2)

    def one_block(i):
        start = i * BLOCK
        q_pos = start + jnp.arange(BLOCK)
        qi = lax.dynamic_slice_in_dim(q, start, BLOCK, axis=1)
        s = jnp.einsum('bqhd,bkhd->bhqk', qi, k, preferred_element_type=jnp.float32) * scale
        if cum is not None:
            ci = lax.dynamic_slice_in_dim(cum, start, BLOCK, axis=2)
            s = s + ci[..., :, None] - cum[..., None, :]
        causal = key_pos[None, :] <= q_pos[:, None]
        s = jnp.where(causal[None, None], s, -jnp.inf)
        p = jax.nn.softmax(s, axis=-1)
        return jnp.einsum('bhqk,bkhd->bqhd', p.astype(v.dtype), v)

    out = lax.map(one_block, jnp.arange(nb))
    return out.swapaxes(0, 1).reshape(B, S, H * v.shape[-1])

def sliding_window_sink_attention(q, k, v, sinks, slopes):
    B, S, Hq, Dh = q.shape
    Hkv = k.shape[2]
    G = Hq // Hkv
    nb = S // BLOCK
    scale = Dh ** -0.5
    qb = q.reshape(B, nb, BLOCK, Hkv, G, Dh)
    kb = k.reshape(B, nb, BLOCK, Hkv, Dh)
    vb = v.reshape(B, nb, BLOCK, Hkv, Dh)
    pad = ((0, 0), (1, 0), (0, 0), (0, 0), (0, 0))
    k_band = jnp.concatenate([jnp.pad(kb, pad)[:, :-1], kb], axis=2)
    v_band = jnp.concatenate([jnp.pad(vb, pad)[:, :-1], vb], axis=2)
    s = jnp.einsum('bnqhgd,bnkhd->bnhgqk', qb, k_band, preferred_element_type=jnp.float32) * scale
    qi = jnp.arange(BLOCK)[:, None]
    kj = jnp.arange(2 * BLOCK)[None, :]
    dist = qi - kj + BLOCK
    key_pos = jnp.arange(nb)[:, None, None] * BLOCK - BLOCK + kj[None]
    valid = (dist >= 0)[None] & (dist < WINDOW)[None] & (key_pos >= 0)
    alibi = slopes.astype(jnp.float32).reshape(Hkv, G, 1, 1) * dist.astype(jnp.float32)
    s = s - alibi
    s = jnp.where(valid[None, :, None, None], s, -jnp.inf)
    sink_col = jnp.broadcast_to(sinks.astype(jnp.float32).reshape(1, 1, Hkv, G, 1, 1), s.shape[:-1] + (1,))
    p = jax.nn.softmax(jnp.concatenate([s, sink_col], axis=-1), axis=-1)[..., :-1]
    out = jnp.einsum('bnhgqk,bnkhd->bnqhgd', p.astype(v.dtype), v_band)
    return out.reshape(B, S, Hq * Dh)

def dsa_attention(q, k, v, q_idx, k_idx, w_idx, slopes):
    B, S, H, Dh = q.shape
    top_k = min(DSA_TOPK_MAX, S // 4)
    nb = S // BLOCK
    scale = Dh ** -0.5
    key_pos = jnp.arange(S)
    w_idx = w_idx.astype(jnp.float32) * (DSA_IDX_HEADS ** -0.5) * (DSA_IDX_DIM ** -0.5)
    gather = jax.vmap(lambda table, idx: table[idx])
    slopes = slopes.astype(jnp.float32)

    def one_block(i):
        start = i * BLOCK
        q_pos = start + jnp.arange(BLOCK)
        qi = lax.dynamic_slice_in_dim(q, start, BLOCK, axis=1)
        qii = lax.dynamic_slice_in_dim(q_idx, start, BLOCK, axis=1)
        wi = lax.dynamic_slice_in_dim(w_idx, start, BLOCK, axis=1)
        idx_logits = jnp.einsum('bqhe,bke->bqhk', qii, k_idx, preferred_element_type=jnp.float32)
        score = jnp.einsum('bqh,bqhk->bqk', wi, jax.nn.relu(idx_logits))
        causal = key_pos[None, :] <= q_pos[:, None]
        score = jnp.where(causal[None], score, -jnp.inf)
        _, sel = lax.top_k(score, top_k)
        k_sel = gather(k, sel)
        v_sel = gather(v, sel)
        logits = jnp.einsum('bqhd,bqkd->bhqk', qi, k_sel, preferred_element_type=jnp.float32) * scale
        dist = (q_pos[None, :, None] - sel).astype(jnp.float32)
        logits = logits - slopes[None, :, None, None] * dist[:, None]
        ok = (sel <= q_pos[None, :, None])[:, None]
        logits = jnp.where(ok, logits, -jnp.inf)
        p = jax.nn.softmax(logits, axis=-1)
        return jnp.einsum('bhqk,bqkd->bqhd', p.astype(v.dtype), v_sel)

    out = lax.map(one_block, jnp.arange(nb))
    return out.swapaxes(0, 1).reshape(B, S, H * Dh)

def hybrid_mixer(h, w_in, b_forget, g_q_mla, w_q_up, g_kv_mla, w_kv_up, sinks, w_out):
    B, S, _ = h.shape
    pos = jnp.arange(S)
    alibi = 2.0 ** (-jnp.arange(1, N_ALIBI + 1, dtype=jnp.float32) * (8.0 / N_ALIBI))
    proj = jnp.einsum('bsd,dn->bsn', h, w_in)
    split_points = np.cumsum(IN_SIZES)[:-1].tolist()
    (a_q, a_k, a_v, a_f, b_cq, b_ckv, b_kr, c_q, c_k, c_v,
     d_q, d_k, d_v, d_qi, d_ki, d_wi) = jnp.split(proj, split_points, axis=-1)

    log_f = jax.nn.log_sigmoid(a_f.astype(jnp.float32) + b_forget.astype(jnp.float32))
    out_a = causal_block_attention(a_q.reshape(B, S, FOX_HEADS, HEAD_DIM),
                                   a_k.reshape(B, S, FOX_HEADS, HEAD_DIM),
                                   a_v.reshape(B, S, FOX_HEADS, HEAD_DIM), log_f)

    q_full = jnp.einsum('bsr,rn->bsn', rmsnorm(b_cq, g_q_mla), w_q_up).reshape(B, S, MLA_HEADS, MLA_NOPE_DIM + MLA_ROPE_DIM)
    kv_full = jnp.einsum('bsr,rn->bsn', rmsnorm(b_ckv, g_kv_mla), w_kv_up).reshape(B, S, MLA_HEADS, MLA_NOPE_DIM + MLA_V_DIM)
    q_nope, q_rot = q_full[..., :MLA_NOPE_DIM], q_full[..., MLA_NOPE_DIM:]
    k_nope, v_mla = kv_full[..., :MLA_NOPE_DIM], kv_full[..., MLA_NOPE_DIM:]
    k_rot = jnp.broadcast_to(rope(b_kr[:, :, None, :], pos), (B, S, MLA_HEADS, MLA_ROPE_DIM))
    q_mla = jnp.concatenate([q_nope, rope(q_rot, pos)], axis=-1)
    k_mla = jnp.concatenate([k_nope, k_rot], axis=-1)
    out_b = causal_block_attention(q_mla, k_mla, v_mla)

    out_c = sliding_window_sink_attention(c_q.reshape(B, S, SWA_HEADS, HEAD_DIM),
                                          c_k.reshape(B, S, SWA_KV_HEADS, HEAD_DIM),
                                          c_v.reshape(B, S, SWA_KV_HEADS, HEAD_DIM),
                                          sinks, alibi[:SWA_HEADS])

    out_d = dsa_attention(d_q.reshape(B, S, DSA_HEADS, HEAD_DIM), d_k, d_v,
                          d_qi.reshape(B, S, DSA_IDX_HEADS, DSA_IDX_DIM), d_ki, d_wi,
                          alibi[SWA_HEADS:])

    merged = jnp.concatenate([out_a, out_b, out_c, out_d], axis=-1)
    return jnp.einsum('bsm,md->bsd', merged, w_out)

def grouped_moe(h, w_router, b_router, w_gate, w_up, w_down):
    B, S, D = h.shape
    t = h.reshape(B * S, D)
    scores = jax.nn.sigmoid(jnp.einsum('td,de->te', t, w_router, preferred_element_type=jnp.float32))
    biased = scores + b_router.astype(jnp.float32)
    grouped = biased.reshape(-1, N_GROUPS, EXPERTS_PER_GROUP)
    group_score = lax.top_k(grouped, 2)[0].sum(-1)
    best_group = jnp.argmax(group_score, axis=-1)
    in_group = jax.nn.one_hot(best_group, N_GROUPS, dtype=jnp.bool_)[:, :, None]
    masked = jnp.where(in_group, grouped, -jnp.inf).reshape(-1, N_EXPERTS)
    _, expert_idx = lax.top_k(masked, TOP_K_EXPERTS)
    w = jnp.take_along_axis(scores, expert_idx, axis=1)
    w = w / jnp.sum(w, axis=-1, keepdims=True)
    gates = jnp.sum(jax.nn.one_hot(expert_idx, N_EXPERTS, dtype=jnp.float32) * w[..., None], axis=1)
    out = jnp.zeros((t.shape[0], D), jnp.float32)
    for e in range(N_EXPERTS):
        hid = jax.nn.silu(t @ w_gate[e]) * (t @ w_up[e])
        out = out + gates[:, e:e + 1] * (hid @ w_down[e]).astype(jnp.float32)
    return out.astype(h.dtype).reshape(B, S, D)

def setup_inputs(seed: int = 0) -> dict:
    key = jax.random.key(seed)
    ks = jax.random.split(key, 24)
    f32 = jnp.float32
    nrm = lambda k, shape, s: jax.random.normal(k, shape, f32) * s
    D = D_MODEL
    return {
        'x': nrm(ks[0], (BATCH, SEQ, D), 1.0),
        'c': nrm(ks[1], (BATCH, D), 1.0),
        'w_ada': nrm(ks[2], (DEPTH, D, 6 * D), 0.5 * D ** -0.5),
        'b_ada': nrm(ks[3], (DEPTH, 6 * D), 0.02),
        'g_norm1': 1.0 + nrm(ks[4], (DEPTH, D), 0.02),
        'w_in': nrm(ks[5], (DEPTH, D, N_IN), D ** -0.5),
        'b_forget': 1.0 + nrm(ks[6], (DEPTH, FOX_HEADS), 0.1),
        'g_q_mla': 1.0 + nrm(ks[7], (DEPTH, MLA_Q_RANK), 0.02),
        'w_q_up': nrm(ks[8], (DEPTH, MLA_Q_RANK, MLA_HEADS * (MLA_NOPE_DIM + MLA_ROPE_DIM)), MLA_Q_RANK ** -0.5),
        'g_kv_mla': 1.0 + nrm(ks[9], (DEPTH, MLA_KV_RANK), 0.02),
        'w_kv_up': nrm(ks[10], (DEPTH, MLA_KV_RANK, MLA_HEADS * (MLA_NOPE_DIM + MLA_V_DIM)), MLA_KV_RANK ** -0.5),
        'sinks': nrm(ks[11], (DEPTH, SWA_HEADS), 0.5),
        'w_out': nrm(ks[12], (DEPTH, D_MIX, D), D_MIX ** -0.5),
        'g_norm2': 1.0 + nrm(ks[13], (DEPTH, D), 0.02),
        'w_router': nrm(ks[14], (D, N_EXPERTS), D ** -0.5),
        'b_router': nrm(ks[15], (N_EXPERTS,), 0.01),
        'w_gate': nrm(ks[16], (DEPTH, N_EXPERTS, D, D_EXPERT), D ** -0.5),
        'w_up': nrm(ks[17], (DEPTH, N_EXPERTS, D, D_EXPERT), D ** -0.5),
        'w_down': nrm(ks[18], (DEPTH, N_EXPERTS, D_EXPERT, D), D_EXPERT ** -0.5),
        'g_final': 1.0 + nrm(ks[19], (D,), 0.02),
    }

def reference(x, c, w_ada, b_ada, g_norm1, w_in, b_forget, g_q_mla, w_q_up, g_kv_mla, w_kv_up,
              sinks, w_out, g_norm2, w_router, b_router, w_gate, w_up, w_down, g_final):
    c_act = jax.nn.silu(c)
    for l in range(DEPTH):
        mod = jnp.einsum('bd,dn->bn', c_act, w_ada[l]) + b_ada[l]
        sh1, sc1, gt1, sh2, sc2, gt2 = jnp.split(mod[:, None, :], 6, axis=-1)
        h = rmsnorm(x, g_norm1[l]) * (1.0 + sc1) + sh1
        x = x + gt1 * hybrid_mixer(h, w_in[l], b_forget[l], g_q_mla[l], w_q_up[l], g_kv_mla[l],
                                   w_kv_up[l], sinks[l], w_out[l])
        h = rmsnorm(x, g_norm2[l]) * (1.0 + sc2) + sh2
        x = x + gt2 * grouped_moe(h, w_router, b_router, w_gate[l], w_up[l], w_down[l])
    return rmsnorm(x, g_final)


_drawn_inputs = setup_inputs


def setup_inputs(seed=0):
    import zlib

    import numpy as np

    out = dict(_drawn_inputs(seed))
    spreads = {}
    factors = {'g_norm1': 2.819,
     'b_forget': 3.225,
     'g_q_mla': 8.0,
     'g_kv_mla': 4.598,
     'g_final': 8.053,
     'sinks': 8.0}
    for name, (base, spread) in spreads.items():
        noise = np.random.default_rng([zlib.crc32(name.encode()), seed]).standard_normal(out[name].shape)
        drawn = base * np.exp(spread * noise) if base else spread * noise
        out[name] = __import__('jax').numpy.asarray(drawn.astype(out[name].dtype))
    for name, factor in factors.items():
        out[name] = (out[name] * factor).astype(out[name].dtype)
    return out
```

```python
import concourse.bass as bass
from concourse import mybir
import numpy as np

F32 = mybir.dt.float32
ALU = mybir.AluOpType
ACT = mybir.ActivationFunctionType
AX = mybir.AxisListType

P = 128
SEQ, D, DEPTH = 512, 1024, 2
TT = SEQ // P
KT = D // P
HD = 64
HEADS = 4
NE, NG, FE = 16, 4, 256
EPS = 1e-6
IDX_HEADS, IDX_DIM, TOPK = 8, 32, 128
NOPE, ROPE = 64, 32
QR, KVR = 256, 128
NEG = -1e30
TAKEN = -3e38
BIG = 3e38

SIZES = [256, 256, 256, 4, 256, 128, 32, 256, 128, 128, 256, 64, 64, 256, 32, 8]
NAMES = ["aq", "ak", "av", "af", "bcq", "bckv", "bkr", "cq", "ck", "cv", "dq", "dk", "dv", "dqi", "dki", "dwi"]
OFF = {n: int(sum(SIZES[:i])) for i, n in enumerate(NAMES)}
N_IN = sum(SIZES)
CHUNKS = [("dq", 384), ("dqi", 296), ("bcq", 384), ("aq", 384), ("ak2", 388), ("cq", 384), ("cv", 128)]
CHUNK_AT = [OFF["dq"], OFF["dqi"], OFF["bcq"], OFF["aq"], OFF["aq"] + 384, OFF["cq"], OFF["cv"]]
SLOTS, SLOT = 4, 8 * 388
MOD_CHUNKS = 6 * D // 512

GROUPS = "ABCD"
UNITS = [(g, i, h) for g in GROUPS for i in range(TT) for h in range(HEADS)]


def keys(g, i):
    if g == "C":
        return (0, P) if i == 0 else ((i - 1) * P, 2 * P)
    return 0, P * (i + 1)


def plan():
    jobs = [("mod", "dve")]
    jobs += [(("h1", k), "act" if k % 2 else "dve") for k in range(KT)]
    jobs += [(("qD", m), "act") for m in range(2)] + [("kvD", "act")]
    jobs += [(("qi", m), "dve") for m in range(2)] + [("kiwi", "dve"), ("vDT", "act"), ("wiT", "dve")]
    jobs += [(("idx", i, h), "act") for i in range(1, TT) for h in range(IDX_HEADS)]
    jobs += [(("cq", m), "act") for m in range(2)] + [("ckv", "act"), ("kr", "act")]
    jobs += [(("qA", m), "act") for m in range(2)] + [(("kA", m), "act") for m in range(2)]
    jobs += [(("vA", i), "act") for i in range(TT)] + [("afT", "act"), ("ssq", "act"), ("ssk", "act")]
    jobs += [(("qC", m), "act") for m in range(2)] + [("kC", "act"), ("vC", "act")]
    jobs += [(("qBn", m), "act") for m in range(2)] + [("qBr", "dve"), ("qBs", "dve")]
    jobs += [(("kBn", m), "act") for m in range(2)] + [(("vB", m), "act") for m in range(2)]
    n = len(UNITS)
    jobs += [(("S", u), "dve") for u in range(3)]
    for u in range(n):
        jobs += [(("T", u), "act" if u % 2 else "dve")]
        if u + 3 < n:
            jobs += [(("S", u + 3), "dve")]
    jobs += [(("mT", k), "act" if k % 2 else "dve") for k in range(KT)]
    jobs += [(("gt1", m), "act") for m in range(2)]
    jobs += [(("out", i, m), "dve") for i in range(TT) for m in range(2)]
    jobs += [(("h2", k), "act" if k % 2 else "dve") for k in range(KT)]
    jobs += [("router", "act")] + [(("gt2", m), "act") for m in range(2)]
    return jobs


def constants():
    q = np.arange(P)[:, None]
    c = np.arange(SEQ)[None, :]
    causal = np.where(c - (SEQ - P) > q, NEG, 0.0)
    dist = q - np.arange(2 * P)[None, :] + P
    window = np.where((dist >= 0) & (dist < P), 0.0, NEG)
    half = ROPE // 2
    inv = 10000.0 ** (-np.arange(half, dtype=np.float32) / np.float32(half))
    ang = (np.arange(SEQ, dtype=np.float32)[None, :] * inv.astype(np.float32)[:, None]).astype(np.float32)
    cos = np.tile(np.cos(ang), (8, 1))
    sin = np.tile(np.concatenate([-np.sin(ang), np.sin(ang)]), (4, 1))
    pos = np.arange(SEQ, dtype=np.float64)
    slopes = 2.0 ** (-np.arange(1, 9, dtype=np.float64))
    rows = np.zeros((2, 4 + 2 + 4 + 1 + 4 + 4, SEQ))
    for n, s in enumerate(slopes):
        at = n if n < 4 else 6 + n - 4
        rows[0, at] = -8 * s * pos
        rows[1, at] = 8 * s
    for at in (4, 5, 10):
        rows[0, at] = 1
        rows[1, at] = pos
    rows[:, 11:] = 1
    f = lambda a: np.ascontiguousarray(a, dtype=np.float32)
    return {"k_causal": f(causal), "k_window": f(window), "k_cos": f(cos), "k_sin": f(sin),
            "k_rows": f(rows), "k_ident": f(np.eye(P))}


def trunk(nc, x_in, c_in, w_ada, b_ada, g_norm1, w_in, b_forget, g_q_mla, w_q_up, g_kv_mla, w_kv_up, sinks,
          w_out, g_norm2, w_router, b_router, w_gate, w_up, w_down, g_final,
          k_causal, k_window, k_cos, k_sin, k_rows, k_ident, out):

    def sb(name, *shape):
        return nc.alloc_sbuf_tensor(name, [P, *shape], F32)

    x = sb("x", TT, D)
    hT = sb("hT", KT, SEQ)
    wbuf = sb("wbuf", SLOTS * SLOT)
    tok = sb("tok", TT, D)
    qA, kA = sb("qA", 4, SEQ), sb("kA", 4, SEQ)
    qB, kB = sb("qB", 4, SEQ), sb("kB", 4, SEQ)
    qC, kC = sb("qC", 4, SEQ), sb("kC", 2, SEQ)
    qD, kD = sb("qD", 4, SEQ), sb("kD", SEQ)
    vA, vB, vC, vD = sb("vA", TT, 260), sb("vB", TT, 256), sb("vC", TT, 128), sb("vD", TT, 64)
    qi, ki = sb("qi", 2, SEQ), sb("ki", SEQ)
    tring = sb("tring", 4, SEQ)
    pring = sb("pring", 3, SEQ)
    wq_n, wq_r, wq_s = sb("wq_n", 2, 256), sb("wq_r", 2, 128), sb("wq_s", 2, 128)
    wk_n, wk_v = sb("wk_n", 256), sb("wk_v", 256)
    ident, ones = sb("ident", P), sb("ones", P)
    causal, window = sb("causal", SEQ), sb("window", 2 * P)
    selmask = sb("selmask", 9 * P)
    gtB = sb("gtB", D)
    modT = sb("modT", 48)
    vecT = sb("vecT", 20)
    scaleT = sb("scaleT", 16)
    small = sb("small", 512)
    cT = small[:, 0:8]
    cact = small[:, 8:16]
    ss = small[:, 16:20]
    rstd = small[:, 20:24]
    sinkb = small[:, 24:28]
    nsink = small[:, 28:32]
    brt = small[:, 32:48]
    bfg = small[:, 48:49]
    epsc = small[:, 49:50]
    onec = small[:, 50:51]
    rsd = small[:, 52:56]
    max8 = small[:, 56:64]
    wi = small[:, 64:96].rearrange("p (i h) -> p i h", i=TT)
    nbfg = small[:, 96:97]
    nmax = small[:, 128:192]
    sums = small[:, 192:256]
    rout = sb("rout", 8, 64)
    wr = sb("wr", KT, NE)
    wkr = sb("wkr", KT, 2 * ROPE)

    latent = tok[:, :, :].rearrange("p i n -> p (i n)")
    cqT = latent[:, 0:1024].rearrange("p (m n) -> p m n", m=2)
    ckvT = latent[:, 1024:1536]
    krT, krS = latent[:, 1536:2048], latent[:, 3584:4096]
    sqT = latent[:, 2048:3584].rearrange("p (m n) -> p m n", m=3)
    rope1, rope2 = qi[:, 0, :], qi[:, 1, :]
    cosT, sinT = pring[:, 0, :], pring[:, 1, :]
    rq, rk = gtB[:, 0:512], gtB[:, 512:1024]
    vdT, kiwiT = tring[:, 2, :], tring[:, 3, :]
    score = tring[:, 0, :]
    relu = [pring[:, 0, :], pring[:, 1, :], pring[:, 2, :]]
    fg = [kB[0:4, n, :] for n in range(4)]
    diag = tring[:, 0:2, :].rearrange("p a n -> p (a n)")

    banks = [nc.alloc_psum_tensor(f"bank{n}", [P, 512], F32) for n in range(8)]

    sem = nc.alloc_semaphore
    consts_landed, consts_set = sem("consts_landed"), sem("consts_set")
    layer_passed = sem("layer_passed")
    layer_end, layer_go, stored = sem("layer_end"), sem("layer_go"), sem("stored")
    c_ready = sem("c_ready")
    fin_squares, fin_root, fin_rstd, fin_rows = sem("fin_squares"), sem("fin_root"), sem("fin_rstd"), sem("fin_rows")
    small_landed, bias_zeroed, nsink_ready = sem("small_landed"), sem("bias_zeroed"), sem("nsink_ready")
    ada_landed = [sem(f"ada_landed{n}") for n in range(3)]
    bada_landed = [sem(f"bada_landed{n}") for n in range(2)]
    ada_used, ada_summed = sem("ada_used"), sem("ada_summed")
    win_landed = [sem(f"win_landed{n}") for n in range(len(CHUNKS))]
    rope_landed, wout_landed = sem("rope_landed"), sem("wout_landed")
    expert_landed = [sem(f"expert_landed{n}") for n in range(2)]
    psum_filled, act_drained, dve_drained = sem("psum_filled"), sem("act_drained"), sem("dve_drained")
    dve_step, act_step = sem("dve_step"), sem("act_step")
    squares_ready, root_ready, xhat_ready = sem("squares_ready"), sem("root_ready"), sem("xhat_ready")
    relu_used, topk_done = sem("relu_used"), sem("topk_done")
    cq_squared, latents_ready, krope_ready = sem("cq_squared"), sem("latents_ready"), sem("krope_ready")
    qrope_ready, scales_ready = sem("qrope_ready"), sem("scales_ready")
    forget_ready, forget_landed = sem("forget_ready"), sem("forget_landed")
    softplus_ready = sem("softplus_ready")
    probs_ready = sem("probs_ready")
    o_filled, o_drained = sem("o_filled"), sem("o_drained")
    diag_ready, gated_ready, x_added = sem("diag_ready"), sem("gated_ready"), sem("x_added")
    gates_ready = sem("gates_ready")
    acc_cleared = sem("acc_cleared")
    gu_filled, silu_ready, hidden_ready = sem("gu_filled"), sem("silu_ready"), sem("hidden_ready")
    down_filled, acc_done = sem("down_filled"), sem("acc_done")
    first_layer_sem, last_layer_sem = small_landed, acc_done

    jobs = plan()
    index = {name: n for n, (name, _) in enumerate(jobs)}
    drainer = dict(jobs)
    ordinal, count = {}, {"act": 0, "dve": 0}
    for name, engine in jobs:
        count[engine] += 1
        ordinal[name] = count[engine]
    RING = 6

    def bank(name):
        return banks[index[name] % RING]

    def wait_filled(eng, name):
        eng.wait_ge(psum_filled, index[name] + 1)

    def wait_drained(eng, name):
        eng.wait_ge(act_drained if drainer[name] == "act" else dve_drained, ordinal[name])

    def wait_bank(pe, name):
        if index[name] >= RING:
            wait_drained(pe, jobs[index[name] - RING][0])

    def slot(n, cols):
        at = (n % SLOTS) * SLOT
        return wbuf[:, at:at + KT * cols].rearrange("p (k n) -> p k n", k=KT)

    def ada_slot(n):
        return wbuf[:, (n % 3) * 4096:(n % 3 + 1) * 4096].rearrange("p (k n) -> p k n", k=KT)

    ada_bias = [pring[:, 0, :], pring[:, 1, :]]
    ada_acc = [tring[:, 0, :], tring[:, 1, :]]
    wo = wbuf[:, 0:KT * D].rearrange("p (k n) -> p k n", k=KT)

    def expert(s):
        b = s * 6144
        return (wbuf[:, b:b + 2048].rearrange("p (k f) -> p k f", k=KT),
                wbuf[:, b + 2048:b + 4096].rearrange("p (k f) -> p k f", k=KT),
                wbuf[:, b + 4096:b + 6144].rearrange("p (k n) -> p k n", k=2))

    chunk_last_job = ["kvD", "kiwi", "ckv", ("kA", 0), ("vA", 3), "kC", "vC"]
    last_unit = len(UNITS) - 1
    MOE_GU, MOE_DN = 4, 8

    CONSTS, SMALLS = 13, 19
    totals = {small_landed: SMALLS * 16, bias_zeroed: 1, ada_used: MOD_CHUNKS, ada_summed: MOD_CHUNKS - 1,
              ada_landed[0]: 64, ada_landed[1]: 64, ada_landed[2]: 64, bada_landed[0]: 96, bada_landed[1]: 96,
              rope_landed: 32, wout_landed: 16, expert_landed[0]: 48 * NE // 2, expert_landed[1]: 48 * NE // 2,
              psum_filled: len(jobs), act_drained: count["act"], dve_drained: count["dve"],
              squares_ready: 2 * TT, root_ready: 2, xhat_ready: 2 * TT, relu_used: 3 * IDX_HEADS, topk_done: 3,
              cq_squared: 3, latents_ready: 1, krope_ready: 2, qrope_ready: 1, scales_ready: 2, nsink_ready: 1,
              forget_ready: 2, forget_landed: 8 * 16, softplus_ready: 1,
              probs_ready: len(UNITS), o_filled: len(UNITS) // HEADS, o_drained: len(UNITS) // HEADS,
              diag_ready: 2, gated_ready: TT, x_added: 3 * TT, gates_ready: 1, acc_cleared: 1,
              gu_filled: MOE_GU * NE, silu_ready: 2 * NE, hidden_ready: 2 * NE + 2, down_filled: MOE_DN * NE,
              acc_done: MOE_DN * (NE + 1)}
    for n, landed in enumerate(win_landed):
        totals[landed] = 16

    with nc.Block() as block:

        @block.gpsimd
        def _(pool):
            nc.gpsimd.memset(ones[:, :], 1.0).then_inc(consts_set, 1)
            nc.gpsimd.memset(epsc, EPS).then_inc(consts_set, 1)
            nc.gpsimd.memset(onec, 1.0).then_inc(consts_set, 1)
            with pool.Fori(0, DEPTH) as l:
                nc.gpsimd.memset(pring[:, 0:2, :], 0.0).then_inc(bias_zeroed, 1)
                pool.sem_inc(acc_done, 8)
                pool.sem_inc(hidden_ready, 2)
                for m, name in enumerate([("cq", 0), ("cq", 1), "ckv"]):
                    wait_drained(pool, name)
                    src = cqT[:, m, :] if m < 2 else ckvT
                    nc.gpsimd.tensor_tensor(sqT[:, m, :], src, src, ALU.mult).then_inc(cq_squared, 1)
                wait_drained(pool, "kr")
                pool.wait_ge(rope_landed, 32)
                nc.gpsimd.tensor_tensor(krT[0:32, :], krT[0:32, :], cosT[0:32, :], ALU.mult).then_inc(krope_ready, 1)
                nc.gpsimd.tensor_tensor(krS[0:32, :], krS[0:32, :], sinT[0:32, :], ALU.mult).then_inc(krope_ready, 1)
                for n in range(2 * TT):
                    wait_drained(pool, ("out", n // 2, n % 2))
                    xs = x[:, n // 2, (n % 2) * 512:(n % 2 + 1) * 512]
                    nc.gpsimd.tensor_tensor(xs, xs, tring[:, n % 4, :], ALU.add).then_inc(x_added, 1)
                wait_filled(pool, ("h2", KT - 1))
                nc.gpsimd.memset(tok[:, :, :], 0.0).then_inc(acc_cleared, 1)
                for i in range(TT):
                    pool.wait_ge(gated_ready, i + 1)
                    nc.gpsimd.tensor_tensor(x[:, i, :], x[:, i, :], tok[:, i, :], ALU.add).then_inc(x_added, 1)
                pool.wait_ge(x_added, 3 * TT)
                pool.sem_inc(layer_end, 1)
                pool.wait_ge(layer_go, l + 1)

        @block.scalar
        def _(act):
            step = [0]

            def link(ins):
                step[0] += 1
                ins.then_inc(act_step, 1)
                act.wait_ge(act_step, step[0])

            def norm_roots(k):
                for i in range(TT):
                    nc.scalar.activation(tok[:, i, :], x[:, i, :], ACT.Square, accum_out=ss[:, i:i + 1])\
                        .then_inc(squares_ready, 1)
                act.wait_ge(squares_ready, TT * (k + 1))
                nc.scalar.activation(rstd, ss, ACT.Sqrt, bias=epsc, scale=1.0 / D).then_inc(root_ready, 1)

            def drain(name, *moves):
                wait_filled(act, name)
                for dst, src in moves:
                    last = nc.scalar.activation(dst, src, ACT.Copy)
                last.then_inc(act_drained, 1)

            def drain_pair(name, dst, m):
                b = bank(name)
                drain(name, (dst[0:64, 2 * m, :], b[0:64, :]), (dst[0:64, 2 * m + 1, :], b[64:128, :]))

            act.wait_ge(consts_landed, CONSTS * 16)
            act.wait_ge(consts_set, 3)
            nc.scalar.activation(cact, cT, ACT.Silu).then_inc(c_ready, 1)
            with act.Fori(0, DEPTH) as l:
                act.wait_ge(small_landed, SMALLS * 16)
                norm_roots(0)
                nc.scalar.activation(nsink, sinkb, ACT.Copy, scale=-1.0).then_inc(nsink_ready, 1)
                link(nc.scalar.activation(nbfg[0:4, :], bfg[0:4, :], ACT.Copy, scale=-1.0))
                act.wait_ge(scales_ready, 2)
                for k in range(1, KT, 2):
                    wait_filled(act, ("h1", k))
                    nc.scalar.activation(hT[:, k, :], bank(("h1", k))[:, :], ACT.Identity,
                                         bias=modT[:, k:k + 1], scale=scaleT[:, k:k + 1]).then_inc(act_drained, 1)
                for m in range(2):
                    drain_pair(("qD", m), qD, m)
                b = bank("kvD")
                drain("kvD", (kD[0:64, :], b[0:64, :]), (vdT[0:64, :], b[64:128, :]))
                drain("vDT", (vD[:, :, :].rearrange("p i n -> p (i n)"), bank("vDT")[:, 0:256]))
                for i in range(1, TT):
                    for h in range(IDX_HEADS):
                        n = (i - 1) * IDX_HEADS + h
                        wait_filled(act, ("idx", i, h))
                        if n >= 3:
                            act.wait_ge(relu_used, n - 2)
                        w = P * (i + 1)
                        nc.scalar.activation(relu[n % 3][:, 0:w], bank(("idx", i, h))[:, 0:w], ACT.Relu)\
                            .then_inc(act_drained, 1)
                for m in range(2):
                    drain(("cq", m), (cqT[:, m, :], bank(("cq", m))[:, :]))
                drain("ckv", (ckvT, bank("ckv")[:, :]))
                b = bank("kr")
                drain("kr", (krT[0:32, :], b[0:32, :]), (krS[0:32, :], b[32:64, :]))
                for m in range(2):
                    drain_pair(("qA", m), qA, m)
                for m in range(2):
                    drain_pair(("kA", m), kA, m)
                for i in range(TT):
                    drain(("vA", i), (vA[:, i, :], bank(("vA", i))[:, 0:260]))
                wait_filled(act, "afT")
                z = bank("afT")[0:4, :]
                link(nc.scalar.activation(fg[2], z, ACT.Abs, bias=bfg[0:4, :]))
                nc.scalar.activation(fg[3], z, ACT.Relu, bias=nbfg[0:4, :], scale=-1.0).then_inc(act_drained, 1)
                link(nc.scalar.activation(fg[2], fg[2], ACT.Exp, scale=-1.0))
                nc.scalar.activation(fg[2], fg[2], ACT.Ln, bias=onec[0:4, :]).then_inc(softplus_ready, 1)
                for name, dst, r in (("ssq", rq, QR), ("ssk", rk, KVR)):
                    wait_filled(act, name)
                    nc.scalar.activation(dst, bank(name)[:, :], ACT.Sqrt, bias=epsc, scale=1.0 / r).then_inc(act_drained, 1)
                for m in range(2):
                    drain_pair(("qC", m), qC, m)
                b = bank("kC")
                drain("kC", (kC[0:64, 0, :], b[0:64, :]), (kC[0:64, 1, :], b[64:128, :]))
                drain("vC", (vC[:, :, :].rearrange("p i n -> p (i n)"), bank("vC")[:, :]))
                for m in range(2):
                    drain_pair(("qBn", m), qB, m)
                act.wait_ge(forget_landed, 8 * 16)
                for m in range(2):
                    drain_pair(("kBn", m), kB, m)
                for m in range(2):
                    drain(("vB", m), (vB[:, 2 * m:2 * m + 2, :].rearrange("p i n -> p (i n)"), bank(("vB", m))[:, :]))

                def exps(u):
                    g, i, h = UNITS[u]
                    n = keys(g, i)[1] + (g == "C")
                    t = tring[:, u % 4, 0:n]
                    wait_drained(act, ("S", u))
                    nc.scalar.activation(t, t, ACT.Exp, bias=nmax[:, u:u + 1], scale=-1.0,
                                         accum_out=sums[:, u:u + 1]).then_inc(probs_ready, 1)

                for u in range(3):
                    exps(u)
                for u in range(len(UNITS)):
                    if u % 2:
                        n = keys(*UNITS[u][:2])[1]
                        drain(("T", u), (pring[:, u % 3, 0:n], bank(("T", u))[:, 0:n]))
                    if u + 3 < len(UNITS):
                        exps(u + 3)
                for k in range(1, KT, 2):
                    drain(("mT", k), (hT[:, k, :], bank(("mT", k))[:, :]))
                for m in range(2):
                    drain(("gt1", m), (gtB[:, m * 512:(m + 1) * 512], bank(("gt1", m))[:, :]))

                act.wait_ge(x_added, 2 * TT)
                norm_roots(1)
                for k in range(1, KT, 2):
                    wait_filled(act, ("h2", k))
                    nc.scalar.activation(hT[:, k, :], bank(("h2", k))[:, :], ACT.Identity,
                                         bias=modT[:, 24 + k:25 + k], scale=scaleT[:, 8 + k:9 + k]).then_inc(act_drained, 1)
                wait_filled(act, "router")
                nc.scalar.activation(rout[:, 0, :], bank("router")[:, 0:64], ACT.Sigmoid).then_inc(act_drained, 1)
                for m in range(2):
                    drain(("gt2", m), (gtB[:, m * 512:(m + 1) * 512], bank(("gt2", m))[:, :]))
                with act.Fori(0, NE) as e:
                    for f in range(2):
                        act.wait_ge(gu_filled, e * MOE_GU + 2 * f + 1)
                        nc.scalar.activation(pring[:, f, :], banks[2 * f][:, :], ACT.Silu).then_inc(silu_ready, 1)
                act.wait_ge(silu_ready, 2 * NE)
                act.sem_inc(layer_end, 1)
                act.wait_ge(layer_go, l + 1)
            totals[act_step] = step[0]
            for i in range(TT):
                nc.scalar.activation(tok[:, i, :], x[:, i, :], ACT.Square, accum_out=ss[:, i:i + 1]).then_inc(fin_squares, 1)
            act.wait_ge(fin_squares, TT)
            nc.scalar.activation(rstd, ss, ACT.Sqrt, bias=epsc, scale=1.0 / D).then_inc(fin_root, 1)

        @block.vector
        def _(dve):
            step = [0]

            def link(ins):
                step[0] += 1
                ins.then_inc(dve_step, 1)
                dve.wait_ge(dve_step, step[0])

            def norm_rows(k):
                dve.wait_ge(root_ready, k + 1)
                link(nc.vector.reciprocal(rstd, rstd))
                for i in range(TT):
                    nc.vector.tensor_scalar(tok[:, i, :], x[:, i, :], rstd[:, i:i + 1], None, ALU.mult)\
                        .then_inc(xhat_ready, 1)

            def rank(dst, src, tmp):
                link(nc.vector.memset(dst, 0.0))
                G = src.shape[1]
                for j in range(4):
                    for lo, hi, op in ((0, j, ALU.is_gt), (j + 1, 4, ALU.is_ge)):
                        if lo < hi:
                            link(nc.vector.tensor_tensor(tmp[:, :, lo:hi], src[:, :, j:j + 1].to_broadcast([P, G, hi - lo]),
                                                         src[:, :, lo:hi], op))
                            link(nc.vector.tensor_tensor(dst[:, :, lo:hi], dst[:, :, lo:hi], tmp[:, :, lo:hi], ALU.add))

            dve.wait_ge(c_ready, 1)
            with dve.Fori(0, DEPTH) as l:
                for n in range(MOD_CHUNKS):
                    a, w = ada_acc[n % 2], ada_slot(n)
                    dve.wait_ge(ada_landed[n % 3], 16 * (n // 3 + 1))
                    dve.wait_ge(bada_landed[n % 2], 16 * (n // 2 + 1))
                    if n >= 2:
                        dve.wait_ge(ada_summed, n - 1)
                    for k in range(KT):
                        ins = nc.vector.scalar_tensor_tensor(out=a, in0=w[:, k, :], scalar=cact[:, k:k + 1],
                                                             in1=a if k else ada_bias[n % 2], op0=ALU.mult, op1=ALU.add)
                        if k < KT - 1:
                            link(ins)
                        else:
                            ins.then_inc(ada_used, 1)
                wait_filled(dve, "mod")
                nc.vector.tensor_copy(modT[:, :], bank("mod")[:, 0:48]).then_inc(dve_drained, 1)
                wait_drained(dve, "mod")
                dve.wait_ge(small_landed, SMALLS * 16)
                nc.vector.scalar_tensor_tensor(out=scaleT[:, 0:8], in0=modT[:, 8:16], scalar=1.0, in1=vecT[:, 0:8],
                                               op0=ALU.add, op1=ALU.mult).then_inc(scales_ready, 1)
                nc.vector.scalar_tensor_tensor(out=scaleT[:, 8:16], in0=modT[:, 32:40], scalar=1.0, in1=vecT[:, 8:16],
                                               op0=ALU.add, op1=ALU.mult).then_inc(scales_ready, 1)
                norm_rows(0)
                dve.wait_ge(scales_ready, 2)
                for k in range(0, KT, 2):
                    wait_filled(dve, ("h1", k))
                    nc.vector.tensor_scalar(hT[:, k, :], bank(("h1", k))[:, :], scaleT[:, k:k + 1], modT[:, k:k + 1],
                                            ALU.mult, ALU.add).then_inc(dve_drained, 1)
                for m in range(2):
                    wait_filled(dve, ("qi", m))
                    nc.vector.tensor_copy(qi[:, m, :], bank(("qi", m))[:, :]).then_inc(dve_drained, 1)
                wait_filled(dve, "kiwi")
                for r in range(4):
                    nc.vector.tensor_copy(ki[32 * r:32 * r + 32, :], bank("kiwi")[0:32, :])
                nc.vector.tensor_copy(kiwiT[0:8, :], bank("kiwi")[32:40, :]).then_inc(dve_drained, 1)
                wait_filled(dve, "wiT")
                nc.vector.tensor_scalar(wi, bank("wiT")[:, 0:32].rearrange("p (i h) -> p i h", i=TT),
                                        (IDX_HEADS * IDX_DIM) ** -0.5, None, ALU.mult).then_inc(dve_drained, 1)
                wait_drained(dve, "wiT")
                at = 0
                for i in range(1, TT):
                    w = P * (i + 1)
                    sc = score[:, 0:w]
                    for h in range(IDX_HEADS):
                        n = (i - 1) * IDX_HEADS + h
                        wait_drained(dve, ("idx", i, h))
                        r = relu[n % 3][:, 0:w]
                        if h == 0:
                            nc.vector.tensor_scalar(sc, r, wi[:, i, 0:1], None, ALU.mult).then_inc(relu_used, 1)
                        else:
                            nc.vector.scalar_tensor_tensor(out=sc, in0=r, scalar=wi[:, i, h:h + 1], in1=sc,
                                                           op0=ALU.mult, op1=ALU.add).then_inc(relu_used, 1)
                        dve.wait_ge(relu_used, n + 1)
                    link(nc.vector.tensor_tensor(sc[:, i * P:w], sc[:, i * P:w], causal[:, SEQ - P:SEQ], ALU.add))
                    for _ in range(TOPK // 8):
                        link(nc.vector.max(max8, sc))
                        link(nc.vector.match_replace(sc, max8, sc, TAKEN))
                    nc.vector.tensor_scalar(selmask[:, at:at + w], sc, TAKEN / 2, NEG, ALU.is_gt, ALU.mult)\
                        .then_inc(topk_done, 1)
                    dve.wait_ge(topk_done, i)
                    at += w
                wait_drained(dve, "afT")
                dve.wait_ge(softplus_ready, 1)
                link(nc.vector.tensor_tensor_scan(fg[1], fg[2], fg[3], 0.0, ALU.add, ALU.add))
                nc.vector.tensor_scalar(fg[0], fg[1], -8.0, None, ALU.mult).then_inc(forget_ready, 1)
                dve.wait_ge(forget_ready, 1)
                nc.vector.tensor_scalar(fg[1], fg[1], 8.0, None, ALU.mult).then_inc(forget_ready, 1)
                wait_drained(dve, "ssk")
                link(nc.vector.reciprocal(rq, rq))
                link(nc.vector.reciprocal(rk, rk))
                for m in range(2):
                    nc.vector.scalar_tensor_tensor(out=cqT[:, m, :], in0=cqT[:, m, :], scalar=vecT[:, 16 + m:17 + m],
                                                   in1=rq, op0=ALU.mult, op1=ALU.mult)
                nc.vector.scalar_tensor_tensor(out=ckvT, in0=ckvT, scalar=vecT[:, 18:19], in1=rk,
                                               op0=ALU.mult, op1=ALU.mult).then_inc(latents_ready, 1)
                dve.wait_ge(rope_landed, 32)
                wait_filled(dve, "qBr")
                nc.vector.tensor_tensor(rope1, bank("qBr")[:, :], cosT, ALU.mult).then_inc(dve_drained, 1)
                wait_filled(dve, "qBs")
                nc.vector.tensor_tensor(rope2, bank("qBs")[:, :], sinT, ALU.mult).then_inc(dve_drained, 1)
                wait_drained(dve, "qBs")
                dve.wait_ge(krope_ready, 2)
                for h in range(HEADS):
                    s = slice(32 * h, 32 * h + 32)
                    nc.vector.tensor_tensor(qB[64:96, h, :], rope1[s, :], rope2[s, :], ALU.add)
                    last = nc.vector.tensor_tensor(kB[64:96, h, :], krT[0:32, :], krS[0:32, :], ALU.add)
                last.then_inc(qrope_ready, 1)

                def scores(u):
                    g, i, h = UNITS[u]
                    n = keys(g, i)[1]
                    t = tring[:, u % 4, :]
                    if g == "C":
                        mask = window[:, 2 * P - n:2 * P]
                        nc.vector.tensor_copy(t[:, n:n + 1], nsink[:, h:h + 1])
                    elif g == "D" and i > 0:
                        at = P * (i * (i + 1) // 2 - 1)
                        mask = selmask[:, at:at + n]
                    else:
                        mask = causal[:, SEQ - n:SEQ]
                    scale = (NOPE + ROPE) ** -0.5 if g == "B" else HD ** -0.5
                    wait_filled(dve, ("S", u))
                    nc.vector.tensor_tensor_reduce(t[:, 0:n], bank(("S", u))[:, 0:n], mask, -scale,
                                                   nsink[:, h:h + 1] if g == "C" else BIG, ALU.add, ALU.min,
                                                   nmax[:, u:u + 1]).then_inc(dve_drained, 1)

                dve.wait_ge(nsink_ready, 1)
                dve.wait_ge(topk_done, TT - 1)
                for u in range(3):
                    scores(u)
                for u in range(len(UNITS)):
                    if u % 2 == 0:
                        n = keys(*UNITS[u][:2])[1]
                        wait_filled(dve, ("T", u))
                        nc.vector.tensor_copy(pring[:, u % 3, 0:n], bank(("T", u))[:, 0:n]).then_inc(dve_drained, 1)
                    if u + 3 < len(UNITS):
                        scores(u + 3)
                    if u % HEADS == 0 and u > 0 or u == last_unit:
                        for og in ([u // HEADS - 1] if u < last_unit else [u // HEADS]):
                            g, i, _ = UNITS[og * HEADS]
                            at = GROUPS.index(g) * HEADS * HD
                            dve.wait_ge(o_filled, og + 1)
                            link(nc.vector.reciprocal(rsd, sums[:, og * HEADS:(og + 1) * HEADS]))
                            nc.vector.tensor_tensor(
                                tok[:, i, at:at + 256].rearrange("p (h d) -> p h d", h=HEADS),
                                banks[6 + og % 2][:, 0:256].rearrange("p (h d) -> p h d", h=HEADS),
                                rsd.unsqueeze(2).to_broadcast([P, HEADS, HD]), ALU.mult).then_inc(o_drained, 1)
                for k in range(0, KT, 2):
                    wait_filled(dve, ("mT", k))
                    nc.vector.tensor_copy(hT[:, k, :], bank(("mT", k))[:, :]).then_inc(dve_drained, 1)

                def diagonals(at):
                    for k in range(KT):
                        last = nc.vector.tensor_scalar(diag[:, k * P:(k + 1) * P], ident[:, :], modT[:, at + k:at + k + 1],
                                                       None, ALU.mult)
                    last.then_inc(diag_ready, 1)

                diagonals(16)
                for n in range(2 * TT):
                    name = ("out", n // 2, n % 2)
                    wait_filled(dve, name)
                    wait_drained(dve, ("gt1", 1))
                    if n >= 4:
                        dve.wait_ge(x_added, n - 3)
                    nc.vector.tensor_tensor(tring[:, n % 4, :], bank(name)[:, :], gtB[:, (n % 2) * 512:(n % 2 + 1) * 512],
                                            ALU.mult).then_inc(dve_drained, 1)
                norm_rows(1)
                for k in range(0, KT, 2):
                    wait_filled(dve, ("h2", k))
                    nc.vector.tensor_scalar(hT[:, k, :], bank(("h2", k))[:, :], scaleT[:, 8 + k:9 + k],
                                            modT[:, 24 + k:25 + k], ALU.mult, ALU.add).then_inc(dve_drained, 1)
                diagonals(40)
                r = [rout[:, n, :] for n in range(8)]
                quads = lambda a: a.rearrange("p (g e) -> p g e", e=4)
                wait_drained(dve, "router")
                link(nc.vector.tensor_tensor(r[1].rearrange("p (i e) -> p i e", e=NE), r[0].rearrange("p (i e) -> p i e", e=NE),
                                             brt.unsqueeze(1).to_broadcast([P, TT, NE]), ALU.add))
                rank(quads(r[2]), quads(r[1]), quads(r[3]))
                link(nc.vector.tensor_scalar(r[2], r[2], 2.0, None, ALU.is_lt))
                link(nc.vector.tensor_tensor(r[3], r[1], r[2], ALU.mult))
                link(nc.vector.tensor_reduce(r[4][:, 0:16], quads(r[3]), AX.X, ALU.add))
                rank(quads(r[5][:, 0:16]), quads(r[4][:, 0:16]), quads(r[6][:, 0:16]))
                link(nc.vector.tensor_scalar(r[5][:, 0:16], r[5][:, 0:16], 1.0, None, ALU.is_lt))
                link(nc.vector.tensor_tensor(quads(r[2]), quads(r[2]), r[5][:, 0:16].unsqueeze(2).to_broadcast([P, 16, 4]), ALU.mult))
                link(nc.vector.tensor_tensor(r[3], r[0], r[2], ALU.mult))
                link(nc.vector.tensor_reduce(r[4][:, 0:4], r[3].rearrange("p (i e) -> p i e", e=NE), AX.X, ALU.add))
                link(nc.vector.reciprocal(r[4][:, 0:4], r[4][:, 0:4]))
                nc.vector.tensor_tensor(r[7].rearrange("p (i e) -> p i e", e=NE), r[3].rearrange("p (i e) -> p i e", e=NE),
                                        r[4][:, 0:4].unsqueeze(2).to_broadcast([P, TT, NE]), ALU.mult).then_inc(gates_ready, 1)
                gates = r[7].rearrange("p (i e) -> p i e", e=NE)
                dve.wait_ge(gates_ready, 1)
                dve.wait_ge(acc_cleared, 1)
                with dve.Fori(0, NE) as e:
                    for f in range(2):
                        dve.wait_ge(gu_filled, e * MOE_GU + 2 * f + 2)
                        dve.wait_ge(silu_ready, e * 2 + f + 1)
                        nc.vector.tensor_tensor(tring[:, 2 + f, :], banks[2 * f + 1][:, :], pring[:, f, :], ALU.mult)\
                            .then_inc(hidden_ready, 1)
                    for n in range(MOE_DN):
                        i, m = n // 2, n % 2
                        a = tok[:, i, m * 512:(m + 1) * 512]
                        dve.wait_ge(down_filled, e * MOE_DN + n + 1)
                        dve.wait_ge(acc_done, e * MOE_DN + n + 1)
                        nc.vector.scalar_tensor_tensor(out=a, in0=banks[4 + n % 4][:, :], scalar=gates[:, i, bass.ds(e, 1)],
                                                       in1=a, op0=ALU.mult, op1=ALU.add).then_inc(acc_done, 1)
                dve.wait_ge(acc_done, (NE + 1) * MOE_DN)
                wait_drained(dve, ("gt2", 1))
                for i in range(TT):
                    nc.vector.tensor_tensor(tok[:, i, :], tok[:, i, :], gtB[:, :], ALU.mult).then_inc(gated_ready, 1)
                dve.wait_ge(gated_ready, TT)
                dve.sem_inc(layer_end, 1)
                dve.wait_ge(layer_go, l + 1)
            totals[dve_step] = step[0]
            dve.wait_ge(fin_root, 1)
            dve.wait_ge(consts_landed, (CONSTS + 1) * 16)
            nc.vector.reciprocal(rstd, rstd).then_inc(fin_rstd, 1)
            dve.wait_ge(fin_rstd, 1)
            for i in range(TT):
                nc.vector.scalar_tensor_tensor(out=tok[:, i, :], in0=x[:, i, :], scalar=rstd[:, i:i + 1], in1=gtB[:, :],
                                               op0=ALU.mult, op1=ALU.mult).then_inc(fin_rows, 1)

        @block.tensor
        def _(pe):
            def mm(dst, lhsT, rhs, first=True, last=True):
                return nc.tensor.matmul(dst, lhsT, rhs, start=first, stop=last)

            def features(name, rows, w, rhs, kt):
                wait_bank(pe, name)
                for k in range(kt):
                    last = mm(bank(name)[0:rows, :], w(k), rhs[:, k, :], k == 0, k == kt - 1)
                last.then_inc(psum_filled, 1)

            def project(name, n, at, rows):
                features(name, rows, lambda k: slot(n, CHUNKS[n][1])[:, k, at:at + rows], hT, KT)

            def turn(name, parts):
                wait_bank(pe, name)
                for dst, src, size in parts:
                    last = nc.tensor.transpose(dst, src, ident[0:size, 0:size])
                last.then_inc(psum_filled, 1)

            def turn_rows(name, k):
                turn(name, [(bank(name)[:, i * P:(i + 1) * P], tok[:, i, k * P:(k + 1) * P], P) for i in range(TT)])

            pe.wait_ge(consts_landed, CONSTS * 16)
            pe.wait_ge(consts_set, 3)
            with pe.Fori(0, DEPTH) as l:
                for n in range(MOD_CHUNKS):
                    pe.wait_ge(ada_used, n + 1)
                    for j in range(4):
                        at = n * 4 + j
                        last = mm(bank("mod")[:, at:at + 1], ada_acc[n % 2][:, j * P:(j + 1) * P], ones[:, 0:1])
                    last.then_inc(ada_summed if n < MOD_CHUNKS - 1 else psum_filled, 1)
                pe.wait_ge(xhat_ready, TT)
                for k in range(KT):
                    turn_rows(("h1", k), k)
                wait_drained(pe, ("h1", KT - 1))
                wait_drained(pe, ("h1", KT - 2))
                pe.wait_ge(win_landed[0], 16)
                for m in range(2):
                    project(("qD", m), 0, m * P, P)
                project("kvD", 0, 256, P)
                pe.wait_ge(win_landed[1], 16)
                for m in range(2):
                    project(("qi", m), 1, m * P, P)
                project("kiwi", 1, 256, 40)
                wait_drained(pe, "kvD")
                turn("vDT", [(bank("vDT")[:, i * 64:(i + 1) * 64], vdT[0:64, i * P:(i + 1) * P], 64) for i in range(TT)])
                wait_drained(pe, "kiwi")
                turn("wiT", [(bank("wiT")[:, i * 8:(i + 1) * 8], kiwiT[0:8, i * P:(i + 1) * P], 8) for i in range(TT)])
                for i in range(1, TT):
                    for h in range(IDX_HEADS):
                        name, r = ("idx", i, h), slice(32 * (h % 4), 32 * (h % 4) + 32)
                        wait_bank(pe, name)
                        mm(bank(name)[:, 0:P * (i + 1)], qi[r, h // 4, i * P:(i + 1) * P], ki[r, 0:P * (i + 1)])\
                            .then_inc(psum_filled, 1)
                pe.wait_ge(win_landed[2], 16)
                for m in range(2):
                    project(("cq", m), 2, m * P, P)
                project("ckv", 2, 256, P)
                pe.wait_ge(small_landed, SMALLS * 16)
                features("kr", 2 * ROPE, lambda k: wkr[:, k, :], hT, KT)
                pe.wait_ge(win_landed[3], 16)
                for m in range(2):
                    project(("qA", m), 3, m * P, P)
                project(("kA", 0), 3, 256, P)
                pe.wait_ge(win_landed[4], 16)
                project(("kA", 1), 4, 0, P)
                for i in range(TT):
                    wait_bank(pe, ("vA", i))
                    for k in range(KT):
                        last = mm(bank(("vA", i))[:, 0:260], hT[:, k, i * P:(i + 1) * P], slot(4, 388)[:, k, 128:388],
                                  k == 0, k == KT - 1)
                    last.then_inc(psum_filled, 1)
                wait_drained(pe, ("vA", TT - 1))
                turn("afT", [(bank("afT")[0:4, i * P:(i + 1) * P], vA[:, i, 256:260], P) for i in range(TT)])
                pe.wait_ge(cq_squared, 3)
                wait_bank(pe, "ssq")
                for m in range(2):
                    last = mm(bank("ssq")[:, :], ones[:, :], sqT[:, m, :], m == 0, m == 1)
                last.then_inc(psum_filled, 1)
                wait_bank(pe, "ssk")
                mm(bank("ssk")[:, :], ones[:, :], sqT[:, 2, :]).then_inc(psum_filled, 1)
                pe.wait_ge(win_landed[5], 16)
                for m in range(2):
                    project(("qC", m), 5, m * P, P)
                project("kC", 5, 256, P)
                pe.wait_ge(win_landed[6], 16)
                wait_bank(pe, "vC")
                for i in range(TT):
                    for k in range(KT):
                        last = mm(bank("vC")[:, i * P:(i + 1) * P], hT[:, k, i * P:(i + 1) * P], slot(6, 128)[:, k, :],
                                  k == 0, k == KT - 1)
                last.then_inc(psum_filled, 1)
                pe.wait_ge(latents_ready, 1)
                pe.wait_ge(small_landed, SMALLS * 16)
                for m in range(2):
                    features(("qBn", m), P, lambda k: wq_n[:, k, m * P:(m + 1) * P], cqT, 2)
                features("qBr", P, lambda k: wq_r[:, k, :], cqT, 2)
                features("qBs", P, lambda k: wq_s[:, k, :], cqT, 2)
                for m in range(2):
                    wait_bank(pe, ("kBn", m))
                    mm(bank(("kBn", m))[:, :], wk_n[:, m * P:(m + 1) * P], ckvT).then_inc(psum_filled, 1)
                for m in range(2):
                    wait_bank(pe, ("vB", m))
                    for j in range(2):
                        i = 2 * m + j
                        last = mm(bank(("vB", m))[:, j * 256:(j + 1) * 256], ckvT[:, i * P:(i + 1) * P], wk_v[:, :])
                    last.then_inc(psum_filled, 1)

                Q = {"A": qA, "B": qB, "C": qC, "D": qD}
                K = {"A": lambda h: kA[:, h, :], "B": lambda h: kB[:, h, :], "C": lambda h: kC[:, h // 2, :],
                     "D": lambda h: kD[:, :]}
                V = {"A": lambda h, t: vA[:, t, h * HD:(h + 1) * HD], "B": lambda h, t: vB[:, t, h * HD:(h + 1) * HD],
                     "C": lambda h, t: vC[:, t, (h // 2) * HD:(h // 2 + 1) * HD], "D": lambda h, t: vD[:, t, :]}

                def unit_scores(u):
                    g, i, h = UNITS[u]
                    k0, n = keys(g, i)
                    rows = NOPE + ROPE if g == "B" else HD + 2
                    wait_bank(pe, ("S", u))
                    mm(bank(("S", u))[:, 0:n], Q[g][0:rows, h, i * P:(i + 1) * P], K[g](h)[0:rows, k0:k0 + n])\
                        .then_inc(psum_filled, 1)

                def unit_turn(u):
                    g, i, _ = UNITS[u]
                    pe.wait_ge(probs_ready, u + 1)
                    b = bank(("T", u))
                    turn(("T", u), [(b[:, t * P:(t + 1) * P], tring[:, u % 4, t * P:(t + 1) * P], P)
                                    for t in range(keys(g, i)[1] // P)])

                def unit_values(u):
                    g, i, h = UNITS[u]
                    k0, n = keys(g, i)
                    og = u // HEADS
                    if h == 0 and og >= 2:
                        pe.wait_ge(o_drained, og - 1)
                    wait_drained(pe, ("T", u))
                    for t in range(n // P):
                        last = mm(banks[6 + og % 2][:, h * HD:(h + 1) * HD], pring[:, u % 3, t * P:(t + 1) * P],
                                  V[g](h, k0 // P + t), t == 0, t == n // P - 1)
                    if h == HEADS - 1:
                        last.then_inc(o_filled, 1)

                pe.wait_ge(forget_landed, 8 * 16)
                pe.wait_ge(qrope_ready, 1)
                wait_drained(pe, ("vB", 1))
                for u in range(3):
                    unit_scores(u)
                for u in range(len(UNITS)):
                    unit_turn(u)
                    if u + 3 < len(UNITS):
                        unit_scores(u + 3)
                    if u > 0:
                        unit_values(u - 1)
                unit_values(last_unit)
                pe.wait_ge(o_drained, len(UNITS) // HEADS)
                for k in range(KT):
                    turn_rows(("mT", k), k)
                pe.wait_ge(diag_ready, 1)

                def spread(name, m):
                    wait_bank(pe, (name, m))
                    mm(bank((name, m))[:, :], ones[:, :], diag[:, m * 512:(m + 1) * 512]).then_inc(psum_filled, 1)

                for m in range(2):
                    spread("gt1", m)
                wait_drained(pe, ("mT", KT - 1))
                wait_drained(pe, ("mT", KT - 2))
                pe.wait_ge(wout_landed, 16)
                for i in range(TT):
                    for m in range(2):
                        name = ("out", i, m)
                        wait_bank(pe, name)
                        for k in range(KT):
                            last = mm(bank(name)[:, :], hT[:, k, i * P:(i + 1) * P], wo[:, k, m * 512:(m + 1) * 512],
                                      k == 0, k == KT - 1)
                        last.then_inc(psum_filled, 1)
                pe.wait_ge(xhat_ready, 2 * TT)
                for k in range(KT):
                    turn_rows(("h2", k), k)
                wait_drained(pe, ("h2", KT - 1))
                wait_drained(pe, ("h2", KT - 2))
                wait_bank(pe, "router")
                for i in range(TT):
                    for k in range(KT):
                        last = mm(bank("router")[:, i * NE:(i + 1) * NE], hT[:, k, i * P:(i + 1) * P], wr[:, k, :],
                                  k == 0, k == KT - 1)
                last.then_inc(psum_filled, 1)
                pe.wait_ge(diag_ready, 2)
                for m in range(2):
                    spread("gt2", m)
                pe.wait_ge(act_drained, count["act"])
                pe.wait_ge(dve_drained, count["dve"])
                with pe.Fori(0, NE // 2) as pair:
                    for s in range(2):
                        e = pair * 2 + s
                        g, u, d = expert(s)
                        pe.wait_ge(expert_landed[s], (pair + 1) * 48)
                        for f in range(2):
                            pe.wait_ge(hidden_ready, e * 2 + (f + 1))
                            for b, w in ((2 * f, g), (2 * f + 1, u)):
                                for k in range(KT):
                                    last = mm(banks[b][:, :], w[:, k, f * P:(f + 1) * P], hT[:, k, :], k == 0, k == KT - 1)
                                last.then_inc(gu_filled, 1)
                        pe.wait_ge(hidden_ready, e * 2 + 4)
                        for n in range(MOE_DN):
                            i, m = n // 2, n % 2
                            pe.wait_ge(acc_done, e * MOE_DN + (n + 5))
                            for f in range(2):
                                last = mm(banks[4 + n % 4][:, :], tring[:, 2 + f, i * P:(i + 1) * P],
                                          d[:, f, m * 512:(m + 1) * 512], f == 0, f == 1)
                            last.then_inc(down_filled, 1)
                pe.sem_inc(layer_end, 1)
                pe.wait_ge(layer_go, l + 1)

        @block.sync
        def _(sp):
            for dst, src in [(x[:, :, :], x_in.rearrange("b (i p) d -> p (b i) d", p=P)),
                             (ident[:, :], k_ident), (causal[:, :], k_causal), (window[:, :], k_window),
                             (qC[64:66, :, :], k_rows[:, 0:4, :]), (kC[64:66, :, :], k_rows[:, 4:6, :]),
                             (qD[64:66, :, :], k_rows[:, 6:10, :]), (kD[64:66, :], k_rows[:, 10, :]),
                             (qA[65:66, :, :], k_rows[0:1, 11:15, :]), (kA[64:65, :, :], k_rows[0:1, 15:19, :]),
                             (wr[:, :, :], w_router.rearrange("(k p) e -> p k e", p=P)),
                             (brt, b_router.rearrange("(a e) -> a e", a=1).partition_broadcast(P)),
                             (cT, c_in.rearrange("b (k p) -> p (b k)", p=P))]:
                sp.dma_start(dst, src, allow_slow_non_contiguous=True).then_inc(consts_landed, 16)

            with sp.Fori(0, DEPTH) as l:
                def layer(t):
                    return t[bass.ds(l, 1)]

                def flat(t, pattern, **kw):
                    return layer(t).rearrange(pattern, **kw)

                for dst, src in [(vecT[:, 0:8], flat(g_norm1, "a (k p) -> p (a k)", p=P)),
                                 (vecT[:, 8:16], flat(g_norm2, "a (k p) -> p (a k)", p=P)),
                                 (vecT[:, 16:18], flat(g_q_mla, "a (k p) -> p (a k)", p=P)),
                                 (vecT[:, 18:19], flat(g_kv_mla, "a (k p) -> p (a k)", p=P)),
                                 (bfg[0:4, :], flat(b_forget, "a h -> h a")),
                                 (sinkb, layer(sinks).partition_broadcast(P))]:
                    sp.dma_start(dst, src, allow_slow_non_contiguous=True).then_inc(small_landed, 16)
                wq = flat(w_q_up, "a (k p) (h e) -> p (a k) h e", p=P, h=HEADS)
                for k in range(2):
                    sp.dma_start(wq_n[:, k, :].rearrange("p (h e) -> p h e", h=HEADS),
                                 wq[:, k, :, 0:NOPE]).then_inc(small_landed, 16)
                    sp.dma_start(wq_r[:, k, :].rearrange("p (h e) -> p h e", h=HEADS),
                                 wq[:, k, :, NOPE:]).then_inc(small_landed, 16)
                    for a in range(2):
                        sp.dma_start(wq_s[:, k, :].rearrange("p (h b e) -> p h b e", h=HEADS, b=2)[:, :, a, :],
                                     wq[:, k, :, NOPE + 16 * (1 - a):NOPE + 16 * (2 - a)],
                                     allow_slow_non_contiguous=True).then_inc(small_landed, 16)
                wkv = flat(w_kv_up, "a p (h b e) -> p (a h) b e", h=HEADS, b=2)
                sp.dma_start(wk_n[:, :].rearrange("p (h e) -> p h e", h=HEADS), wkv[:, :, 0, :]).then_inc(small_landed, 16)
                sp.dma_start(wk_v[:, :].rearrange("p (h e) -> p h e", h=HEADS), wkv[:, :, 1, :]).then_inc(small_landed, 16)

                wi_d = flat(w_in, "a (k p) n -> p (a k) n", p=P)
                for at, frm, n in ((0, 0, ROPE), (ROPE, ROPE // 2, ROPE // 2), (ROPE * 3 // 2, 0, ROPE // 2)):
                    sp.dma_start(wkr[:, :, at:at + n], wi_d[:, :, OFF["bkr"] + frm:OFF["bkr"] + frm + n],
                                 allow_slow_non_contiguous=True).then_inc(small_landed, 16)

                sp.wait_ge(bias_zeroed, 1)
                wa = flat(w_ada, "a (k p) n -> p (a k) n", p=P)
                for n in range(MOD_CHUNKS):
                    if n >= 3:
                        sp.wait_ge(ada_used, n - 2)
                    sp.dma_start(ada_slot(n), wa[:, :, n * 512:(n + 1) * 512]).then_inc(ada_landed[n % 3], 16)
                    if n >= 2:
                        sp.wait_ge(ada_used, n - 1)
                    sp.dma_start(ada_bias[n % 2][0:1, :], layer(b_ada)[:, n * 512:(n + 1) * 512])\
                        .then_inc(bada_landed[n % 2], 16)
                sp.wait_ge(ada_used, MOD_CHUNKS)

                for n, (_, cols) in enumerate(CHUNKS):
                    if n >= SLOTS:
                        wait_filled(sp, chunk_last_job[n - SLOTS])
                    sp.dma_start(slot(n, cols), wi_d[:, :, CHUNK_AT[n]:CHUNK_AT[n] + cols]).then_inc(win_landed[n], 16)
                sp.wait_ge(relu_used, 3 * IDX_HEADS)
                sp.dma_start(cosT, k_cos).then_inc(rope_landed, 16)
                sp.dma_start(sinT, k_sin).then_inc(rope_landed, 16)
                sp.wait_ge(forget_ready, 2)
                for h in range(HEADS):
                    sp.dma_start(qA[64:65, h, :], fg[0][h:h + 1, :]).then_inc(forget_landed, 16)
                    sp.dma_start(kA[65:66, h, :], fg[1][h:h + 1, :]).then_inc(forget_landed, 16)
                wait_filled(sp, "vC")
                sp.dma_start(wo, flat(w_out, "a (k p) n -> p (a k) n", p=P)).then_inc(wout_landed, 16)

                wait_filled(sp, ("out", TT - 1, 1))

                def load(e, s):
                    g, u, d = expert(s)
                    at = (bass.ds(l, 1), bass.ds(e, 1))
                    sp.dma_start(g, w_gate[at].rearrange("a e (k p) f -> p (a e k) f", p=P)).then_inc(expert_landed[s], 16)
                    sp.dma_start(u, w_up[at].rearrange("a e (k p) f -> p (a e k) f", p=P)).then_inc(expert_landed[s], 16)
                    sp.dma_start(d, w_down[at].rearrange("a e (k p) f -> p (a e k) f", p=P)).then_inc(expert_landed[s], 16)
                load(0, 0)
                load(1, 1)
                with sp.Fori(1, NE // 2) as pair:
                    for s in range(2):
                        sp.wait_ge(down_filled, (pair * 2 + (s - 1)) * MOE_DN)
                        load(pair * 2 + s, s)

                sp.wait_ge(layer_end, (l + 1) * 4)
                sp.sem_inc(layer_passed, 1)
                for s, last in totals.items():
                    sp.wait_ge(s, last)
                sp.sem_clear(range(first_layer_sem.num, last_layer_sem.num + 1))
                sp.sem_inc(layer_go, 1)
            sp.dma_start(gtB[:, :], g_final.rearrange("(a n) -> a n", a=1).partition_broadcast(P)).then_inc(consts_landed, 16)
            for i in range(TT):
                sp.wait_ge(fin_rows, i + 1)
                sp.dma_start(out.rearrange("b (i p) d -> p (b i) d", p=P)[:, i, :], tok[:, i, :]).then_inc(stored, 16)
            sp.wait_ge(stored, 16 * TT)


_INS = ["x", "c", "w_ada", "b_ada", "g_norm1", "w_in", "b_forget", "g_q_mla", "w_q_up", "g_kv_mla", "w_kv_up",
        "sinks", "w_out", "g_norm2", "w_router", "b_router", "w_gate", "w_up", "w_down", "g_final"]


def kernel(**inputs):
    import concourse.bacc as _bacc
    from concourse.bass_utils import run_bass_kernel_spmd as _run

    nc = _bacc.Bacc("TRN2", target_bir_lowering=False, num_devices=1)
    arrays, args = {}, []
    given = {name: np.ascontiguousarray(inputs[name]) for name in _INS}
    given.update(constants())
    for name, a in given.items():
        arrays[f"in_{name}"] = a
        args.append(nc.dram_tensor(f"in_{name}", a.shape, mybir.dt.from_np(a.dtype), kind="ExternalInput").ap())
    args.append(nc.dram_tensor("out_0", (1, SEQ, D), F32, kind="ExternalOutput").ap())
    trunk(nc, *args)
    r = _run(nc, [arrays], core_ids=[0])
    return r.results[0]["out_0"]
```

```python
import concourse.bass as bass
from concourse import mybir
import numpy as np

F32 = mybir.dt.float32
I32 = mybir.dt.int32
ALU = mybir.AluOpType
ACT = mybir.ActivationFunctionType
AX = mybir.AxisListType

P = 128
SEQ, D, DEPTH = 512, 1024, 2
TT = SEQ // P
KT = D // P
HD = 64
HEADS = 4
NE, NG, FE = 16, 4, 256
EPS = 1e-6
IDX_HEADS, IDX_DIM, TOPK = 8, 32, 128
NOPE, ROPE = 64, 32
QR, KVR = 256, 128
NEG = -1e30
TAKEN = -3e38
BIG = 3e38

SIZES = [256, 256, 256, 4, 256, 128, 32, 256, 128, 128, 256, 64, 64, 256, 32, 8]
NAMES = ["aq", "ak", "av", "af", "bcq", "bckv", "bkr", "cq", "ck", "cv", "dq", "dk", "dv", "dqi", "dki", "dwi"]
OFF = {n: int(sum(SIZES[:i])) for i, n in enumerate(NAMES)}
N_IN = sum(SIZES)
CHUNKS = [("dq", 384), ("dqi", 296), ("bcq", 384), ("aq", 384), ("ak2", 388), ("cq", 384), ("cv", 128)]
CHUNK_AT = [OFF["dq"], OFF["dqi"], OFF["bcq"], OFF["aq"], OFF["aq"] + 384, OFF["cq"], OFF["cv"]]
SLOTS, SLOT = 4, 8 * 388
MOD_CHUNKS = 6 * D // 512

MAX_TILES = NE + 8
OTHERS = MAX_TILES - NE

GROUPS = "ABCD"
UNITS = [(g, i, h) for g in GROUPS for i in range(TT) for h in range(HEADS)]


def keys(g, i):
    if g == "C":
        return (0, P) if i == 0 else ((i - 1) * P, 2 * P)
    return 0, P * (i + 1)


def plan():
    jobs = [("mod", "dve")]
    jobs += [(("h1", k), "act" if k % 2 else "dve") for k in range(KT)]
    jobs += [(("qD", m), "act") for m in range(2)] + [("kvD", "act")]
    jobs += [(("qi", m), "dve") for m in range(2)] + [("kiwi", "dve"), ("vDT", "act"), ("wiT", "dve")]
    jobs += [(("idx", i, h), "act") for i in range(1, TT) for h in range(IDX_HEADS)]
    jobs += [(("cq", m), "act") for m in range(2)] + [("ckv", "act"), ("kr", "act")]
    jobs += [(("qA", m), "act") for m in range(2)] + [(("kA", m), "act") for m in range(2)]
    jobs += [(("vA", i), "act") for i in range(TT)] + [("afT", "act"), ("ssq", "act"), ("ssk", "act")]
    jobs += [(("qC", m), "act") for m in range(2)] + [("kC", "act"), ("vC", "act")]
    jobs += [(("qBn", m), "act") for m in range(2)] + [("qBr", "dve"), ("qBs", "dve")]
    jobs += [(("kBn", m), "act") for m in range(2)] + [(("vB", m), "act") for m in range(2)]
    n = len(UNITS)
    jobs += [(("S", u), "dve") for u in range(3)]
    for u in range(n):
        jobs += [(("T", u), "act" if u % 2 else "dve")]
        if u + 3 < n:
            jobs += [(("S", u + 3), "dve")]
    jobs += [(("mT", k), "act" if k % 2 else "dve") for k in range(KT)]
    jobs += [((name, m), "act") for name in ("gt1", "sc2", "sh2") for m in range(2)]
    jobs += [(("out", i, m), "dve") for i in range(TT) for m in range(2)]
    jobs += [(("h2", k), "act" if k % 2 else "dve") for k in range(KT)]
    jobs += [(("gt2", m), "act") for m in range(2)] + [("router", "act"), ("pos", "dve"), ("inv", "dve")]
    return jobs


def constants():
    q = np.arange(P)[:, None]
    c = np.arange(SEQ)[None, :]
    causal = np.where(c - (SEQ - P) > q, NEG, 0.0)
    dist = q - np.arange(2 * P)[None, :] + P
    window = np.where((dist >= 0) & (dist < P), 0.0, NEG)
    half = ROPE // 2
    inv = 10000.0 ** (-np.arange(half, dtype=np.float32) / np.float32(half))
    ang = (np.arange(SEQ, dtype=np.float32)[None, :] * inv.astype(np.float32)[:, None]).astype(np.float32)
    cos = np.tile(np.cos(ang), (8, 1))
    sin = np.tile(np.concatenate([-np.sin(ang), np.sin(ang)]), (4, 1))
    pos = np.arange(SEQ, dtype=np.float64)
    slopes = 2.0 ** (-np.arange(1, 9, dtype=np.float64))
    rows = np.zeros((2, 4 + 2 + 4 + 1 + 4 + 4, SEQ))
    for n, s in enumerate(slopes):
        at = n if n < 4 else 6 + n - 4
        rows[0, at] = -8 * s * pos
        rows[1, at] = 8 * s
    for at in (4, 5, 10):
        rows[0, at] = 1
        rows[1, at] = pos
    rows[:, 11:] = 1
    route = np.concatenate([np.broadcast_to(np.arange(P), (P, P)), np.triu(np.ones((P, P)), 1),
                            np.arange(TT)[None, :] * P + q], axis=1)
    f = lambda a: np.ascontiguousarray(a, dtype=np.float32)
    return {"k_causal": f(causal), "k_window": f(window), "k_cos": f(cos), "k_sin": f(sin),
            "k_rows": f(rows), "k_ident": f(np.eye(P)), "k_route": f(route), "k_zero": f(np.zeros((P, D)))}


def trunk(nc, x_in, c_in, w_ada, b_ada, g_norm1, w_in, b_forget, g_q_mla, w_q_up, g_kv_mla, w_kv_up, sinks,
          w_out, g_norm2, w_router, b_router, w_gate, w_up, w_down, g_final,
          k_causal, k_window, k_cos, k_sin, k_rows, k_ident, k_route, k_zero, out):

    def sb(name, *shape):
        return nc.alloc_sbuf_tensor(name, [P, *shape], F32)

    x = sb("x", TT, D)
    hT = sb("hT", KT, SEQ)
    wbuf = sb("wbuf", SLOTS * SLOT)
    tok = sb("tok", TT, D)
    qA, kA = sb("qA", 4, SEQ), sb("kA", 4, SEQ)
    qB, kB = sb("qB", 4, SEQ), sb("kB", 4, SEQ)
    qC, kC = sb("qC", 4, SEQ), sb("kC", 2, SEQ)
    qD, kD = sb("qD", 4, SEQ), sb("kD", SEQ)
    vA, vB, vC, vD = sb("vA", TT, 260), sb("vB", TT, 256), sb("vC", TT, 128), sb("vD", TT, 64)
    qi, ki = sb("qi", 2, SEQ), sb("ki", SEQ)
    tring = sb("tring", 4, SEQ)
    pring = sb("pring", 3, SEQ)
    wq_n, wq_r, wq_s = sb("wq_n", 2, 256), sb("wq_r", 2, 128), sb("wq_s", 2, 128)
    wk_n, wk_v = sb("wk_n", 256), sb("wk_v", 256)
    ident, ones = sb("ident", P), sb("ones", P)
    causal, window = sb("causal", SEQ), sb("window", 2 * P)
    selmask = sb("selmask", 9 * P)
    gtB = sb("gtB", D)
    modT = sb("modT", 48)
    vecT = sb("vecT", 20)
    scaleT = sb("scaleT", 16)
    small = sb("small", 512)
    cT = small[:, 0:8]
    cact = small[:, 8:16]
    ss = small[:, 16:20]
    rstd = small[:, 20:24]
    sinkb = small[:, 24:28]
    nsink = small[:, 28:32]
    brt = small[:, 32:48]
    bfg = small[:, 48:49]
    epsc = small[:, 49:50]
    onec = small[:, 50:51]
    rsd = small[:, 52:56]
    max8 = small[:, 56:64]
    wi = small[:, 64:96].rearrange("p (i h) -> p i h", i=TT)
    nbfg = small[:, 96:97]
    nmax = small[:, 128:192]
    sums = small[:, 192:256]
    route = sb("route", 2 * P + TT)
    iota, before, token = route[:, 0:P], route[:, P:2 * P], route[:, 2 * P:2 * P + TT]
    ints = nc.alloc_sbuf_tensor("ints", [P, 128], I32)
    row_of = ints[:, 0:8]
    tile_i, slot_i = ints[:, 8:16], ints[:, 16:24]
    token_of = ints[:, 24:24 + MAX_TILES]
    expert_of = ints[:, 48:48 + MAX_TILES]
    pairs_i = ints[:, 72:73]
    gather_idx = [ints[:, 73:74], ints[:, 74:75]]
    wr = sb("wr", KT, NE)
    wkr = sb("wkr", KT, 2 * ROPE)

    latent = tok[:, :, :].rearrange("p i n -> p (i n)")
    cqT = latent[:, 0:1024].rearrange("p (m n) -> p m n", m=2)
    ckvT = latent[:, 1024:1536]
    krT, krS = latent[:, 1536:2048], latent[:, 3584:4096]
    sqT = latent[:, 2048:3584].rearrange("p (m n) -> p m n", m=3)
    rope1, rope2 = qi[:, 0, :], qi[:, 1, :]
    cosT, sinT = pring[:, 0, :], pring[:, 1, :]
    rq, rk = gtB[:, 0:512], gtB[:, 512:1024]
    vdT, kiwiT = tring[:, 2, :], tring[:, 3, :]
    score = tring[:, 0, :]
    relu = [pring[:, 0, :], pring[:, 1, :], pring[:, 2, :]]
    fg = [kB[0:4, n, :] for n in range(4)]
    tflat = tring[:, :, :].rearrange("p a n -> p (a n)")
    pflat = pring[:, :, :].rearrange("p a n -> p (a n)")
    diags = [tflat[:, 0:D], tflat[:, D:2 * D], pflat[:, 0:D], pflat[:, 0:D]]
    sc2B = vA[:, :, :].rearrange("p i n -> p (i n)")[:, 0:D]
    sh2B = vB[:, :, :].rearrange("p i n -> p (i n)")
    rout = qi[:, 0, :].rearrange("p (n e) -> p n e", e=64)
    mk = qi[:, 1, 0:128].rearrange("p (c n) -> p c n", c=2)
    prod = qi[:, 1, 128:256].rearrange("p (c n) -> p c n", c=2)
    posb, rowf = qi[:, 1, 256:336], qi[:, 1, 336:400]
    tiny = qi[:, 1, 400:512]
    vcf = vC[:, :, :].rearrange("p i n -> p (i n)")
    in_slot = tflat[:, 0:8 * P].rearrange("p (n s) -> p n s", n=8)
    in_tile = vcf[:, 0:8 * MAX_TILES].rearrange("p (n s) -> p n s", n=8)
    xg, ysb = [tok[:, s, :] for s in range(2)], [tok[:, 2 + s, :] for s in range(2)]
    xgT = [hT[:, 2 * s:2 * s + 2, :].rearrange("p a n -> p (a n)") for s in range(2)]
    sg = [tflat[:, D + 256 * s:D + 256 * (s + 1)] for s in range(2)]
    hid = [tflat[:, D + 512 + 256 * s:D + 512 + 256 * (s + 1)] for s in range(2)]
    h2_rows = nc.dram_tensor("h2_rows", [SEQ, D], F32, kind="Internal").ap()
    y_rows = nc.dram_tensor("y_rows", [MAX_TILES * P, D], F32, kind="Internal").ap()

    banks = [nc.alloc_psum_tensor(f"bank{n}", [P, 512], F32) for n in range(8)]

    sem = nc.alloc_semaphore
    consts_landed, consts_set = sem("consts_landed"), sem("consts_set")
    layer_passed = sem("layer_passed")
    layer_end, layer_go, stored = sem("layer_end"), sem("layer_go"), sem("stored")
    c_ready = sem("c_ready")
    fin_squares, fin_root, fin_rstd, fin_rows = sem("fin_squares"), sem("fin_root"), sem("fin_rstd"), sem("fin_rows")
    small_landed, bias_zeroed, nsink_ready = sem("small_landed"), sem("bias_zeroed"), sem("nsink_ready")
    ada_landed = [sem(f"ada_landed{n}") for n in range(3)]
    bada_landed = [sem(f"bada_landed{n}") for n in range(2)]
    ada_used, ada_summed = sem("ada_used"), sem("ada_summed")
    win_landed = [sem(f"win_landed{n}") for n in range(len(CHUNKS))]
    rope_landed, wout_landed = sem("rope_landed"), sem("wout_landed")
    psum_filled, act_drained, dve_drained = sem("psum_filled"), sem("act_drained"), sem("dve_drained")
    dve_step, act_step = sem("dve_step"), sem("act_step")
    squares_ready, root_ready, xhat_ready = sem("squares_ready"), sem("root_ready"), sem("xhat_ready")
    relu_used, topk_done = sem("relu_used"), sem("topk_done")
    cq_squared, latents_ready, krope_ready = sem("cq_squared"), sem("latents_ready"), sem("krope_ready")
    qrope_ready, scales_ready = sem("qrope_ready"), sem("scales_ready")
    forget_ready, forget_landed = sem("forget_ready"), sem("forget_landed")
    softplus_ready = sem("softplus_ready")
    probs_ready = sem("probs_ready")
    o_filled, o_drained = sem("o_filled"), sem("o_drained")
    diag_ready, gated_ready, x_added = sem("diag_ready"), sem("gated_ready"), sem("x_added")
    rows2_scaled, rows2_ready, h2_stored = sem("rows2_scaled"), sem("rows2_ready"), sem("h2_stored")
    chosen, gates_ready, onehots_ready, routed = sem("chosen"), sem("gates_ready"), sem("onehots_ready"), sem("routed")
    gu_landed, d_landed = [sem(f"gu_landed{n}") for n in range(2)], [sem(f"d_landed{n}") for n in range(2)]
    idx_ready, y_cleared = sem("idx_ready"), sem("y_cleared")
    xg_landed = [sem(f"xg_landed{n}") for n in range(2)]
    xt_filled, xt_act, xt_dve = sem("xt_filled"), sem("xt_act"), sem("xt_dve")
    gu_filled, silu_ready, hidden_ready = sem("gu_filled"), sem("silu_ready"), sem("hidden_ready")
    down_filled, y_act, y_dve = sem("down_filled"), sem("y_act"), sem("y_dve")
    y_stored = [sem(f"y_stored{n}") for n in range(2)]
    choice_landed = [sem(f"choice_landed{n}") for n in range(TT)]
    sp_passed, pool_passed = sem("sp_passed"), sem("pool_passed")
    last_of_layer = sem("combined")
    combined = last_of_layer
    first_layer_sem, last_layer_sem = small_landed, last_of_layer

    jobs = plan()
    index = {name: n for n, (name, _) in enumerate(jobs)}
    drainer = dict(jobs)
    ordinal, count = {}, {"act": 0, "dve": 0}
    for name, engine in jobs:
        count[engine] += 1
        ordinal[name] = count[engine]
    RING = 6

    def bank(name):
        return banks[index[name] % RING]

    def wait_filled(eng, name):
        eng.wait_ge(psum_filled, index[name] + 1)

    def wait_drained(eng, name):
        eng.wait_ge(act_drained if drainer[name] == "act" else dve_drained, ordinal[name])

    def wait_bank(pe, name):
        if index[name] >= RING:
            wait_drained(pe, jobs[index[name] - RING][0])

    def slot(n, cols):
        at = (n % SLOTS) * SLOT
        return wbuf[:, at:at + KT * cols].rearrange("p (k n) -> p k n", k=KT)

    def ada_slot(n):
        return wbuf[:, (n % 3) * 4096:(n % 3 + 1) * 4096].rearrange("p (k n) -> p k n", k=KT)

    ada_bias = [pring[:, 0, :], pring[:, 1, :]]
    ada_acc = [tring[:, 0, :], tring[:, 1, :]]
    wo = wbuf[:, 0:KT * D].rearrange("p (k n) -> p k n", k=KT)

    def expert(s):
        b = s * 6144
        return (wbuf[:, b:b + 2048].rearrange("p (k f) -> p k f", k=KT),
                wbuf[:, b + 2048:b + 4096].rearrange("p (k f) -> p k f", k=KT),
                wbuf[:, b + 4096:b + 6144].rearrange("p (k n) -> p k n", k=2))

    chunk_last_job = ["kvD", "kiwi", "ckv", ("kA", 0), ("vA", 3), "kC", "vC"]
    last_unit = len(UNITS) - 1

    def pairs_of(eng):
        eng.wait_ge(routed, 1)
        return eng.value_load(pairs_i[0:1, 0:1], min_val=NE // 2, max_val=MAX_TILES // 2)

    CONSTS, SMALLS = 14, 19
    totals = {small_landed: SMALLS * 16, bias_zeroed: 1, ada_used: MOD_CHUNKS, ada_summed: MOD_CHUNKS - 1,
              ada_landed[0]: 64, ada_landed[1]: 64, ada_landed[2]: 64, bada_landed[0]: 96, bada_landed[1]: 96,
              rope_landed: 32, wout_landed: 16,
              psum_filled: len(jobs), act_drained: count["act"], dve_drained: count["dve"],
              squares_ready: 2 * TT, root_ready: 2, xhat_ready: TT, relu_used: 3 * IDX_HEADS, topk_done: 3,
              cq_squared: 3, latents_ready: 1, krope_ready: 2, qrope_ready: 1, scales_ready: 2, nsink_ready: 1,
              forget_ready: 2, forget_landed: 8 * 16, softplus_ready: 1,
              probs_ready: len(UNITS), o_filled: len(UNITS) // HEADS, o_drained: len(UNITS) // HEADS,
              diag_ready: 4, gated_ready: TT, x_added: 3 * TT, gates_ready: 1, rows2_scaled: TT, rows2_ready: TT,
              h2_stored: 16 * TT, y_cleared: 16 * OTHERS, chosen: 1, onehots_ready: 1, routed: 1, combined: TT}
    for landed in choice_landed:
        totals[landed] = 32

    def pair_totals(pairs):
        return {gu_landed[0]: pairs * 32, gu_landed[1]: pairs * 32, d_landed[0]: pairs * 16, d_landed[1]: pairs * 16,
                idx_ready: pairs * 2, xg_landed[0]: pairs * 16, xg_landed[1]: pairs * 16, xt_filled: pairs * 4,
                xt_act: pairs * 2 + 2, xt_dve: pairs * 2 + 2, gu_filled: pairs * 2, silu_ready: pairs * 2,
                hidden_ready: pairs * 2, down_filled: pairs * 4, y_act: pairs * 2 + 2, y_dve: pairs * 2 + 2,
                y_stored[0]: pairs * 16 + 16, y_stored[1]: pairs * 16 + 16}

    for n, landed in enumerate(win_landed):
        totals[landed] = 16

    with nc.Block() as block:

        @block.gpsimd
        def _(pool):
            nc.gpsimd.memset(ones[:, :], 1.0).then_inc(consts_set, 1)
            nc.gpsimd.memset(epsc, EPS).then_inc(consts_set, 1)
            nc.gpsimd.memset(onec, 1.0).then_inc(consts_set, 1)
            with pool.Fori(0, DEPTH) as l:
                nc.gpsimd.memset(pring[:, 0:2, :], 0.0).then_inc(bias_zeroed, 1)
                pool.sem_inc(xt_act, 2)
                pool.sem_inc(xt_dve, 2)
                pool.sem_inc(y_act, 2)
                pool.sem_inc(y_dve, 2)
                pool.sem_inc(y_stored[0], 16)
                pool.sem_inc(y_stored[1], 16)
                for m, name in enumerate([("cq", 0), ("cq", 1), "ckv"]):
                    wait_drained(pool, name)
                    src = cqT[:, m, :] if m < 2 else ckvT
                    nc.gpsimd.tensor_tensor(sqT[:, m, :], src, src, ALU.mult).then_inc(cq_squared, 1)
                wait_drained(pool, "kr")
                pool.wait_ge(rope_landed, 32)
                nc.gpsimd.tensor_tensor(krT[0:32, :], krT[0:32, :], cosT[0:32, :], ALU.mult).then_inc(krope_ready, 1)
                nc.gpsimd.tensor_tensor(krS[0:32, :], krS[0:32, :], sinT[0:32, :], ALU.mult).then_inc(krope_ready, 1)
                for n in range(2 * TT):
                    wait_drained(pool, ("out", n // 2, n % 2))
                    xs = x[:, n // 2, (n % 2) * 512:(n % 2 + 1) * 512]
                    nc.gpsimd.tensor_tensor(xs, xs, tring[:, n % 4, :], ALU.add).then_inc(x_added, 1)
                for i in range(TT):
                    pool.wait_ge(rows2_scaled, i + 1)
                    wait_drained(pool, ("sh2", 1))
                    nc.gpsimd.tensor_tensor(tok[:, i, :], tok[:, i, :], sh2B, ALU.add).then_inc(rows2_ready, 1)
                pool.wait_ge(h2_stored, 16 * TT)
                wait_drained(pool, "inv")
                pairs = pairs_of(pool)
                with pool.Fori(0, pairs) as pair:
                    for s in range(2):
                        t = pair * 2 + s
                        pool.wait_ge(xt_act, t + 1)
                        pool.wait_ge(xt_dve, t + 1)
                        nc.gpsimd.tensor_copy(gather_idx[s], token_of[:, bass.ds(t, 1)]).then_inc(idx_ready, 1)
                        pool.wait_ge(idx_ready, t + 1)
                        pool.sem_inc(pool_passed, 1)
                        pool.indirect_dma_start(xg[s], None, h2_rows, bass.IndirectOffsetOnAxis(ap=gather_idx[s], axis=0))\
                            .then_inc(xg_landed[s], 16)
                pool.wait_ge(y_cleared, 16 * OTHERS)
                for s in range(2):
                    pool.wait_ge(y_stored[s], pairs * 16 + 16)
                pool.sem_inc(pool_passed, 1)
                for i in range(TT):
                    for c, dst in enumerate((tok[:, i, :], hT[:, 2 * i:2 * i + 2, :].rearrange("p a n -> p (a n)"))):
                        pool.indirect_dma_start(dst, None, y_rows,
                                                bass.IndirectOffsetOnAxis(ap=row_of[:, c * TT + i:c * TT + i + 1], axis=0))\
                            .then_inc(choice_landed[i], 16)
                for i in range(TT):
                    pool.wait_ge(gated_ready, i + 1)
                    nc.gpsimd.tensor_tensor(x[:, i, :], x[:, i, :], tok[:, i, :], ALU.add).then_inc(x_added, 1)
                pool.wait_ge(x_added, 3 * TT)
                for s in range(2):
                    pool.wait_ge(xg_landed[s], pairs * 16)
                    pool.sem_inc(pool_passed, 1)
                for landed in choice_landed:
                    pool.wait_ge(landed, 32)
                for first, last in ((xg_landed[0], xg_landed[-1]), (choice_landed[0], choice_landed[-1])):
                    pool.dma_reset(range(first.num, last.num + 1))
                pool.sem_inc(layer_end, 1)
                pool.wait_ge(layer_go, l + 1)

        @block.scalar
        def _(act):
            step = [0]

            def link(ins):
                step[0] += 1
                ins.then_inc(act_step, 1)
                act.wait_ge(act_step, step[0])

            def norm_roots(k):
                for i in range(TT):
                    nc.scalar.activation(tok[:, i, :], x[:, i, :], ACT.Square, accum_out=ss[:, i:i + 1])\
                        .then_inc(squares_ready, 1)
                act.wait_ge(squares_ready, TT * (k + 1))
                nc.scalar.activation(rstd, ss, ACT.Sqrt, bias=epsc, scale=1.0 / D).then_inc(root_ready, 1)

            def drain(name, *moves):
                wait_filled(act, name)
                for dst, src in moves:
                    last = nc.scalar.activation(dst, src, ACT.Copy)
                last.then_inc(act_drained, 1)

            def drain_pair(name, dst, m):
                b = bank(name)
                drain(name, (dst[0:64, 2 * m, :], b[0:64, :]), (dst[0:64, 2 * m + 1, :], b[64:128, :]))

            act.wait_ge(consts_landed, CONSTS * 16)
            act.wait_ge(consts_set, 3)
            nc.scalar.activation(cact, cT, ACT.Silu).then_inc(c_ready, 1)
            with act.Fori(0, DEPTH) as l:
                act.wait_ge(small_landed, SMALLS * 16)
                norm_roots(0)
                nc.scalar.activation(nsink, sinkb, ACT.Copy, scale=-1.0).then_inc(nsink_ready, 1)
                link(nc.scalar.activation(nbfg[0:4, :], bfg[0:4, :], ACT.Copy, scale=-1.0))
                act.wait_ge(scales_ready, 2)
                for k in range(1, KT, 2):
                    wait_filled(act, ("h1", k))
                    nc.scalar.activation(hT[:, k, :], bank(("h1", k))[:, :], ACT.Identity,
                                         bias=modT[:, k:k + 1], scale=scaleT[:, k:k + 1]).then_inc(act_drained, 1)
                for m in range(2):
                    drain_pair(("qD", m), qD, m)
                b = bank("kvD")
                drain("kvD", (kD[0:64, :], b[0:64, :]), (vdT[0:64, :], b[64:128, :]))
                drain("vDT", (vD[:, :, :].rearrange("p i n -> p (i n)"), bank("vDT")[:, 0:256]))
                for i in range(1, TT):
                    for h in range(IDX_HEADS):
                        n = (i - 1) * IDX_HEADS + h
                        wait_filled(act, ("idx", i, h))
                        if n >= 3:
                            act.wait_ge(relu_used, n - 2)
                        w = P * (i + 1)
                        nc.scalar.activation(relu[n % 3][:, 0:w], bank(("idx", i, h))[:, 0:w], ACT.Relu)\
                            .then_inc(act_drained, 1)
                for m in range(2):
                    drain(("cq", m), (cqT[:, m, :], bank(("cq", m))[:, :]))
                drain("ckv", (ckvT, bank("ckv")[:, :]))
                b = bank("kr")
                drain("kr", (krT[0:32, :], b[0:32, :]), (krS[0:32, :], b[32:64, :]))
                for m in range(2):
                    drain_pair(("qA", m), qA, m)
                for m in range(2):
                    drain_pair(("kA", m), kA, m)
                for i in range(TT):
                    drain(("vA", i), (vA[:, i, :], bank(("vA", i))[:, 0:260]))
                wait_filled(act, "afT")
                z = bank("afT")[0:4, :]
                link(nc.scalar.activation(fg[2], z, ACT.Abs, bias=bfg[0:4, :]))
                nc.scalar.activation(fg[3], z, ACT.Relu, bias=nbfg[0:4, :], scale=-1.0).then_inc(act_drained, 1)
                link(nc.scalar.activation(fg[2], fg[2], ACT.Exp, scale=-1.0))
                nc.scalar.activation(fg[2], fg[2], ACT.Ln, bias=onec[0:4, :]).then_inc(softplus_ready, 1)
                for name, dst, r in (("ssq", rq, QR), ("ssk", rk, KVR)):
                    wait_filled(act, name)
                    nc.scalar.activation(dst, bank(name)[:, :], ACT.Sqrt, bias=epsc, scale=1.0 / r).then_inc(act_drained, 1)
                for m in range(2):
                    drain_pair(("qC", m), qC, m)
                b = bank("kC")
                drain("kC", (kC[0:64, 0, :], b[0:64, :]), (kC[0:64, 1, :], b[64:128, :]))
                drain("vC", (vC[:, :, :].rearrange("p i n -> p (i n)"), bank("vC")[:, :]))
                for m in range(2):
                    drain_pair(("qBn", m), qB, m)
                act.wait_ge(forget_landed, 8 * 16)
                for m in range(2):
                    drain_pair(("kBn", m), kB, m)
                for m in range(2):
                    drain(("vB", m), (vB[:, 2 * m:2 * m + 2, :].rearrange("p i n -> p (i n)"), bank(("vB", m))[:, :]))

                def exps(u):
                    g, i, h = UNITS[u]
                    n = keys(g, i)[1] + (g == "C")
                    t = tring[:, u % 4, 0:n]
                    wait_drained(act, ("S", u))
                    nc.scalar.activation(t, t, ACT.Exp, bias=nmax[:, u:u + 1], scale=-1.0,
                                         accum_out=sums[:, u:u + 1]).then_inc(probs_ready, 1)

                for u in range(3):
                    exps(u)
                for u in range(len(UNITS)):
                    if u % 2:
                        n = keys(*UNITS[u][:2])[1]
                        drain(("T", u), (pring[:, u % 3, 0:n], bank(("T", u))[:, 0:n]))
                    if u + 3 < len(UNITS):
                        exps(u + 3)
                for k in range(1, KT, 2):
                    drain(("mT", k), (hT[:, k, :], bank(("mT", k))[:, :]))
                for name, dst in (("gt1", gtB[:, :]), ("sc2", sc2B), ("sh2", sh2B)):
                    for m in range(2):
                        drain((name, m), (dst[:, m * 512:(m + 1) * 512], bank((name, m))[:, :]))

                act.wait_ge(x_added, 2 * TT)
                norm_roots(1)
                for k in range(1, KT, 2):
                    drain(("h2", k), (hT[:, k, :], bank(("h2", k))[:, :]))
                for m in range(2):
                    drain(("gt2", m), (gtB[:, m * 512:(m + 1) * 512], bank(("gt2", m))[:, :]))
                wait_filled(act, "router")
                nc.scalar.activation(rout[:, 0, :], bank("router")[:, 0:64], ACT.Sigmoid).then_inc(act_drained, 1)
                pairs = pairs_of(act)
                with act.Fori(0, pairs) as pair:
                    for s in range(2):
                        act.wait_ge(xt_filled, pair * 4 + (2 * s + 1))
                        nc.scalar.activation(xgT[s][:, 0:512], banks[0][:, :], ACT.Copy).then_inc(xt_act, 1)
                    for s in range(2):
                        act.wait_ge(gu_filled, pair * 2 + (s + 1))
                        nc.scalar.activation(sg[s], banks[2 + s][:, 0:256], ACT.Silu).then_inc(silu_ready, 1)
                    for s in range(2):
                        act.wait_ge(down_filled, pair * 4 + (2 * s + 1))
                        act.wait_ge(y_stored[s], pair * 16 + 16)
                        nc.scalar.activation(ysb[s][:, 0:512], banks[4 + 2 * s][:, :], ACT.Copy).then_inc(y_act, 1)
                act.sem_inc(layer_end, 1)
                act.wait_ge(layer_go, l + 1)
            totals[act_step] = step[0]
            for i in range(TT):
                nc.scalar.activation(tok[:, i, :], x[:, i, :], ACT.Square, accum_out=ss[:, i:i + 1]).then_inc(fin_squares, 1)
            act.wait_ge(fin_squares, TT)
            nc.scalar.activation(rstd, ss, ACT.Sqrt, bias=epsc, scale=1.0 / D).then_inc(fin_root, 1)

        @block.vector
        def _(dve):
            step = [0]

            def link(ins):
                step[0] += 1
                ins.then_inc(dve_step, 1)
                dve.wait_ge(dve_step, step[0])

            def norm_rows(k):
                dve.wait_ge(root_ready, k + 1)
                link(nc.vector.reciprocal(rstd, rstd))
                for i in range(TT):
                    nc.vector.tensor_scalar(tok[:, i, :], x[:, i, :], rstd[:, i:i + 1], None, ALU.mult)\
                        .then_inc(xhat_ready, 1)

            def rank(dst, src, tmp):
                link(nc.vector.memset(dst, 0.0))
                G = src.shape[1]
                for j in range(4):
                    for lo, hi, op in ((0, j, ALU.is_gt), (j + 1, 4, ALU.is_ge)):
                        if lo < hi:
                            link(nc.vector.tensor_tensor(tmp[:, :, lo:hi], src[:, :, j:j + 1].to_broadcast([P, G, hi - lo]),
                                                         src[:, :, lo:hi], op))
                            link(nc.vector.tensor_tensor(dst[:, :, lo:hi], dst[:, :, lo:hi], tmp[:, :, lo:hi], ALU.add))

            dve.wait_ge(c_ready, 1)
            with dve.Fori(0, DEPTH) as l:
                for n in range(MOD_CHUNKS):
                    a, w = ada_acc[n % 2], ada_slot(n)
                    dve.wait_ge(ada_landed[n % 3], 16 * (n // 3 + 1))
                    dve.wait_ge(bada_landed[n % 2], 16 * (n // 2 + 1))
                    if n >= 2:
                        dve.wait_ge(ada_summed, n - 1)
                    for k in range(KT):
                        ins = nc.vector.scalar_tensor_tensor(out=a, in0=w[:, k, :], scalar=cact[:, k:k + 1],
                                                             in1=a if k else ada_bias[n % 2], op0=ALU.mult, op1=ALU.add)
                        if k < KT - 1:
                            link(ins)
                        else:
                            ins.then_inc(ada_used, 1)
                wait_filled(dve, "mod")
                nc.vector.tensor_copy(modT[:, :], bank("mod")[:, 0:48]).then_inc(dve_drained, 1)
                wait_drained(dve, "mod")
                dve.wait_ge(small_landed, SMALLS * 16)
                nc.vector.scalar_tensor_tensor(out=scaleT[:, 0:8], in0=modT[:, 8:16], scalar=1.0, in1=vecT[:, 0:8],
                                               op0=ALU.add, op1=ALU.mult).then_inc(scales_ready, 1)
                nc.vector.scalar_tensor_tensor(out=scaleT[:, 8:16], in0=modT[:, 32:40], scalar=1.0, in1=vecT[:, 8:16],
                                               op0=ALU.add, op1=ALU.mult).then_inc(scales_ready, 1)
                norm_rows(0)
                dve.wait_ge(scales_ready, 2)
                for k in range(0, KT, 2):
                    wait_filled(dve, ("h1", k))
                    nc.vector.tensor_scalar(hT[:, k, :], bank(("h1", k))[:, :], scaleT[:, k:k + 1], modT[:, k:k + 1],
                                            ALU.mult, ALU.add).then_inc(dve_drained, 1)
                for m in range(2):
                    wait_filled(dve, ("qi", m))
                    nc.vector.tensor_copy(qi[:, m, :], bank(("qi", m))[:, :]).then_inc(dve_drained, 1)
                wait_filled(dve, "kiwi")
                for r in range(4):
                    nc.vector.tensor_copy(ki[32 * r:32 * r + 32, :], bank("kiwi")[0:32, :])
                nc.vector.tensor_copy(kiwiT[0:8, :], bank("kiwi")[32:40, :]).then_inc(dve_drained, 1)
                wait_filled(dve, "wiT")
                nc.vector.tensor_scalar(wi, bank("wiT")[:, 0:32].rearrange("p (i h) -> p i h", i=TT),
                                        (IDX_HEADS * IDX_DIM) ** -0.5, None, ALU.mult).then_inc(dve_drained, 1)
                wait_drained(dve, "wiT")
                at = 0
                for i in range(1, TT):
                    w = P * (i + 1)
                    sc = score[:, 0:w]
                    for h in range(IDX_HEADS):
                        n = (i - 1) * IDX_HEADS + h
                        wait_drained(dve, ("idx", i, h))
                        r = relu[n % 3][:, 0:w]
                        if h == 0:
                            nc.vector.tensor_scalar(sc, r, wi[:, i, 0:1], None, ALU.mult).then_inc(relu_used, 1)
                        else:
                            nc.vector.scalar_tensor_tensor(out=sc, in0=r, scalar=wi[:, i, h:h + 1], in1=sc,
                                                           op0=ALU.mult, op1=ALU.add).then_inc(relu_used, 1)
                        dve.wait_ge(relu_used, n + 1)
                    link(nc.vector.tensor_tensor(sc[:, i * P:w], sc[:, i * P:w], causal[:, SEQ - P:SEQ], ALU.add))
                    for _ in range(TOPK // 8):
                        link(nc.vector.max(max8, sc))
                        link(nc.vector.match_replace(sc, max8, sc, TAKEN))
                    nc.vector.tensor_scalar(selmask[:, at:at + w], sc, TAKEN / 2, NEG, ALU.is_gt, ALU.mult)\
                        .then_inc(topk_done, 1)
                    dve.wait_ge(topk_done, i)
                    at += w
                wait_drained(dve, "afT")
                dve.wait_ge(softplus_ready, 1)
                link(nc.vector.tensor_tensor_scan(fg[1], fg[2], fg[3], 0.0, ALU.add, ALU.add))
                nc.vector.tensor_scalar(fg[0], fg[1], -8.0, None, ALU.mult).then_inc(forget_ready, 1)
                dve.wait_ge(forget_ready, 1)
                nc.vector.tensor_scalar(fg[1], fg[1], 8.0, None, ALU.mult).then_inc(forget_ready, 1)
                wait_drained(dve, "ssk")
                link(nc.vector.reciprocal(rq, rq))
                link(nc.vector.reciprocal(rk, rk))
                for m in range(2):
                    nc.vector.scalar_tensor_tensor(out=cqT[:, m, :], in0=cqT[:, m, :], scalar=vecT[:, 16 + m:17 + m],
                                                   in1=rq, op0=ALU.mult, op1=ALU.mult)
                nc.vector.scalar_tensor_tensor(out=ckvT, in0=ckvT, scalar=vecT[:, 18:19], in1=rk,
                                               op0=ALU.mult, op1=ALU.mult).then_inc(latents_ready, 1)
                dve.wait_ge(rope_landed, 32)
                wait_filled(dve, "qBr")
                nc.vector.tensor_tensor(rope1, bank("qBr")[:, :], cosT, ALU.mult).then_inc(dve_drained, 1)
                wait_filled(dve, "qBs")
                nc.vector.tensor_tensor(rope2, bank("qBs")[:, :], sinT, ALU.mult).then_inc(dve_drained, 1)
                wait_drained(dve, "qBs")
                dve.wait_ge(krope_ready, 2)
                for h in range(HEADS):
                    s = slice(32 * h, 32 * h + 32)
                    nc.vector.tensor_tensor(qB[64:96, h, :], rope1[s, :], rope2[s, :], ALU.add)
                    last = nc.vector.tensor_tensor(kB[64:96, h, :], krT[0:32, :], krS[0:32, :], ALU.add)
                last.then_inc(qrope_ready, 1)

                def scores(u):
                    g, i, h = UNITS[u]
                    n = keys(g, i)[1]
                    t = tring[:, u % 4, :]
                    if g == "C":
                        mask = window[:, 2 * P - n:2 * P]
                        nc.vector.tensor_copy(t[:, n:n + 1], nsink[:, h:h + 1])
                    elif g == "D" and i > 0:
                        at = P * (i * (i + 1) // 2 - 1)
                        mask = selmask[:, at:at + n]
                    else:
                        mask = causal[:, SEQ - n:SEQ]
                    scale = (NOPE + ROPE) ** -0.5 if g == "B" else HD ** -0.5
                    wait_filled(dve, ("S", u))
                    nc.vector.tensor_tensor_reduce(t[:, 0:n], bank(("S", u))[:, 0:n], mask, -scale,
                                                   nsink[:, h:h + 1] if g == "C" else BIG, ALU.add, ALU.min,
                                                   nmax[:, u:u + 1]).then_inc(dve_drained, 1)

                dve.wait_ge(nsink_ready, 1)
                dve.wait_ge(topk_done, TT - 1)
                for u in range(3):
                    scores(u)
                for u in range(len(UNITS)):
                    if u % 2 == 0:
                        n = keys(*UNITS[u][:2])[1]
                        wait_filled(dve, ("T", u))
                        nc.vector.tensor_copy(pring[:, u % 3, 0:n], bank(("T", u))[:, 0:n]).then_inc(dve_drained, 1)
                    if u + 3 < len(UNITS):
                        scores(u + 3)
                    if u % HEADS == 0 and u > 0 or u == last_unit:
                        for og in ([u // HEADS - 1] if u < last_unit else [u // HEADS]):
                            g, i, _ = UNITS[og * HEADS]
                            at = GROUPS.index(g) * HEADS * HD
                            dve.wait_ge(o_filled, og + 1)
                            link(nc.vector.reciprocal(rsd, sums[:, og * HEADS:(og + 1) * HEADS]))
                            nc.vector.tensor_tensor(
                                tok[:, i, at:at + 256].rearrange("p (h d) -> p h d", h=HEADS),
                                banks[6 + og % 2][:, 0:256].rearrange("p (h d) -> p h d", h=HEADS),
                                rsd.unsqueeze(2).to_broadcast([P, HEADS, HD]), ALU.mult).then_inc(o_drained, 1)
                for k in range(0, KT, 2):
                    wait_filled(dve, ("mT", k))
                    nc.vector.tensor_copy(hT[:, k, :], bank(("mT", k))[:, :]).then_inc(dve_drained, 1)

                def diagonals(n, v):
                    for k in range(KT):
                        last = nc.vector.tensor_scalar(diags[n][:, k * P:(k + 1) * P], ident[:, :], v[:, k:k + 1],
                                                       None, ALU.mult)
                    last.then_inc(diag_ready, 1)

                diagonals(0, modT[:, 16:24])
                diagonals(1, scaleT[:, 8:16])
                diagonals(2, modT[:, 24:32])
                for n in range(2 * TT):
                    name = ("out", n // 2, n % 2)
                    wait_filled(dve, name)
                    wait_drained(dve, ("gt1", 1))
                    if n >= 4:
                        dve.wait_ge(x_added, n - 3)
                    nc.vector.tensor_tensor(tring[:, n % 4, :], bank(name)[:, :], gtB[:, (n % 2) * 512:(n % 2 + 1) * 512],
                                            ALU.mult).then_inc(dve_drained, 1)
                dve.wait_ge(root_ready, 2)
                wait_drained(dve, ("sc2", 1))
                link(nc.vector.reciprocal(rstd, rstd))
                for i in range(TT):
                    nc.vector.scalar_tensor_tensor(out=tok[:, i, :], in0=x[:, i, :], scalar=rstd[:, i:i + 1], in1=sc2B,
                                                   op0=ALU.mult, op1=ALU.mult).then_inc(rows2_scaled, 1)
                wait_filled(dve, ("sh2", 1))
                diagonals(3, modT[:, 40:48])
                for k in range(0, KT, 2):
                    wait_filled(dve, ("h2", k))
                    nc.vector.tensor_copy(hT[:, k, :], bank(("h2", k))[:, :]).then_inc(dve_drained, 1)
                r = [rout[:, n, :] for n in range(8)]
                quads = lambda a: a.rearrange("p (g e) -> p g e", e=4)
                wait_drained(dve, "router")
                link(nc.vector.tensor_tensor(r[1].rearrange("p (i e) -> p i e", e=NE), r[0].rearrange("p (i e) -> p i e", e=NE),
                                             brt.unsqueeze(1).to_broadcast([P, TT, NE]), ALU.add))
                rank(quads(r[2]), quads(r[1]), quads(r[3]))
                link(nc.vector.tensor_scalar(r[4], r[2], 2.0, None, ALU.is_lt))
                link(nc.vector.tensor_tensor(r[3], r[1], r[4], ALU.mult))
                link(nc.vector.tensor_reduce(r[4][:, 0:16], quads(r[3]), AX.X, ALU.add))
                rank(quads(r[5][:, 0:16]), quads(r[4][:, 0:16]), quads(r[6][:, 0:16]))
                link(nc.vector.tensor_scalar(r[5][:, 0:16], r[5][:, 0:16], 1.0, None, ALU.is_lt))
                best = r[5][:, 0:16].unsqueeze(2).to_broadcast([P, 16, 4])
                for c in range(2):
                    link(nc.vector.tensor_scalar(mk[:, c, :], r[2], float(c), None, ALU.is_equal))
                    link(nc.vector.tensor_tensor(quads(mk[:, c, :]), quads(mk[:, c, :]), best, ALU.mult))
                nc.vector.tensor_tensor(r[7], mk[:, 0, :], mk[:, 1, :], ALU.add).then_inc(chosen, 1)

                def of_choice(dst, src):
                    for c in range(2):
                        link(nc.vector.tensor_tensor(prod[:, c, :], mk[:, c, :], src, ALU.mult))
                    link(nc.vector.tensor_reduce(dst, prod.rearrange("p c (i e) -> p (c i) e", e=NE), AX.X, ALU.add))

                gates, den = tiny[:, 0:8], tiny[:, 8:12]
                of_choice(gates, r[0])
                link(nc.vector.tensor_tensor(den, gates[:, 0:TT], gates[:, TT:2 * TT], ALU.add))
                link(nc.vector.reciprocal(den, den))
                link(nc.vector.tensor_tensor(gates[:, 0:TT], gates[:, 0:TT], den, ALU.mult))
                nc.vector.tensor_tensor(gates[:, TT:2 * TT], gates[:, TT:2 * TT], den, ALU.mult).then_inc(gates_ready, 1)
                wait_filled(dve, "pos")
                nc.vector.tensor_copy(posb, bank("pos")[:, 0:80]).then_inc(dve_drained, 1)
                wait_drained(dve, "pos")
                pos, cnt = posb[:, 0:64], posb[:, 64:80]
                more, upto, first = tiny[:, 16:32], tiny[:, 32:48], tiny[:, 48:64]
                link(nc.vector.tensor_scalar(more, cnt, float(P), None, ALU.is_gt))
                for n in (2, 3):
                    link(nc.vector.scalar_tensor_tensor(out=more, in0=cnt, scalar=float(n * P), in1=more,
                                                        op0=ALU.is_gt, op1=ALU.add))
                link(nc.vector.tensor_tensor_scan(upto, ones[:, 0:NE], more, 0.0, ALU.mult, ALU.add))
                link(nc.vector.scalar_tensor_tensor(out=first, in0=upto, scalar=float(NE - 1), in1=more,
                                                    op0=ALU.add, op1=ALU.subtract))
                link(nc.vector.tensor_tensor(first, first, iota[:, 0:NE], ALU.subtract))
                four = lambda a: a.rearrange("p (i e) -> p i e", e=NE)
                over = lambda a: a.unsqueeze(1).to_broadcast([P, TT, NE])
                link(nc.vector.tensor_scalar(rowf, pos, float(P), None, ALU.is_ge))
                link(nc.vector.tensor_tensor(four(rowf), four(rowf), over(first), ALU.mult))
                link(nc.vector.tensor_tensor(four(rowf), four(rowf), over(iota[:, 0:NE]), ALU.add))
                link(nc.vector.scalar_tensor_tensor(out=rowf, in0=rowf, scalar=float(P), in1=pos, op0=ALU.mult, op1=ALU.add))
                rows = tiny[:, 64:72]
                of_choice(rows, rowf)
                link(nc.vector.tensor_copy(row_of, rows))
                link(nc.vector.tensor_scalar(tile_i, row_of, 7, None, ALU.logical_shift_right))
                link(nc.vector.tensor_scalar(slot_i, row_of, P - 1, None, ALU.bitwise_and))
                link(nc.vector.tensor_copy(tiny[:, 72:88], ints[:, 8:24]))
                for n in range(8):
                    nc.vector.tensor_scalar(in_slot[:, n, :], iota, tiny[:, 80 + n:81 + n], None, ALU.is_equal)
                    last = nc.vector.tensor_scalar(in_tile[:, n, :], iota[:, 0:MAX_TILES], tiny[:, 72 + n:73 + n],
                                                   token[:, n % TT:n % TT + 1], ALU.is_equal, ALU.mult)
                last.then_inc(onehots_ready, 1)
                full = [P, OTHERS, NE]
                ends = rout[:, 1:3, :].rearrange("p a n -> p (a n)").rearrange("p (k e) -> p k e", e=NE)
                link(nc.vector.tensor_tensor(ends, upto.unsqueeze(1).to_broadcast(full),
                                             iota[:, 0:OTHERS].unsqueeze(2).to_broadcast(full), ALU.is_le))
                link(nc.vector.tensor_reduce(tiny[:, 88:88 + OTHERS], ends, AX.X, ALU.add))
                link(nc.vector.tensor_scalar(tiny[:, 88:88 + OTHERS], tiny[:, 88:88 + OTHERS], float(NE - 1), None, ALU.min))
                nc.vector.tensor_copy(expert_of[:, 0:NE], iota[:, 0:NE])
                nc.vector.tensor_copy(expert_of[:, NE:MAX_TILES], tiny[:, 88:88 + OTHERS])
                np_f = tiny[:, 96:97]
                link(nc.vector.tensor_scalar(np_f, upto[:, NE - 1:NE], 1.0, float(NE // 2), ALU.is_ge, ALU.add))
                for n in (3, 5, 7):
                    link(nc.vector.scalar_tensor_tensor(out=np_f, in0=upto[:, NE - 1:NE], scalar=float(n), in1=np_f,
                                                        op0=ALU.is_ge, op1=ALU.add))
                nc.vector.tensor_copy(pairs_i, np_f).then_inc(routed, 1)
                wait_filled(dve, "inv")
                nc.vector.tensor_copy(token_of, bank("inv")[:, 0:MAX_TILES]).then_inc(dve_drained, 1)
                pairs = pairs_of(dve)
                with dve.Fori(0, pairs) as pair:
                    for s in range(2):
                        dve.wait_ge(xt_filled, pair * 4 + (2 * s + 2))
                        nc.vector.tensor_copy(xgT[s][:, 512:1024], banks[1][:, :]).then_inc(xt_dve, 1)
                    for s in range(2):
                        dve.wait_ge(silu_ready, pair * 2 + (s + 1))
                        nc.vector.tensor_tensor(hid[s], banks[2 + s][:, 256:512], sg[s], ALU.mult).then_inc(hidden_ready, 1)
                    for s in range(2):
                        dve.wait_ge(down_filled, pair * 4 + (2 * s + 2))
                        dve.wait_ge(y_stored[s], pair * 16 + 16)
                        nc.vector.tensor_copy(ysb[s][:, 512:1024], banks[5 + 2 * s][:, :]).then_inc(y_dve, 1)
                dve.wait_ge(gates_ready, 1)
                wait_drained(dve, ("gt2", 1))
                for i in range(TT):
                    dve.wait_ge(choice_landed[i], 32)
                    y0, y1 = tok[:, i, :], hT[:, 2 * i:2 * i + 2, :].rearrange("p a n -> p (a n)")
                    link(nc.vector.tensor_scalar(y0, y0, gates[:, i:i + 1], None, ALU.mult))
                    nc.vector.scalar_tensor_tensor(out=y0, in0=y1, scalar=gates[:, TT + i:TT + i + 1], in1=y0,
                                                   op0=ALU.mult, op1=ALU.add).then_inc(combined, 1)
                    dve.wait_ge(combined, i + 1)
                    nc.vector.tensor_tensor(y0, y0, gtB[:, :], ALU.mult).then_inc(gated_ready, 1)
                dve.wait_ge(gated_ready, TT)
                dve.sem_inc(layer_end, 1)
                dve.wait_ge(layer_go, l + 1)
            totals[dve_step] = step[0]
            dve.wait_ge(fin_root, 1)
            dve.wait_ge(consts_landed, (CONSTS + 1) * 16)
            nc.vector.reciprocal(rstd, rstd).then_inc(fin_rstd, 1)
            dve.wait_ge(fin_rstd, 1)
            for i in range(TT):
                nc.vector.scalar_tensor_tensor(out=tok[:, i, :], in0=x[:, i, :], scalar=rstd[:, i:i + 1], in1=gtB[:, :],
                                               op0=ALU.mult, op1=ALU.mult).then_inc(fin_rows, 1)

        @block.tensor
        def _(pe):
            def mm(dst, lhsT, rhs, first=True, last=True):
                return nc.tensor.matmul(dst, lhsT, rhs, start=first, stop=last)

            def features(name, rows, w, rhs, kt):
                wait_bank(pe, name)
                for k in range(kt):
                    last = mm(bank(name)[0:rows, :], w(k), rhs[:, k, :], k == 0, k == kt - 1)
                last.then_inc(psum_filled, 1)

            def project(name, n, at, rows):
                features(name, rows, lambda k: slot(n, CHUNKS[n][1])[:, k, at:at + rows], hT, KT)

            def turn(name, parts):
                wait_bank(pe, name)
                for dst, src, size in parts:
                    last = nc.tensor.transpose(dst, src, ident[0:size, 0:size])
                last.then_inc(psum_filled, 1)

            def turn_rows(name, k):
                turn(name, [(bank(name)[:, i * P:(i + 1) * P], tok[:, i, k * P:(k + 1) * P], P) for i in range(TT)])

            pe.wait_ge(consts_landed, CONSTS * 16)
            pe.wait_ge(consts_set, 3)
            with pe.Fori(0, DEPTH) as l:
                for n in range(MOD_CHUNKS):
                    pe.wait_ge(ada_used, n + 1)
                    for j in range(4):
                        at = n * 4 + j
                        last = mm(bank("mod")[:, at:at + 1], ada_acc[n % 2][:, j * P:(j + 1) * P], ones[:, 0:1])
                    last.then_inc(ada_summed if n < MOD_CHUNKS - 1 else psum_filled, 1)
                pe.wait_ge(xhat_ready, TT)
                for k in range(KT):
                    turn_rows(("h1", k), k)
                wait_drained(pe, ("h1", KT - 1))
                wait_drained(pe, ("h1", KT - 2))
                pe.wait_ge(win_landed[0], 16)
                for m in range(2):
                    project(("qD", m), 0, m * P, P)
                project("kvD", 0, 256, P)
                pe.wait_ge(win_landed[1], 16)
                for m in range(2):
                    project(("qi", m), 1, m * P, P)
                project("kiwi", 1, 256, 40)
                wait_drained(pe, "kvD")
                turn("vDT", [(bank("vDT")[:, i * 64:(i + 1) * 64], vdT[0:64, i * P:(i + 1) * P], 64) for i in range(TT)])
                wait_drained(pe, "kiwi")
                turn("wiT", [(bank("wiT")[:, i * 8:(i + 1) * 8], kiwiT[0:8, i * P:(i + 1) * P], 8) for i in range(TT)])
                for i in range(1, TT):
                    for h in range(IDX_HEADS):
                        name, r = ("idx", i, h), slice(32 * (h % 4), 32 * (h % 4) + 32)
                        wait_bank(pe, name)
                        mm(bank(name)[:, 0:P * (i + 1)], qi[r, h // 4, i * P:(i + 1) * P], ki[r, 0:P * (i + 1)])\
                            .then_inc(psum_filled, 1)
                pe.wait_ge(win_landed[2], 16)
                for m in range(2):
                    project(("cq", m), 2, m * P, P)
                project("ckv", 2, 256, P)
                pe.wait_ge(small_landed, SMALLS * 16)
                features("kr", 2 * ROPE, lambda k: wkr[:, k, :], hT, KT)
                pe.wait_ge(win_landed[3], 16)
                for m in range(2):
                    project(("qA", m), 3, m * P, P)
                project(("kA", 0), 3, 256, P)
                pe.wait_ge(win_landed[4], 16)
                project(("kA", 1), 4, 0, P)
                for i in range(TT):
                    wait_bank(pe, ("vA", i))
                    for k in range(KT):
                        last = mm(bank(("vA", i))[:, 0:260], hT[:, k, i * P:(i + 1) * P], slot(4, 388)[:, k, 128:388],
                                  k == 0, k == KT - 1)
                    last.then_inc(psum_filled, 1)
                wait_drained(pe, ("vA", TT - 1))
                turn("afT", [(bank("afT")[0:4, i * P:(i + 1) * P], vA[:, i, 256:260], P) for i in range(TT)])
                pe.wait_ge(cq_squared, 3)
                wait_bank(pe, "ssq")
                for m in range(2):
                    last = mm(bank("ssq")[:, :], ones[:, :], sqT[:, m, :], m == 0, m == 1)
                last.then_inc(psum_filled, 1)
                wait_bank(pe, "ssk")
                mm(bank("ssk")[:, :], ones[:, :], sqT[:, 2, :]).then_inc(psum_filled, 1)
                pe.wait_ge(win_landed[5], 16)
                for m in range(2):
                    project(("qC", m), 5, m * P, P)
                project("kC", 5, 256, P)
                pe.wait_ge(win_landed[6], 16)
                wait_bank(pe, "vC")
                for i in range(TT):
                    for k in range(KT):
                        last = mm(bank("vC")[:, i * P:(i + 1) * P], hT[:, k, i * P:(i + 1) * P], slot(6, 128)[:, k, :],
                                  k == 0, k == KT - 1)
                last.then_inc(psum_filled, 1)
                pe.wait_ge(latents_ready, 1)
                pe.wait_ge(small_landed, SMALLS * 16)
                for m in range(2):
                    features(("qBn", m), P, lambda k: wq_n[:, k, m * P:(m + 1) * P], cqT, 2)
                features("qBr", P, lambda k: wq_r[:, k, :], cqT, 2)
                features("qBs", P, lambda k: wq_s[:, k, :], cqT, 2)
                for m in range(2):
                    wait_bank(pe, ("kBn", m))
                    mm(bank(("kBn", m))[:, :], wk_n[:, m * P:(m + 1) * P], ckvT).then_inc(psum_filled, 1)
                for m in range(2):
                    wait_bank(pe, ("vB", m))
                    for j in range(2):
                        i = 2 * m + j
                        last = mm(bank(("vB", m))[:, j * 256:(j + 1) * 256], ckvT[:, i * P:(i + 1) * P], wk_v[:, :])
                    last.then_inc(psum_filled, 1)

                Q = {"A": qA, "B": qB, "C": qC, "D": qD}
                K = {"A": lambda h: kA[:, h, :], "B": lambda h: kB[:, h, :], "C": lambda h: kC[:, h // 2, :],
                     "D": lambda h: kD[:, :]}
                V = {"A": lambda h, t: vA[:, t, h * HD:(h + 1) * HD], "B": lambda h, t: vB[:, t, h * HD:(h + 1) * HD],
                     "C": lambda h, t: vC[:, t, (h // 2) * HD:(h // 2 + 1) * HD], "D": lambda h, t: vD[:, t, :]}

                def unit_scores(u):
                    g, i, h = UNITS[u]
                    k0, n = keys(g, i)
                    rows = NOPE + ROPE if g == "B" else HD + 2
                    wait_bank(pe, ("S", u))
                    mm(bank(("S", u))[:, 0:n], Q[g][0:rows, h, i * P:(i + 1) * P], K[g](h)[0:rows, k0:k0 + n])\
                        .then_inc(psum_filled, 1)

                def unit_turn(u):
                    g, i, _ = UNITS[u]
                    pe.wait_ge(probs_ready, u + 1)
                    b = bank(("T", u))
                    turn(("T", u), [(b[:, t * P:(t + 1) * P], tring[:, u % 4, t * P:(t + 1) * P], P)
                                    for t in range(keys(g, i)[1] // P)])

                def unit_values(u):
                    g, i, h = UNITS[u]
                    k0, n = keys(g, i)
                    og = u // HEADS
                    if h == 0 and og >= 2:
                        pe.wait_ge(o_drained, og - 1)
                    wait_drained(pe, ("T", u))
                    for t in range(n // P):
                        last = mm(banks[6 + og % 2][:, h * HD:(h + 1) * HD], pring[:, u % 3, t * P:(t + 1) * P],
                                  V[g](h, k0 // P + t), t == 0, t == n // P - 1)
                    if h == HEADS - 1:
                        last.then_inc(o_filled, 1)

                pe.wait_ge(forget_landed, 8 * 16)
                pe.wait_ge(qrope_ready, 1)
                wait_drained(pe, ("vB", 1))
                for u in range(3):
                    unit_scores(u)
                for u in range(len(UNITS)):
                    unit_turn(u)
                    if u + 3 < len(UNITS):
                        unit_scores(u + 3)
                    if u > 0:
                        unit_values(u - 1)
                unit_values(last_unit)
                pe.wait_ge(o_drained, len(UNITS) // HEADS)
                for k in range(KT):
                    turn_rows(("mT", k), k)

                def spread(name, n):
                    pe.wait_ge(diag_ready, n + 1)
                    for m in range(2):
                        wait_bank(pe, (name, m))
                        mm(bank((name, m))[:, :], ones[:, :], diags[n][:, m * 512:(m + 1) * 512]).then_inc(psum_filled, 1)

                spread("gt1", 0)
                spread("sc2", 1)
                spread("sh2", 2)
                wait_drained(pe, ("mT", KT - 1))
                wait_drained(pe, ("mT", KT - 2))
                pe.wait_ge(wout_landed, 16)
                for i in range(TT):
                    for m in range(2):
                        name = ("out", i, m)
                        wait_bank(pe, name)
                        for k in range(KT):
                            last = mm(bank(name)[:, :], hT[:, k, i * P:(i + 1) * P], wo[:, k, m * 512:(m + 1) * 512],
                                      k == 0, k == KT - 1)
                        last.then_inc(psum_filled, 1)
                pe.wait_ge(rows2_ready, TT)
                for k in range(KT):
                    turn_rows(("h2", k), k)
                spread("gt2", 3)
                wait_drained(pe, ("h2", KT - 1))
                wait_drained(pe, ("h2", KT - 2))
                wait_bank(pe, "router")
                for i in range(TT):
                    for k in range(KT):
                        last = mm(bank("router")[:, i * NE:(i + 1) * NE], hT[:, k, i * P:(i + 1) * P], wr[:, k, :],
                                  k == 0, k == KT - 1)
                last.then_inc(psum_filled, 1)
                pe.wait_ge(chosen, 1)
                wait_bank(pe, "pos")
                sel = rout[:, 7, :]
                for i in range(TT):
                    for j in range(i + 1):
                        mm(bank("pos")[:, i * NE:(i + 1) * NE], ones[:, :] if j < i else before,
                           sel[:, j * NE:(j + 1) * NE], j == 0, j == i)
                for j in range(TT):
                    last = mm(bank("pos")[:, 64:80], ones[:, :], sel[:, j * NE:(j + 1) * NE], j == 0, j == TT - 1)
                last.then_inc(psum_filled, 1)
                pe.wait_ge(onehots_ready, 1)
                wait_bank(pe, "inv")
                for n in range(8):
                    last = mm(bank("inv")[:, 0:MAX_TILES], in_slot[:, n, :], in_tile[:, n, :], n == 0, n == 7)
                last.then_inc(psum_filled, 1)
                pe.wait_ge(act_drained, count["act"])
                pe.wait_ge(dve_drained, count["dve"])
                pairs = pairs_of(pe)
                with pe.Fori(0, pairs) as pair:
                    for s in range(2):
                        t = pair * 2 + s
                        pe.wait_ge(xg_landed[s], pair * 16 + 16)
                        for half, taken in ((0, xt_act), (1, xt_dve)):
                            pe.wait_ge(taken, t + 2)
                            for k in range(4):
                                last = nc.tensor.transpose(banks[half][:, k * P:(k + 1) * P],
                                                           xg[s][:, (4 * half + k) * P:(4 * half + k + 1) * P], ident[:, :])
                            last.then_inc(xt_filled, 1)
                    for s in range(2):
                        t = pair * 2 + s
                        g, u, d = expert(s)
                        pe.wait_ge(xt_act, t + 3)
                        pe.wait_ge(xt_dve, t + 3)
                        pe.wait_ge(gu_landed[s], pair * 32 + 32)
                        for n in range(4):
                            w = (g, u)[n // 2]
                            for k in range(KT):
                                last = mm(banks[2 + s][:, n * P:(n + 1) * P], w[:, k, (n % 2) * P:(n % 2 + 1) * P],
                                          xgT[s][:, k * P:(k + 1) * P], k == 0, k == KT - 1)
                        last.then_inc(gu_filled, 1)
                    for s in range(2):
                        t = pair * 2 + s
                        g, u, d = expert(s)
                        pe.wait_ge(hidden_ready, t + 1)
                        pe.wait_ge(d_landed[s], pair * 16 + 16)
                        for m, taken in ((0, y_act), (1, y_dve)):
                            pe.wait_ge(taken, t + 1)
                            for f in range(2):
                                last = mm(banks[4 + 2 * s + m][:, :], hid[s][:, f * P:(f + 1) * P],
                                          d[:, f, m * 512:(m + 1) * 512], f == 0, f == 1)
                            last.then_inc(down_filled, 1)
                pe.sem_inc(layer_end, 1)
                pe.wait_ge(layer_go, l + 1)

        @block.sync
        def _(sp):
            for dst, src in [(x[:, :, :], x_in.rearrange("b (i p) d -> p (b i) d", p=P)),
                             (ident[:, :], k_ident), (route[:, :], k_route), (causal[:, :], k_causal), (window[:, :], k_window),
                             (qC[64:66, :, :], k_rows[:, 0:4, :]), (kC[64:66, :, :], k_rows[:, 4:6, :]),
                             (qD[64:66, :, :], k_rows[:, 6:10, :]), (kD[64:66, :], k_rows[:, 10, :]),
                             (qA[65:66, :, :], k_rows[0:1, 11:15, :]), (kA[64:65, :, :], k_rows[0:1, 15:19, :]),
                             (wr[:, :, :], w_router.rearrange("(k p) e -> p k e", p=P)),
                             (brt, b_router.rearrange("(a e) -> a e", a=1).partition_broadcast(P)),
                             (cT, c_in.rearrange("b (k p) -> p (b k)", p=P))]:
                sp.dma_start(dst, src, allow_slow_non_contiguous=True).then_inc(consts_landed, 16)

            with sp.Fori(0, DEPTH) as l:
                def layer(t):
                    return t[bass.ds(l, 1)]

                def flat(t, pattern, **kw):
                    return layer(t).rearrange(pattern, **kw)

                for dst, src in [(vecT[:, 0:8], flat(g_norm1, "a (k p) -> p (a k)", p=P)),
                                 (vecT[:, 8:16], flat(g_norm2, "a (k p) -> p (a k)", p=P)),
                                 (vecT[:, 16:18], flat(g_q_mla, "a (k p) -> p (a k)", p=P)),
                                 (vecT[:, 18:19], flat(g_kv_mla, "a (k p) -> p (a k)", p=P)),
                                 (bfg[0:4, :], flat(b_forget, "a h -> h a")),
                                 (sinkb, layer(sinks).partition_broadcast(P))]:
                    sp.dma_start(dst, src, allow_slow_non_contiguous=True).then_inc(small_landed, 16)
                wq = flat(w_q_up, "a (k p) (h e) -> p (a k) h e", p=P, h=HEADS)
                for k in range(2):
                    sp.dma_start(wq_n[:, k, :].rearrange("p (h e) -> p h e", h=HEADS),
                                 wq[:, k, :, 0:NOPE]).then_inc(small_landed, 16)
                    sp.dma_start(wq_r[:, k, :].rearrange("p (h e) -> p h e", h=HEADS),
                                 wq[:, k, :, NOPE:]).then_inc(small_landed, 16)
                    for a in range(2):
                        sp.dma_start(wq_s[:, k, :].rearrange("p (h b e) -> p h b e", h=HEADS, b=2)[:, :, a, :],
                                     wq[:, k, :, NOPE + 16 * (1 - a):NOPE + 16 * (2 - a)],
                                     allow_slow_non_contiguous=True).then_inc(small_landed, 16)
                wkv = flat(w_kv_up, "a p (h b e) -> p (a h) b e", h=HEADS, b=2)
                sp.dma_start(wk_n[:, :].rearrange("p (h e) -> p h e", h=HEADS), wkv[:, :, 0, :]).then_inc(small_landed, 16)
                sp.dma_start(wk_v[:, :].rearrange("p (h e) -> p h e", h=HEADS), wkv[:, :, 1, :]).then_inc(small_landed, 16)

                wi_d = flat(w_in, "a (k p) n -> p (a k) n", p=P)
                for at, frm, n in ((0, 0, ROPE), (ROPE, ROPE // 2, ROPE // 2), (ROPE * 3 // 2, 0, ROPE // 2)):
                    sp.dma_start(wkr[:, :, at:at + n], wi_d[:, :, OFF["bkr"] + frm:OFF["bkr"] + frm + n],
                                 allow_slow_non_contiguous=True).then_inc(small_landed, 16)

                sp.wait_ge(bias_zeroed, 1)
                wa = flat(w_ada, "a (k p) n -> p (a k) n", p=P)
                for n in range(MOD_CHUNKS):
                    if n >= 3:
                        sp.wait_ge(ada_used, n - 2)
                    sp.dma_start(ada_slot(n), wa[:, :, n * 512:(n + 1) * 512]).then_inc(ada_landed[n % 3], 16)
                    if n >= 2:
                        sp.wait_ge(ada_used, n - 1)
                    sp.dma_start(ada_bias[n % 2][0:1, :], layer(b_ada)[:, n * 512:(n + 1) * 512])\
                        .then_inc(bada_landed[n % 2], 16)
                sp.wait_ge(ada_used, MOD_CHUNKS)

                for n, (_, cols) in enumerate(CHUNKS):
                    if n >= SLOTS:
                        wait_filled(sp, chunk_last_job[n - SLOTS])
                    sp.dma_start(slot(n, cols), wi_d[:, :, CHUNK_AT[n]:CHUNK_AT[n] + cols]).then_inc(win_landed[n], 16)
                sp.wait_ge(relu_used, 3 * IDX_HEADS)
                sp.dma_start(cosT, k_cos).then_inc(rope_landed, 16)
                sp.dma_start(sinT, k_sin).then_inc(rope_landed, 16)
                sp.wait_ge(forget_ready, 2)
                for h in range(HEADS):
                    sp.dma_start(qA[64:65, h, :], fg[0][h:h + 1, :]).then_inc(forget_landed, 16)
                    sp.dma_start(kA[65:66, h, :], fg[1][h:h + 1, :]).then_inc(forget_landed, 16)
                wait_filled(sp, "vC")
                sp.dma_start(wo, flat(w_out, "a (k p) n -> p (a k) n", p=P)).then_inc(wout_landed, 16)

                for n in range(OTHERS):
                    sp.dma_start(y_rows[(NE + n) * P:(NE + n + 1) * P, :], k_zero).then_inc(y_cleared, 16)
                wait_filled(sp, ("out", TT - 1, 1))

                def load_gu(e, s):
                    for dst, w in zip(expert(s), (w_gate, w_up)):
                        sp.dma_start(dst, w[bass.ds(l, 1), bass.ds(e, 1)].rearrange("a e (k p) f -> p (a e k) f", p=P))\
                            .then_inc(gu_landed[s], 16)

                def load_d(e, s):
                    sp.dma_start(expert(s)[2], w_down[bass.ds(l, 1), bass.ds(e, 1)]
                                 .rearrange("a e (k p) f -> p (a e k) f", p=P)).then_inc(d_landed[s], 16)

                for s in range(2):
                    load_gu(s, s)
                    load_d(s, s)
                for i in range(TT):
                    sp.wait_ge(rows2_ready, i + 1)
                    sp.dma_start(h2_rows[i * P:(i + 1) * P, :], tok[:, i, :]).then_inc(h2_stored, 16)
                pairs = pairs_of(sp)
                sp.wait_ge(y_cleared, 16 * OTHERS)

                def store(t, s):
                    sp.wait_ge(y_act, t + 3)
                    sp.wait_ge(y_dve, t + 3)
                    sp.sem_inc(sp_passed, 1)
                    sp.dma_start(y_rows[bass.ds(t * P, P), :], ysb[s]).then_inc(y_stored[s], 16)

                with sp.Fori(1, pairs) as pair:
                    experts = [sp.value_load(expert_of[0:1, bass.ds(pair * 2 + s, 1)], min_val=0, max_val=NE - 1)
                               for s in range(2)]
                    for s in range(2):
                        sp.wait_ge(gu_filled, pair * 2 + (s - 1))
                        sp.sem_inc(sp_passed, 1)
                        load_gu(experts[s], s)
                    for s in range(2):
                        sp.wait_ge(down_filled, pair * 4 + (2 * s - 2))
                        sp.sem_inc(sp_passed, 1)
                        load_d(experts[s], s)
                        store(pair * 2 + (s - 2), s)
                for s in range(2):
                    store(pairs * 2 + (s - 2), s)

                sp.wait_ge(layer_end, (l + 1) * 4)
                sp.sem_inc(layer_passed, 1)
                for counter, last in pair_totals(pairs).items():
                    sp.wait_ge(counter, last)
                    sp.sem_inc(sp_passed, 1)
                sp.sem_inc(sp_passed, 1)
                for counter, last in totals.items():
                    sp.wait_ge(counter, last)
                sp.sem_clear(range(first_layer_sem.num, last_layer_sem.num + 1))
                sp.sem_inc(layer_go, 1)
            sp.dma_start(gtB[:, :], g_final.rearrange("(a n) -> a n", a=1).partition_broadcast(P)).then_inc(consts_landed, 16)
            for i in range(TT):
                sp.wait_ge(fin_rows, i + 1)
                sp.dma_start(out.rearrange("b (i p) d -> p (b i) d", p=P)[:, i, :], tok[:, i, :]).then_inc(stored, 16)
            sp.wait_ge(stored, 16 * TT)


_INS = ["x", "c", "w_ada", "b_ada", "g_norm1", "w_in", "b_forget", "g_q_mla", "w_q_up", "g_kv_mla", "w_kv_up",
        "sinks", "w_out", "g_norm2", "w_router", "b_router", "w_gate", "w_up", "w_down", "g_final"]


def kernel(**inputs):
    import concourse.bacc as _bacc
    from concourse.bass_utils import run_bass_kernel_spmd as _run

    nc = _bacc.Bacc("TRN2", target_bir_lowering=False, num_devices=1)
    arrays, args = {}, []
    given = {name: np.ascontiguousarray(inputs[name]) for name in _INS}
    given.update(constants())
    for name, a in given.items():
        arrays[f"in_{name}"] = a
        args.append(nc.dram_tensor(f"in_{name}", a.shape, mybir.dt.from_np(a.dtype), kind="ExternalInput").ap())
    args.append(nc.dram_tensor("out_0", (1, SEQ, D), F32, kind="ExternalOutput").ap())
    trunk(nc, *args)
    r = _run(nc, [arrays], core_ids=[0])
    return r.results[0]["out_0"]
```

```python
import concourse.bass as bass
from concourse import mybir
import numpy as np

F32 = mybir.dt.float32
I32 = mybir.dt.int32
ALU = mybir.AluOpType
ACT = mybir.ActivationFunctionType
AX = mybir.AxisListType

P = 128
SEQ, D, DEPTH = 512, 1024, 2
TT = SEQ // P
KT = D // P
HD = 64
HEADS = 4
NE, NG, FE = 16, 4, 256
EPS = 1e-6
IDX_HEADS, IDX_DIM, TOPK = 8, 32, 128
NOPE, ROPE = 64, 32
QR, KVR = 256, 128
NEG = -1e30
TAKEN = -3e38
BIG = 3e38

SIZES = [256, 256, 256, 4, 256, 128, 32, 256, 128, 128, 256, 64, 64, 256, 32, 8]
NAMES = ["aq", "ak", "av", "af", "bcq", "bckv", "bkr", "cq", "ck", "cv", "dq", "dk", "dv", "dqi", "dki", "dwi"]
OFF = {n: int(sum(SIZES[:i])) for i, n in enumerate(NAMES)}
N_IN = sum(SIZES)
CHUNKS = [("index", 360), ("dq", 384), ("bcq", 384), ("aq", 384), ("ak2", 388), ("cq", 384), ("cv", 128)]
INDEX_PARTS = [(OFF["dqi"], 288), (OFF["bkr"], 32), (OFF["bkr"] + 16, 16), (OFF["bkr"], 16), (OFF["dwi"], 8)]
CHUNK_AT = [None, OFF["dq"], OFF["bcq"], OFF["aq"], OFF["aq"] + 384, OFF["cq"], OFF["cv"]]
SLOTS, SLOT = 2, 8 * 388
ADA = 256
ADA_SLOT = KT * ADA
OWN, NEXT = 4 * D // ADA, 2 * D // ADA
MODS = OWN + NEXT

MAX_TILES = NE + 8
OTHERS = MAX_TILES - NE

GROUPS = "ABCD"
UNITS = [(g, i, h) for g in GROUPS for i in range(TT) for h in range(HEADS)]
WITH_UNITS = 10
STEPS = [(j, k) for j in range(WITH_UNITS, OWN) for k in range(KT)]
STEP_AT = {u: STEPS[len(STEPS) * u // len(UNITS):len(STEPS) * (u + 1) // len(UNITS)] for u in range(len(UNITS))}
MOD_AT = {next(u for u in range(len(UNITS)) if (j, KT - 1) in STEP_AT[u]) + 2: j for j in range(WITH_UNITS, OWN - 1)}


def keys(g, i):
    if g == "C":
        return (0, P) if i == 0 else ((i - 1) * P, 2 * P)
    return 0, P * (i + 1)


def idx_jobs(i, *hosts):
    return [j for n, host in enumerate(hosts) for j in [(("idx", i, 4 * n + h), "act") for h in range(4)] + [(host, "act")]]


def mod_jobs(*chunks):
    return [(("mod", j), "dve") for j in chunks]


def h2_jobs(i):
    return [(("h2", i, 0), "act"), (("h2", i, 1), "dve")]


def plan():
    jobs = [("bias", "act")]
    jobs += [(("h1", k), "act" if k % 2 else "dve") for k in range(KT)]
    jobs += [(("qi", m), "act") for m in range(2)] + [("kiwi", "act")] + mod_jobs(0, 1)
    jobs += [(("qD", 0), "act"), ("wiT", "dve")]
    idx1 = idx_jobs(1, ("qD", 1), "kvD")
    jobs += idx1[:5] + mod_jobs(2, 3) + idx1[5:]
    jobs += [(("cq", 0), "act"), ("vDT", "act"), (("cq", 1), "act"), ("ckv", "act")] + mod_jobs(4, 5)
    idx2, idx3 = idx_jobs(2, ("qA", 0), ("qA", 1)), idx_jobs(3, ("kA", 1), ("qC", 0))
    jobs += idx2
    jobs += [(("kA", 0), "act"), ("ssq", "act"), ("ssk", "act")]
    jobs += idx3[:5] + [(("vA", i), "act") for i in range(TT)] + [("afT", "act")] + idx3[5:] + mod_jobs(6, 7)
    jobs += [(("qC", 1), "act"), ("kC", "act"), ("vC", "act")]
    jobs += [(("qBn", m), "act") for m in range(2)] + [("qBr", "dve"), ("qBs", "dve")]
    jobs += [(("kBn", m), "act") for m in range(2)] + [(("vB", m), "act") for m in range(2)]
    jobs += mod_jobs(8, 9)
    n = len(UNITS)
    jobs += [(("S", u), "dve") for u in range(3)]
    for u in range(n):
        jobs += [(("T", u), "act" if u % 2 else "dve")]
        if u + 3 < n:
            jobs += [(("S", u + 3), "dve")]
        if u in MOD_AT:
            jobs += mod_jobs(MOD_AT[u])
    jobs += [(("mT", k), "act" if k % 2 else "dve") for k in range(KT)]
    jobs += mod_jobs(OWN - 1)
    for i in range(TT):
        jobs += [(("out", i, 0), "dve")]
        if i > 0:
            jobs += mod_jobs(OWN + 2 * i - 1)
        if i > 1:
            jobs += [(("router", i - 2), "act")]
        if i == 0:
            jobs += [(("gt1", m), "act") for m in range(2)]
        jobs += [(("out", i, 1), "dve")]
        if i > 0:
            jobs += h2_jobs(i - 1)
        if i < TT - 1:
            jobs += mod_jobs(OWN + 2 * i)
    jobs += [(("gt2", m), "act") for m in range(2)] + [(("router", TT - 2), "act")]
    jobs += mod_jobs(MODS - 2, MODS - 1) + h2_jobs(TT - 1) + [(("router", TT - 1), "act")]
    jobs += [("pos", "dve"), ("inv", "dve")]
    return jobs


def constants():
    q = np.arange(P)[:, None]
    c = np.arange(SEQ)[None, :]
    causal = np.where(c - (SEQ - P) > q, NEG, 0.0)
    dist = q - np.arange(2 * P)[None, :] + P
    window = np.where((dist >= 0) & (dist < P), 0.0, NEG)
    half = ROPE // 2
    inv = 10000.0 ** (-np.arange(half, dtype=np.float32) / np.float32(half))
    ang = (np.arange(SEQ, dtype=np.float32)[None, :] * inv.astype(np.float32)[:, None]).astype(np.float32)
    cos = np.tile(np.cos(ang), (8, 1))
    sin = np.tile(np.concatenate([-np.sin(ang), np.sin(ang)]), (4, 1))
    pos = np.arange(SEQ, dtype=np.float64)
    slopes = 2.0 ** (-np.arange(1, 9, dtype=np.float64))
    rows = np.zeros((2, 4 + 2 + 4 + 1 + 4 + 4, SEQ))
    for n, s in enumerate(slopes):
        at = n if n < 4 else 6 + n - 4
        rows[0, at] = -8 * s * pos
        rows[1, at] = 8 * s
    for at in (4, 5, 10):
        rows[0, at] = 1
        rows[1, at] = pos
    rows[:, 11:] = 1
    route = np.concatenate([np.broadcast_to(np.arange(P), (P, P)), np.triu(np.ones((P, P)), 1),
                            np.tile(np.arange(TT)[None, :] * P + q + 1, (1, 2)),
                            np.broadcast_to(np.tril(np.ones((4, 4)), -1).reshape(1, 16), (P, 16))], axis=1)
    f = lambda a: np.ascontiguousarray(a, dtype=np.float32)
    return {"k_causal": f(causal), "k_window": f(window), "k_cos": f(cos), "k_sin": f(sin),
            "k_rows": f(rows), "k_ident": f(np.eye(P)), "k_route": f(route), "k_zero": f(np.zeros((P, D)))}


def trunk(nc, x_in, c_in, w_ada, b_ada, g_norm1, w_in, b_forget, g_q_mla, w_q_up, g_kv_mla, w_kv_up, sinks,
          w_out, g_norm2, w_router, b_router, w_gate, w_up, w_down, g_final,
          k_causal, k_window, k_cos, k_sin, k_rows, k_ident, k_route, k_zero, out):

    def sb(name, *shape):
        return nc.alloc_sbuf_tensor(name, [P, *shape], F32)

    x = sb("x", TT, D)
    hT = sb("hT", KT, SEQ)
    wbuf = sb("wbuf", KT * D + 2 * ADA_SLOT)
    tok = sb("tok", TT, D)
    qA, kA = sb("qA", 4, SEQ), sb("kA", 4, SEQ)
    qB, kB = sb("qB", 4, SEQ), sb("kB", 4, SEQ)
    qC, kC = sb("qC", 4, SEQ), sb("kC", 2, SEQ)
    qD, kD = sb("qD", 4, SEQ), sb("kD", SEQ)
    vA, vB, vC, vD = sb("vA", TT, 260), sb("vB", TT, 256), sb("vC", TT, 128), sb("vD", TT, 64)
    qi, ki = sb("qi", 2, SEQ), sb("ki", SEQ)
    tring = sb("tring", 4, SEQ)
    pring = sb("pring", 3, SEQ)
    wq_n, wq_r, wq_s = sb("wq_n", 2, 256), sb("wq_r", 2, 128), sb("wq_s", 2, 128)
    wk_n, wk_v = sb("wk_n", 256), sb("wk_v", 256)
    ident, ones = sb("ident", P), sb("ones", P)
    causal, window = sb("causal", SEQ), sb("window", 2 * P)
    selmask = sb("selmask", 9 * P)
    gtB = sb("gtB", D)
    modT = sb("modT", 48)
    biasT = sb("biasT", 48)
    bada = sb("bada", P)
    ada_acc = sb("ada_acc", 2, ADA)
    vecT = sb("vecT", 20)
    scaleT = sb("scaleT", 16)
    small = sb("small", 256)
    cT = small[:, 0:8]
    cact = small[:, 8:16]
    ss = small[:, 16:20]
    rstd = small[:, 20:24]
    sinkb = small[:, 24:28]
    nsink = small[:, 28:32]
    brt = small[:, 32:48]
    bfg = small[:, 48:49]
    epsc = small[:, 49:50]
    onec = small[:, 50:51]
    rsd = small[:, 52:56]
    max8 = small[:, 56:64]
    wi = small[:, 64:96].rearrange("p (i h) -> p i h", i=TT)
    nbfg = small[:, 96:97]
    nmax = small[:, 128:192]
    sums = small[:, 192:256]
    route = sb("route", 2 * P + 2 * TT + 16)
    iota, before, token1 = route[:, 0:P], route[:, P:2 * P], route[:, 2 * P:2 * P + 2 * TT]
    earlier = route[:, 2 * P + 2 * TT:2 * P + 2 * TT + 16].rearrange("p (a b) -> p a b", b=4)
    ints = nc.alloc_sbuf_tensor("ints", [P, 128], I32)
    row_of = ints[:, 0:8]
    tile_i, slot_i = ints[:, 8:16], ints[:, 16:24]
    token_of = ints[:, 24:24 + MAX_TILES]
    expert_of = ints[:, 48:48 + MAX_TILES]
    pairs_i = ints[:, 72:73]
    gather_idx = [ints[:, 73:74], ints[:, 74:75]]
    next_i = ints[:, 76:76 + DEPTH]
    wr = sb("wr", KT, NE)

    latent = tok[:, :, :].rearrange("p i n -> p (i n)")
    cqT = latent[:, 0:1024].rearrange("p (m n) -> p m n", m=2)
    ckvT = latent[:, 1024:1536]
    krT, krS = latent[:, 1536:2048], latent[:, 3584:4096]
    sqT = latent[:, 2048:3584].rearrange("p (m n) -> p m n", m=3)
    rope1, rope2 = qi[:, 0, :], qi[:, 1, :]
    cosT, sinT = pring[:, 0, :], pring[:, 1, :]
    rq, rk = gtB[:, 0:512], gtB[:, 512:1024]
    first_acc = tring[:, :, :].rearrange("p a n -> p (a n)").rearrange("p (j n) -> p j n", j=NEXT)
    vdT, kiwiT = tring[:, 2, :], tring[:, 3, :]
    score = tring[:, 0, :]
    relu = [pring[:, 0, :], pring[:, 1, :], pring[:, 2, :]]
    fg = [kB[0:4, n, :] for n in range(4)]
    tflat = tring[:, :, :].rearrange("p a n -> p (a n)")
    pflat = pring[:, :, :].rearrange("p a n -> p (a n)")
    diags = [tflat[:, 2 * SEQ:2 * SEQ + D], pflat[:, 0:D]]
    rout = qi[:, 0, :].rearrange("p (n e) -> p n e", e=64)
    mk = qi[:, 1, 0:128].rearrange("p (c n) -> p c n", c=2)
    prod = qi[:, 1, 128:256].rearrange("p (c n) -> p c n", c=2)
    posb, rowf = qi[:, 1, 256:336], qi[:, 1, 336:400]
    tiny = qi[:, 1, 400:512]
    vcf = vC[:, :, :].rearrange("p i n -> p (i n)")
    in_slot = tflat[:, 0:8 * P].rearrange("p (n s) -> p n s", n=8)
    in_tile = vcf[:, 0:8 * MAX_TILES].rearrange("p (n s) -> p n s", n=8)
    xg, ysb = [tok[:, s, :] for s in range(2)], [tok[:, 2 + s, :] for s in range(2)]
    xgT = [hT[:, 2 * s:2 * s + 2, :].rearrange("p a n -> p (a n)") for s in range(2)]
    sg = [tflat[:, D + 256 * s:D + 256 * (s + 1)] for s in range(2)]
    hid = [tflat[:, D + 512 + 256 * s:D + 512 + 256 * (s + 1)] for s in range(2)]
    norm_rows2 = nc.dram_tensor("norm_rows2", [SEQ, D], F32, kind="Internal").ap()
    y_rows = nc.dram_tensor("y_rows", [MAX_TILES * P, D], F32, kind="Internal").ap()

    banks = [nc.alloc_psum_tensor(f"bank{n}", [P, 512], F32) for n in range(8)]

    sem = nc.alloc_semaphore
    consts_landed, consts_set = sem("consts_landed"), sem("consts_set")
    layer_passed = sem("layer_passed")
    layer_end, layer_go, stored = sem("layer_end"), sem("layer_go"), sem("stored")
    padded, rows_landed = sem("padded"), sem("rows_landed")
    c_landed, c_ready, next_ready, first_bias_ready = sem("c_landed"), sem("c_ready"), sem("next_ready"), sem("first_bias_ready")
    first_ada_landed, first_bada_landed = [sem(f"first_ada_landed{n}") for n in range(4)], sem("first_bada_landed")
    first_small_landed = sem("first_small_landed")
    first_used, first_filled, first_turned, first_mod = sem("first_used"), sem("first_filled"), sem("first_turned"), sem("first_mod")
    first_step, first_squares, first_root = sem("first_step"), sem("first_squares"), sem("first_root")
    first_rows, first_scaled = sem("first_rows"), sem("first_scaled")
    fin_rows = sem("fin_rows")
    small_landed, nsink_ready = sem("small_landed"), sem("nsink_ready")
    ada_landed, ada_used = [sem(f"ada_landed{n}") for n in range(2)], sem("ada_used")
    win_landed = [sem(f"win_landed{n}") for n in range(len(CHUNKS))]
    rope_landed, wout_landed = sem("rope_landed"), sem("wout_landed")
    psum_filled, act_drained, dve_drained = sem("psum_filled"), sem("act_drained"), sem("dve_drained")
    dve_step, act_step = sem("dve_step"), sem("act_step")
    squares_ready, root_ready, xhat_ready = sem("squares_ready"), sem("root_ready"), sem("xhat_ready")
    relu_used, topk_done = sem("relu_used"), sem("topk_done")
    cq_squared, latents_ready, krope_ready = sem("cq_squared"), sem("latents_ready"), sem("krope_ready")
    qrope_ready, scales_ready = sem("qrope_ready"), sem("scales_ready")
    forget_ready, forget_landed = sem("forget_ready"), sem("forget_landed")
    softplus_ready = sem("softplus_ready")
    probs_ready = sem("probs_ready")
    o_filled, o_drained = sem("o_filled"), sem("o_drained")
    diag_ready, x_added = sem("diag_ready"), sem("x_added")
    rows2_ready, rows2_stored = sem("rows2_ready"), sem("rows2_stored")
    chosen, gates_ready, onehots_ready, routed = sem("chosen"), sem("gates_ready"), sem("onehots_ready"), sem("routed")
    gu_landed, d_landed = [sem(f"gu_landed{n}") for n in range(2)], [sem(f"d_landed{n}") for n in range(2)]
    idx_ready, y_cleared = sem("idx_ready"), sem("y_cleared")
    xg_landed = [sem(f"xg_landed{n}") for n in range(2)]
    xt_filled, xt_act, xt_dve = sem("xt_filled"), sem("xt_act"), sem("xt_dve")
    gu_filled, silu_ready, hidden_ready = sem("gu_filled"), sem("silu_ready"), sem("hidden_ready")
    down_filled, y_taken = sem("down_filled"), sem("y_taken")
    y_stored = [sem(f"y_stored{n}") for n in range(2)]
    choice_landed = [sem(f"choice_landed{n}") for n in range(TT)]
    sp_passed, pool_passed, dve_passed, pe_passed = [sem(f"{e}_passed") for e in ("sp", "pool", "dve", "pe")]
    last_of_layer = sem("combined")
    combined = last_of_layer
    first_layer_sem, last_layer_sem = small_landed, last_of_layer

    jobs = plan()
    index = {name: n for n, (name, _) in enumerate(jobs)}
    drainer = dict(jobs)
    ordinal, count = {}, {"act": 0, "dve": 0}
    for name, engine in jobs:
        count[engine] += 1
        ordinal[name] = count[engine]
    RING = 6

    def bank(name):
        return banks[index[name] % RING]

    def wait_filled(eng, name):
        eng.wait_ge(psum_filled, index[name] + 1)

    def wait_drained(eng, name):
        eng.wait_ge(act_drained if drainer[name] == "act" else dve_drained, ordinal[name])

    def wait_bank(pe, name):
        if index[name] >= RING:
            wait_drained(pe, jobs[index[name] - RING][0])

    def slot(n, cols):
        at = (n % SLOTS) * SLOT
        return wbuf[:, at:at + KT * cols].rearrange("p (k n) -> p k n", k=KT)

    def ada_slot(j):
        at = KT * D + (j % 2) * ADA_SLOT
        return wbuf[:, at:at + ADA_SLOT].rearrange("p (k n) -> p k n", k=KT)

    def first_slot(j):
        if j % 4 < 2:
            return ada_slot(j % 4)
        return (qB, kB)[j % 4 - 2][:, :, :].rearrange("p h n -> p (h n)").rearrange("p (k n) -> p k n", k=KT)

    def mod_col(j):
        return (2 * D // P + j * (ADA // P)) % 48

    wo = wbuf[:, 0:KT * D].rearrange("p (k n) -> p k n", k=KT)

    def expert(s):
        b = s * 6144
        return (wbuf[:, b:b + 2048].rearrange("p (k f) -> p k f", k=KT),
                wbuf[:, b + 2048:b + 4096].rearrange("p (k f) -> p k f", k=KT),
                wbuf[:, b + 4096:b + 6144].rearrange("p (k n) -> p k n", k=2))

    chunk_last_job = ["kiwi", "kvD", "ckv", ("kA", 0), ("vA", 3), "kC", "vC"]
    last_unit = len(UNITS) - 1

    def pairs_of(eng):
        eng.wait_ge(routed, 1)
        return eng.value_load(pairs_i[0:1, 0:1], min_val=NE // 2, max_val=MAX_TILES // 2)

    CONSTS, SMALLS = 7, 16 + 2 + len(INDEX_PARTS)
    totals = {small_landed: SMALLS * 16, ada_used: MODS, 
              ada_landed[0]: MODS // 2 * 16, ada_landed[1]: MODS // 2 * 16,
              rope_landed: 32, wout_landed: 16,
              psum_filled: len(jobs), act_drained: count["act"], dve_drained: count["dve"],
              squares_ready: 2 * TT, root_ready: 2 * TT, xhat_ready: TT, relu_used: 3 * IDX_HEADS, topk_done: 3,
              cq_squared: 3, latents_ready: 1, krope_ready: 2 + HEADS, qrope_ready: 1, scales_ready: 2, nsink_ready: 1,
              forget_ready: 2, forget_landed: 8 * 16, softplus_ready: 1,
              probs_ready: len(UNITS), o_filled: len(UNITS) // HEADS, o_drained: len(UNITS) // HEADS,
              diag_ready: 2, x_added: 2 * TT, gates_ready: 1, rows2_ready: TT,
              rows2_stored: 16 * TT, y_cleared: 16 * OTHERS, chosen: 1, onehots_ready: 1, routed: 1, combined: 2 * TT}
    for landed in choice_landed:
        totals[landed] = 32

    def pair_totals(pairs):
        return {gu_landed[0]: pairs * 32, gu_landed[1]: pairs * 32, d_landed[0]: pairs * 16, d_landed[1]: pairs * 16,
                idx_ready: pairs * 2, xg_landed[0]: pairs * 16, xg_landed[1]: pairs * 16, xt_filled: pairs * 4,
                xt_act: pairs * 2 + 2, xt_dve: pairs * 2 + 2, gu_filled: pairs * 2, silu_ready: pairs * 2,
                hidden_ready: pairs * 2 + 2, down_filled: pairs * 4 + 4, y_taken: pairs * 4 + 8,
                y_stored[0]: pairs * 16 + 16, y_stored[1]: pairs * 16 + 16}

    for landed in win_landed[1:]:
        totals[landed] = 16

    with nc.Block() as block:

        @block.gpsimd
        def _(pool):
            nc.gpsimd.memset(ones[:, :], 1.0).then_inc(consts_set, 1)
            nc.gpsimd.memset(epsc, EPS).then_inc(consts_set, 1)
            nc.gpsimd.memset(onec, 1.0).then_inc(consts_set, 1)
            pool.wait_ge(consts_set, 3)
            for n, t in enumerate((qC, kC, qD, kD, qA, kA)):
                nc.gpsimd.memset(t[64:128, :, :] if t is not kD else kD[64:128, :], 0.0).then_inc(padded, 1)
                pool.wait_ge(padded, n + 1)
            pool.wait_ge(first_used, NEXT)
            for n, t in enumerate((qB, kB)):
                nc.gpsimd.memset(t[96:128, :, :], 0.0).then_inc(padded, 1)
                pool.wait_ge(padded, n + 7)
            with pool.Fori(0, DEPTH) as l:
                pool.sem_inc(xt_act, 2)
                pool.sem_inc(xt_dve, 2)
                pool.sem_inc(y_taken, 8)
                pool.sem_inc(hidden_ready, 2)
                pool.sem_inc(down_filled, 4)
                pool.sem_inc(y_stored[0], 16)
                pool.sem_inc(y_stored[1], 16)
                for m, name in enumerate([("cq", 0), ("cq", 1), "ckv"]):
                    wait_drained(pool, name)
                    src = cqT[:, m, :] if m < 2 else ckvT
                    nc.gpsimd.tensor_tensor(sqT[:, m, :], src, src, ALU.mult).then_inc(cq_squared, 1)
                wait_drained(pool, "kiwi")
                pool.wait_ge(rope_landed, 32)
                nc.gpsimd.tensor_tensor(krT[0:32, :], krT[0:32, :], cosT[0:32, :], ALU.mult).then_inc(krope_ready, 1)
                nc.gpsimd.tensor_tensor(krS[0:32, :], krS[0:32, :], sinT[0:32, :], ALU.mult).then_inc(krope_ready, 1)
                pool.wait_ge(krope_ready, 2)
                for h in range(HEADS):
                    nc.gpsimd.tensor_tensor(kB[64:96, h, :], krT[0:32, :], krS[0:32, :], ALU.add).then_inc(krope_ready, 1)
                pool.wait_ge(rows2_stored, 16 * TT)
                wait_drained(pool, "inv")
                pairs = pairs_of(pool)
                with pool.Fori(0, pairs) as pair:
                    for s in range(2):
                        t = pair * 2 + s
                        pool.wait_ge(xt_act, t + 1)
                        pool.wait_ge(xt_dve, t + 1)
                        nc.gpsimd.tensor_copy(gather_idx[s], token_of[:, bass.ds(t, 1)]).then_inc(idx_ready, 1)
                        pool.wait_ge(idx_ready, t + 1)
                        pool.sem_inc(pool_passed, 1)
                        pool.indirect_dma_start(xg[s], None, norm_rows2, bass.IndirectOffsetOnAxis(ap=gather_idx[s], axis=0))\
                            .then_inc(xg_landed[s], 16)
                pool.wait_ge(y_cleared, 16 * OTHERS)
                for s in range(2):
                    pool.wait_ge(y_stored[s], pairs * 16 + 16)
                pool.sem_inc(pool_passed, 1)
                for i in range(TT):
                    for c, dst in enumerate((tok[:, i, :], hT[:, 2 * i:2 * i + 2, :].rearrange("p a n -> p (a n)"))):
                        pool.indirect_dma_start(dst, None, y_rows,
                                                bass.IndirectOffsetOnAxis(ap=row_of[:, c * TT + i:c * TT + i + 1], axis=0))\
                            .then_inc(choice_landed[i], 16)
                for s in range(2):
                    pool.wait_ge(xg_landed[s], pairs * 16)
                    pool.sem_inc(pool_passed, 1)
                for landed in choice_landed:
                    pool.wait_ge(landed, 32)
                for first, last in ((xg_landed[0], xg_landed[-1]), (choice_landed[0], choice_landed[-1])):
                    pool.dma_reset(range(first.num, last.num + 1))
                pool.sem_inc(layer_end, 1)
                pool.wait_ge(layer_go, l + 1)

        @block.scalar
        def _(act):
            step = [0]

            def link(ins):
                step[0] += 1
                ins.then_inc(act_step, 1)
                act.wait_ge(act_step, step[0])

            def norm_root(i, squares, roots, n):
                nc.scalar.activation(tok[:, i, :], x[:, i, :], ACT.Square, accum_out=ss[:, i:i + 1]).then_inc(squares, 1)
                act.wait_ge(squares, n)
                nc.scalar.activation(rstd[:, i:i + 1], ss[:, i:i + 1], ACT.Sqrt, bias=epsc, scale=1.0 / D).then_inc(roots, 1)

            def drain(name, *moves):
                wait_filled(act, name)
                for dst, src in moves:
                    last = nc.scalar.activation(dst, src, ACT.Copy)
                last.then_inc(act_drained, 1)

            def drain_pair(name, dst, m):
                b = bank(name)
                drain(name, (dst[0:64, 2 * m, :], b[0:64, :]), (dst[0:64, 2 * m + 1, :], b[64:128, :]))

            act.wait_ge(c_landed, 16)
            nc.scalar.activation(cact, cT, ACT.Silu).then_inc(c_ready, 1)
            act.wait_ge(consts_landed, CONSTS * 16)
            act.wait_ge(consts_set, 3)
            for i in range(TT):
                norm_root(i, first_squares, first_root, i + 1)
            act.wait_ge(first_small_landed, SMALLS * 16)
            act.wait_ge(first_scaled, 1)
            with act.Fori(0, DEPTH) as l:
                drain("bias", (biasT[:, :], bank("bias")[:, 0:48]))
                nc.scalar.activation(nsink, sinkb, ACT.Copy, scale=-1.0).then_inc(nsink_ready, 1)
                link(nc.scalar.activation(nbfg[0:4, :], bfg[0:4, :], ACT.Copy, scale=-1.0))
                for k in range(1, KT, 2):
                    wait_filled(act, ("h1", k))
                    nc.scalar.activation(hT[:, k, :], bank(("h1", k))[:, :], ACT.Identity,
                                         bias=modT[:, k:k + 1], scale=scaleT[:, k:k + 1]).then_inc(act_drained, 1)
                def relus(i, first):
                    for h in range(first, first + 4):
                        n = (i - 1) * IDX_HEADS + h
                        wait_filled(act, ("idx", i, h))
                        if n >= 3:
                            act.wait_ge(relu_used, n - 2)
                        w = P * (i + 1)
                        nc.scalar.activation(relu[n % 3][:, 0:w], bank(("idx", i, h))[:, 0:w], ACT.Relu)\
                            .then_inc(act_drained, 1)

                for m in range(2):
                    drain(("qi", m), (qi[:, m, :], bank(("qi", m))[:, :]))
                b = bank("kiwi")
                drain("kiwi", (kiwiT[0:8, :], b[96:104, :]), *((ki[32 * r:32 * r + 32, :], b[0:32, :]) for r in range(4)),
                      (krT[0:32, :], b[32:64, :]), (krS[0:32, :], b[64:96, :]))
                drain_pair(("qD", 0), qD, 0)
                relus(1, 0)
                drain_pair(("qD", 1), qD, 1)
                relus(1, 4)
                b = bank("kvD")
                drain("kvD", (kD[0:64, :], b[0:64, :]), (vdT[0:64, :], b[64:128, :]))
                drain(("cq", 0), (cqT[:, 0, :], bank(("cq", 0))[:, :]))
                drain("vDT", (vD[:, :, :].rearrange("p i n -> p (i n)"), bank("vDT")[:, 0:256]))
                drain(("cq", 1), (cqT[:, 1, :], bank(("cq", 1))[:, :]))
                drain("ckv", (ckvT, bank("ckv")[:, :]))
                for m in range(2):
                    relus(2, 4 * m)
                    drain_pair(("qA", m), qA, m)
                drain_pair(("kA", 0), kA, 0)
                for name, dst, r in (("ssq", rq, QR), ("ssk", rk, KVR)):
                    wait_filled(act, name)
                    nc.scalar.activation(dst, bank(name)[:, :], ACT.Sqrt, bias=epsc, scale=1.0 / r).then_inc(act_drained, 1)
                relus(3, 0)
                drain_pair(("kA", 1), kA, 1)
                for i in range(TT):
                    drain(("vA", i), (vA[:, i, :], bank(("vA", i))[:, 0:260]))
                wait_filled(act, "afT")
                z = bank("afT")[0:4, :]
                link(nc.scalar.activation(fg[2], z, ACT.Abs, bias=bfg[0:4, :]))
                nc.scalar.activation(fg[3], z, ACT.Relu, bias=nbfg[0:4, :], scale=-1.0).then_inc(act_drained, 1)
                link(nc.scalar.activation(fg[2], fg[2], ACT.Exp, scale=-1.0))
                nc.scalar.activation(fg[2], fg[2], ACT.Ln, bias=onec[0:4, :]).then_inc(softplus_ready, 1)
                relus(3, 4)
                drain_pair(("qC", 0), qC, 0)
                drain_pair(("qC", 1), qC, 1)
                b = bank("kC")
                drain("kC", (kC[0:64, 0, :], b[0:64, :]), (kC[0:64, 1, :], b[64:128, :]))
                drain("vC", (vC[:, :, :].rearrange("p i n -> p (i n)"), bank("vC")[:, :]))
                for m in range(2):
                    drain_pair(("qBn", m), qB, m)
                act.wait_ge(forget_landed, 8 * 16)
                for m in range(2):
                    drain_pair(("kBn", m), kB, m)
                for m in range(2):
                    drain(("vB", m), (vB[:, 2 * m:2 * m + 2, :].rearrange("p i n -> p (i n)"), bank(("vB", m))[:, :]))

                def exps(u):
                    g, i, h = UNITS[u]
                    n = keys(g, i)[1] + (g == "C")
                    t = tring[:, u % 4, 0:n]
                    wait_drained(act, ("S", u))
                    nc.scalar.activation(t, t, ACT.Exp, bias=nmax[:, u:u + 1], scale=-1.0,
                                         accum_out=sums[:, u:u + 1]).then_inc(probs_ready, 1)

                for u in range(3):
                    exps(u)
                for u in range(len(UNITS)):
                    if u % 2:
                        n = keys(*UNITS[u][:2])[1]
                        drain(("T", u), (pring[:, u % 3, 0:n], bank(("T", u))[:, 0:n]))
                    if u + 3 < len(UNITS):
                        exps(u + 3)
                for k in range(1, KT, 2):
                    drain(("mT", k), (hT[:, k, :], bank(("mT", k))[:, :]))
                def spread(name):
                    for m in range(2):
                        drain((name, m), (gtB[:, m * 512:(m + 1) * 512], bank((name, m))[:, :]))

                def modulate2(dst, src, k):
                    return nc.scalar.activation(dst, src, ACT.Identity, bias=modT[:, 24 + k:25 + k],
                                                scale=scaleT[:, 8 + k:9 + k])

                def h2_half(i):
                    wait_filled(act, ("h2", i, 0))
                    for k in range(4):
                        last = modulate2(hT[:, k, i * P:(i + 1) * P], bank(("h2", i, 0))[:, k * P:(k + 1) * P], k)
                    last.then_inc(act_drained, 1)

                act.wait_ge(scales_ready, 1)

                def router(i):
                    wait_filled(act, ("router", i))
                    nc.scalar.activation(rout[:, 0, i * NE:(i + 1) * NE], bank(("router", i))[:, 0:NE], ACT.Sigmoid)\
                        .then_inc(act_drained, 1)

                spread("gt1")
                for i in range(TT):
                    if i > 0:
                        h2_half(i - 1)
                    act.wait_ge(x_added, 2 * i + 2)
                    norm_root(i, squares_ready, root_ready, i + 1)
                    if 0 < i < TT - 1:
                        router(i - 1)
                wait_drained(act, ("out", TT - 1, 1))
                spread("gt2")
                router(TT - 2)
                h2_half(TT - 1)
                router(TT - 1)
                pairs = pairs_of(act)
                with act.Fori(0, pairs) as pair:
                    for s in range(2):
                        act.wait_ge(xt_filled, pair * 4 + (2 * s + 1))
                        for k in range(4):
                            last = modulate2(xgT[s][:, k * P:(k + 1) * P], banks[0][:, k * P:(k + 1) * P], k)
                        last.then_inc(xt_act, 1)
                    for s in range(2):
                        act.wait_ge(gu_filled, pair * 2 + (s + 1))
                        nc.scalar.activation(sg[s], banks[2 + s][:, 0:256], ACT.Silu).then_inc(silu_ready, 1)
                for i in range(TT):
                    act.wait_ge(combined, 2 * i + 2)
                    norm_root(i, squares_ready, root_ready, TT + i + 1)
                act.sem_inc(layer_end, 1)
                act.wait_ge(layer_go, l + 1)
            totals[act_step] = step[0]

        @block.vector
        def _(dve):
            step = [0]

            def link(ins):
                step[0] += 1
                ins.then_inc(dve_step, 1)
                dve.wait_ge(dve_step, step[0])

            def norm_rows(i, roots, n, after, ready):
                dve.wait_ge(roots, n)
                after(nc.vector.reciprocal(rstd[:, i:i + 1], rstd[:, i:i + 1]))
                nc.vector.tensor_scalar(tok[:, i, :], x[:, i, :], rstd[:, i:i + 1], None, ALU.mult).then_inc(ready, 1)

            def first_link(ins):
                first[0] += 1
                ins.then_inc(first_step, 1)
                dve.wait_ge(first_step, first[0])

            def scale1(ready):
                nc.vector.scalar_tensor_tensor(out=scaleT[:, 0:8], in0=modT[:, 8:16], scalar=1.0, in1=vecT[:, 0:8],
                                               op0=ALU.add, op1=ALU.mult).then_inc(ready, 1)

            def ada_step(out, slot, k):
                if k == 0:
                    return nc.vector.tensor_scalar(out, slot[:, 0, :], cact[:, 0:1], None, ALU.mult)
                return nc.vector.scalar_tensor_tensor(out=out, in0=slot[:, k, :], scalar=cact[:, k:k + 1], in1=out,
                                                      op0=ALU.mult, op1=ALU.add)

            def rank(dst, src, tmp, equal):
                full = [P, src.shape[1], 4, 4]
                tmp, equal = (a.rearrange("p (g j) -> p g j", j=16).rearrange("p g (a b) -> p g a b", b=4) for a in (tmp, equal))
                mine, other = src.unsqueeze(3).to_broadcast(full), src.unsqueeze(2).to_broadcast(full)
                nc.vector.tensor_tensor(tmp, other, mine, ALU.is_gt)
                link(nc.vector.tensor_tensor(equal, other, mine, ALU.is_equal))
                link(nc.vector.tensor_tensor(equal, equal, earlier.unsqueeze(1).to_broadcast(full), ALU.mult))
                link(nc.vector.tensor_tensor(tmp, tmp, equal, ALU.add))
                link(nc.vector.tensor_reduce(dst, tmp, AX.X, ALU.add))

            dve.wait_ge(c_ready, 1)
            first, ticks = [0], {}
            for j0 in range(0, NEXT, 2):
                for k in range(KT):
                    for j in (j0, j0 + 1):
                        if k == 0:
                            dve.wait_ge(first_ada_landed[j % 4], 16 * (j // 4 + 1))
                        else:
                            dve.wait_ge(first_step, ticks[j])
                        ins = ada_step(first_acc[:, j, :], first_slot(j), k)
                        if k < KT - 1:
                            first[0] += 1
                            ticks[j] = first[0]
                            ins.then_inc(first_step, 1)
                        else:
                            ins.then_inc(first_used, 1)
                if j0 > 0:
                    norm_rows(j0 // 2 - 1, first_root, j0 // 2, first_link, first_rows)
            norm_rows(TT - 1, first_root, TT, first_link, first_rows)
            dve.wait_ge(consts_landed, CONSTS * 16)
            nc.vector.tensor_scalar(next_i, iota[:, 0:DEPTH], 1.0, float(DEPTH - 1), ALU.add, ALU.min).then_inc(next_ready, 1)
            dve.wait_ge(first_turned, 1)
            nc.vector.tensor_copy(biasT[:, 0:16], banks[7][:, 0:16]).then_inc(first_bias_ready, 1)
            dve.wait_ge(first_bias_ready, 1)
            dve.wait_ge(first_filled, 1)
            nc.vector.tensor_tensor(modT[:, 0:16], banks[6][:, 0:16], biasT[:, 0:16], ALU.add).then_inc(first_mod, 1)
            dve.wait_ge(first_mod, 1)
            dve.wait_ge(first_small_landed, SMALLS * 16)
            scale1(first_scaled)
            dve.wait_ge(first_scaled, 1)
            with dve.Fori(0, DEPTH) as l:
                ticks = {}

                def mod_step(j, k):
                    if k == 0:
                        dve.wait_ge(ada_landed[j % 2], 16 * (j // 2 + 1))
                    else:
                        dve.wait_ge(dve_step, ticks[j])
                    ins = ada_step(ada_acc[:, j % 2, :], ada_slot(j), k)
                    if k < KT - 1:
                        step[0] += 1
                        ticks[j] = step[0]
                        ins.then_inc(dve_step, 1)
                    else:
                        ins.then_inc(ada_used, 1)

                def mod_chunks(*chunks):
                    for k in range(KT):
                        for j in chunks:
                            mod_step(j, k)

                def mod_drain(j):
                    at = mod_col(j)
                    wait_filled(dve, ("mod", j))
                    nc.vector.tensor_tensor(modT[:, at:at + 2], bank(("mod", j))[:, 0:2], biasT[:, 2 * j:2 * j + 2], ALU.add)\
                        .then_inc(dve_drained, 1)

                for k in range(0, KT, 2):
                    wait_filled(dve, ("h1", k))
                    nc.vector.tensor_scalar(hT[:, k, :], bank(("h1", k))[:, :], scaleT[:, k:k + 1], modT[:, k:k + 1],
                                            ALU.mult, ALU.add).then_inc(dve_drained, 1)
                mod_chunks(0, 1)
                wait_drained(dve, "bias")
                mod_drain(0)
                mod_drain(1)
                mod_chunks(2, 3)
                wait_filled(dve, "wiT")
                nc.vector.tensor_scalar(wi, bank("wiT")[:, 0:32].rearrange("p (i h) -> p i h", i=TT),
                                        (IDX_HEADS * IDX_DIM) ** -0.5, None, ALU.mult).then_inc(dve_drained, 1)
                wait_drained(dve, "wiT")

                def index_sums(i, first):
                    sc = score[:, 0:P * (i + 1)]
                    for h in range(first, first + 4):
                        n = (i - 1) * IDX_HEADS + h
                        wait_drained(dve, ("idx", i, h))
                        r = relu[n % 3][:, 0:P * (i + 1)]
                        if h == 0:
                            nc.vector.tensor_scalar(sc, r, wi[:, i, 0:1], None, ALU.mult).then_inc(relu_used, 1)
                        else:
                            nc.vector.scalar_tensor_tensor(out=sc, in0=r, scalar=wi[:, i, h:h + 1], in1=sc,
                                                           op0=ALU.mult, op1=ALU.add).then_inc(relu_used, 1)
                        dve.wait_ge(relu_used, n + 1)

                def top(i):
                    at, w = P * (i * (i + 1) // 2 - 1), P * (i + 1)
                    sc = score[:, 0:w]
                    link(nc.vector.tensor_tensor(sc[:, i * P:w], sc[:, i * P:w], causal[:, SEQ - P:SEQ], ALU.add))
                    for _ in range(TOPK // 8):
                        link(nc.vector.max(max8, sc))
                        link(nc.vector.match_replace(sc, max8, sc, TAKEN))
                    nc.vector.tensor_scalar(selmask[:, at:at + w], sc, TAKEN / 2, NEG, ALU.is_gt, ALU.mult)\
                        .then_inc(topk_done, 1)
                    dve.wait_ge(topk_done, i)

                index_sums(1, 0)
                mod_drain(2)
                mod_drain(3)
                index_sums(1, 4)
                top(1)
                mod_chunks(4, 5)
                mod_drain(4)
                mod_drain(5)
                index_sums(2, 0)
                index_sums(2, 4)
                top(2)
                mod_chunks(6, 7)
                index_sums(3, 0)
                wait_drained(dve, "ssk")
                link(nc.vector.reciprocal(rq, rq))
                link(nc.vector.reciprocal(rk, rk))
                for m in range(2):
                    nc.vector.scalar_tensor_tensor(out=cqT[:, m, :], in0=cqT[:, m, :], scalar=vecT[:, 16 + m:17 + m],
                                                   in1=rq, op0=ALU.mult, op1=ALU.mult)
                nc.vector.scalar_tensor_tensor(out=ckvT, in0=ckvT, scalar=vecT[:, 18:19], in1=rk,
                                               op0=ALU.mult, op1=ALU.mult).then_inc(latents_ready, 1)
                index_sums(3, 4)
                wait_drained(dve, "afT")
                dve.wait_ge(softplus_ready, 1)
                link(nc.vector.tensor_tensor_scan(fg[1], fg[2], fg[3], 0.0, ALU.add, ALU.add))
                nc.vector.tensor_scalar(fg[0], fg[1], -8.0, None, ALU.mult).then_inc(forget_ready, 1)
                dve.wait_ge(forget_ready, 1)
                nc.vector.tensor_scalar(fg[1], fg[1], 8.0, None, ALU.mult).then_inc(forget_ready, 1)
                mod_drain(6)
                mod_drain(7)
                top(3)
                mod_chunks(8, 9)
                dve.wait_ge(rope_landed, 32)
                wait_filled(dve, "qBr")
                nc.vector.tensor_tensor(rope1, bank("qBr")[:, :], cosT, ALU.mult).then_inc(dve_drained, 1)
                wait_filled(dve, "qBs")
                nc.vector.tensor_tensor(rope2, bank("qBs")[:, :], sinT, ALU.mult).then_inc(dve_drained, 1)
                wait_drained(dve, "qBs")
                for h in range(HEADS):
                    s = slice(32 * h, 32 * h + 32)
                    last = nc.vector.tensor_tensor(qB[64:96, h, :], rope1[s, :], rope2[s, :], ALU.add)
                last.then_inc(qrope_ready, 1)

                mod_drain(8)
                mod_drain(9)

                def scores(u):
                    g, i, h = UNITS[u]
                    n = keys(g, i)[1]
                    t = tring[:, u % 4, :]
                    if g == "C":
                        mask = window[:, 2 * P - n:2 * P]
                        nc.vector.tensor_copy(t[:, n:n + 1], nsink[:, h:h + 1])
                    elif g == "D" and i > 0:
                        at = P * (i * (i + 1) // 2 - 1)
                        mask = selmask[:, at:at + n]
                    else:
                        mask = causal[:, SEQ - n:SEQ]
                    scale = (NOPE + ROPE) ** -0.5 if g == "B" else HD ** -0.5
                    wait_filled(dve, ("S", u))
                    nc.vector.tensor_tensor_reduce(t[:, 0:n], bank(("S", u))[:, 0:n], mask, -scale,
                                                   nsink[:, h:h + 1] if g == "C" else BIG, ALU.add, ALU.min,
                                                   nmax[:, u:u + 1]).then_inc(dve_drained, 1)

                dve.wait_ge(nsink_ready, 1)
                dve.wait_ge(topk_done, TT - 1)
                for u in range(3):
                    scores(u)
                for u in range(len(UNITS)):
                    if u % 2 == 0:
                        n = keys(*UNITS[u][:2])[1]
                        wait_filled(dve, ("T", u))
                        nc.vector.tensor_copy(pring[:, u % 3, 0:n], bank(("T", u))[:, 0:n]).then_inc(dve_drained, 1)
                    if u + 3 < len(UNITS):
                        scores(u + 3)
                    if u in MOD_AT:
                        mod_drain(MOD_AT[u])
                    for j, k in STEP_AT[u]:
                        mod_step(j, k)
                    if u % HEADS == 0 and u > 0 or u == last_unit:
                        for og in ([u // HEADS - 1] if u < last_unit else [u // HEADS]):
                            g, i, _ = UNITS[og * HEADS]
                            at = GROUPS.index(g) * HEADS * HD
                            dve.wait_ge(o_filled, og + 1)
                            link(nc.vector.reciprocal(rsd, sums[:, og * HEADS:(og + 1) * HEADS]))
                            nc.vector.tensor_tensor(
                                tok[:, i, at:at + 256].rearrange("p (h d) -> p h d", h=HEADS),
                                banks[6 + og % 2][:, 0:256].rearrange("p (h d) -> p h d", h=HEADS),
                                rsd.unsqueeze(2).to_broadcast([P, HEADS, HD]), ALU.mult).then_inc(o_drained, 1)
                for k in range(0, KT, 2):
                    wait_filled(dve, ("mT", k))
                    nc.vector.tensor_copy(hT[:, k, :], bank(("mT", k))[:, :]).then_inc(dve_drained, 1)

                def diagonals(n, v):
                    for k in range(KT):
                        last = nc.vector.tensor_scalar(diags[n][:, k * P:(k + 1) * P], ident[:, :], v[:, k:k + 1],
                                                       None, ALU.mult)
                    last.then_inc(diag_ready, 1)

                diagonals(0, modT[:, 16:24])
                mod_drain(OWN - 1)
                nc.vector.scalar_tensor_tensor(out=scaleT[:, 8:16], in0=modT[:, 32:40], scalar=1.0, in1=vecT[:, 8:16],
                                               op0=ALU.add, op1=ALU.mult).then_inc(scales_ready, 1)
                dve.wait_ge(scales_ready, 1)
                mod_chunks(OWN)

                def h2_half(i):
                    wait_filled(dve, ("h2", i, 1))
                    for k in range(4):
                        last = modulate2(hT[:, 4 + k, i * P:(i + 1) * P], bank(("h2", i, 1))[:, k * P:(k + 1) * P], 4 + k)
                    last.then_inc(dve_drained, 1)

                def modulate2(dst, src, k):
                    return nc.vector.tensor_scalar(dst, src, scaleT[:, 8 + k:9 + k], modT[:, 24 + k:25 + k], ALU.mult, ALU.add)

                for i in range(TT):
                    for m in range(2):
                        n, name = 2 * i + m, ("out", i, m)
                        wait_filled(dve, name)
                        wait_drained(dve, ("gt1", 1))
                        if n >= 2:
                            dve.wait_ge(x_added, n - 1)
                        nc.vector.tensor_tensor(tring[:, n % 2, :], bank(name)[:, :], gtB[:, m * 512:(m + 1) * 512],
                                                ALU.mult).then_inc(dve_drained, 1)
                        wait_drained(dve, name)
                        xs = x[:, i, m * 512:(m + 1) * 512]
                        nc.vector.tensor_tensor(xs, xs, tring[:, n % 2, :], ALU.add).then_inc(x_added, 1)
                        if m == 0 and i > 0:
                            mod_drain(OWN + 2 * i - 1)
                            if i == TT - 1:
                                mod_chunks(MODS - 1)
                    if i > 0:
                        h2_half(i - 1)
                    if i < TT - 1:
                        mod_chunks(OWN + 2 * i + 1)
                    norm_rows(i, root_ready, i + 1, link, rows2_ready)
                    if i < TT - 1:
                        mod_drain(OWN + 2 * i)
                        mod_chunks(OWN + 2 * i + 2)
                    if i == TT - 2:
                        diagonals(1, modT[:, 40:48])
                mod_drain(MODS - 2)
                mod_drain(MODS - 1)
                h2_half(TT - 1)
                r = [rout[:, n, :] for n in range(8)]
                quads = lambda a: a.rearrange("p (g e) -> p g e", e=4)
                wait_drained(dve, ("router", TT - 1))
                link(nc.vector.tensor_tensor(r[1].rearrange("p (i e) -> p i e", e=NE), r[0].rearrange("p (i e) -> p i e", e=NE),
                                             brt.unsqueeze(1).to_broadcast([P, TT, NE]), ALU.add))
                rank(quads(r[2]), quads(r[1]), selmask[:, 0:256], selmask[:, 256:512])
                link(nc.vector.tensor_scalar(r[4], r[2], 2.0, None, ALU.is_lt))
                link(nc.vector.tensor_tensor(r[3], r[1], r[4], ALU.mult))
                link(nc.vector.tensor_reduce(r[4][:, 0:16], quads(r[3]), AX.X, ALU.add))
                rank(quads(r[5][:, 0:16]), quads(r[4][:, 0:16]), selmask[:, 0:64], selmask[:, 64:128])
                link(nc.vector.tensor_scalar(r[5][:, 0:16], r[5][:, 0:16], 1.0, None, ALU.is_lt))
                best = r[5][:, 0:16].unsqueeze(2).to_broadcast([P, 16, 4])
                for c in range(2):
                    link(nc.vector.tensor_scalar(mk[:, c, :], r[2], float(c), None, ALU.is_equal))
                    link(nc.vector.tensor_tensor(quads(mk[:, c, :]), quads(mk[:, c, :]), best, ALU.mult))
                nc.vector.tensor_tensor(r[7], mk[:, 0, :], mk[:, 1, :], ALU.add).then_inc(chosen, 1)

                def of_choice(dst, src):
                    for c in range(2):
                        link(nc.vector.tensor_tensor(prod[:, c, :], mk[:, c, :], src, ALU.mult))
                    link(nc.vector.tensor_reduce(dst, prod.rearrange("p c (i e) -> p (c i) e", e=NE), AX.X, ALU.add))

                gates, den = tiny[:, 0:8], tiny[:, 8:12]
                of_choice(gates, r[0])
                link(nc.vector.tensor_tensor(den, gates[:, 0:TT], gates[:, TT:2 * TT], ALU.add))
                link(nc.vector.reciprocal(den, den))
                link(nc.vector.tensor_tensor(gates[:, 0:TT], gates[:, 0:TT], den, ALU.mult))
                nc.vector.tensor_tensor(gates[:, TT:2 * TT], gates[:, TT:2 * TT], den, ALU.mult).then_inc(gates_ready, 1)
                wait_filled(dve, "pos")
                nc.vector.tensor_copy(posb, bank("pos")[:, 0:80]).then_inc(dve_drained, 1)
                wait_drained(dve, "pos")
                pos, cnt = posb[:, 0:64], posb[:, 64:80]
                more, upto, first = tiny[:, 16:32], tiny[:, 32:48], tiny[:, 48:64]
                link(nc.vector.tensor_scalar(more, cnt, float(P), None, ALU.is_gt))
                for n in (2, 3):
                    link(nc.vector.scalar_tensor_tensor(out=more, in0=cnt, scalar=float(n * P), in1=more,
                                                        op0=ALU.is_gt, op1=ALU.add))
                link(nc.vector.tensor_tensor_scan(upto, ones[:, 0:NE], more, 0.0, ALU.mult, ALU.add))
                link(nc.vector.scalar_tensor_tensor(out=first, in0=upto, scalar=float(NE - 1), in1=more,
                                                    op0=ALU.add, op1=ALU.subtract))
                link(nc.vector.tensor_tensor(first, first, iota[:, 0:NE], ALU.subtract))
                four = lambda a: a.rearrange("p (i e) -> p i e", e=NE)
                over = lambda a: a.unsqueeze(1).to_broadcast([P, TT, NE])
                link(nc.vector.tensor_scalar(rowf, pos, float(P), None, ALU.is_ge))
                link(nc.vector.tensor_tensor(four(rowf), four(rowf), over(first), ALU.mult))
                link(nc.vector.tensor_tensor(four(rowf), four(rowf), over(iota[:, 0:NE]), ALU.add))
                link(nc.vector.scalar_tensor_tensor(out=rowf, in0=rowf, scalar=float(P), in1=pos, op0=ALU.mult, op1=ALU.add))
                rows = tiny[:, 64:72]
                of_choice(rows, rowf)
                link(nc.vector.tensor_copy(row_of, rows))
                link(nc.vector.tensor_scalar(tile_i, row_of, 7, None, ALU.logical_shift_right))
                link(nc.vector.tensor_scalar(slot_i, row_of, P - 1, None, ALU.bitwise_and))
                link(nc.vector.tensor_copy(tiny[:, 72:88], ints[:, 8:24]))
                dve.wait_ge(x_added, 2 * TT)
                slots, tiles = [P, 8, P], [P, 8, MAX_TILES]
                link(nc.vector.tensor_tensor(in_tile, iota[:, 0:MAX_TILES].unsqueeze(1).to_broadcast(tiles),
                                             tiny[:, 72:80].unsqueeze(2).to_broadcast(tiles), ALU.is_equal))
                nc.vector.tensor_tensor(in_tile, in_tile, token1.unsqueeze(2).to_broadcast(tiles), ALU.mult)
                nc.vector.tensor_tensor(in_slot, iota.unsqueeze(1).to_broadcast(slots),
                                        tiny[:, 80:88].unsqueeze(2).to_broadcast(slots), ALU.is_equal).then_inc(onehots_ready, 1)
                full = [P, OTHERS, NE]
                ends = rout[:, 1:3, :].rearrange("p a n -> p (a n)").rearrange("p (k e) -> p k e", e=NE)
                link(nc.vector.tensor_tensor(ends, upto.unsqueeze(1).to_broadcast(full),
                                             iota[:, 0:OTHERS].unsqueeze(2).to_broadcast(full), ALU.is_le))
                link(nc.vector.tensor_reduce(tiny[:, 88:88 + OTHERS], ends, AX.X, ALU.add))
                link(nc.vector.tensor_scalar(tiny[:, 88:88 + OTHERS], tiny[:, 88:88 + OTHERS], float(NE - 1), None, ALU.min))
                nc.vector.tensor_copy(expert_of[:, 0:NE], iota[:, 0:NE])
                nc.vector.tensor_copy(expert_of[:, NE:MAX_TILES], tiny[:, 88:88 + OTHERS])
                np_f = tiny[:, 96:97]
                link(nc.vector.tensor_scalar(np_f, upto[:, NE - 1:NE], 1.0, float(NE // 2), ALU.is_ge, ALU.add))
                for n in (3, 5, 7):
                    link(nc.vector.scalar_tensor_tensor(out=np_f, in0=upto[:, NE - 1:NE], scalar=float(n), in1=np_f,
                                                        op0=ALU.is_ge, op1=ALU.add))
                nc.vector.tensor_copy(pairs_i, np_f).then_inc(routed, 1)
                wait_filled(dve, "inv")
                nc.vector.tensor_scalar(token_of, bank("inv")[:, 0:MAX_TILES], -1.0, 0.0, ALU.add, ALU.max)\
                    .then_inc(dve_drained, 1)
                pairs = pairs_of(dve)

                def turned(pair, s):
                    dve.wait_ge(xt_filled, pair * 4 + (2 * s + 2))
                    for k in range(4):
                        last = modulate2(xgT[s][:, (4 + k) * P:(5 + k) * P], banks[1][:, k * P:(k + 1) * P], 4 + k)
                    last.then_inc(xt_dve, 1)

                def hidden(pair, s):
                    dve.wait_ge(silu_ready, pair * 2 + (s + 1))
                    nc.vector.tensor_tensor(hid[s], banks[2 + s][:, 256:512], sg[s], ALU.mult).then_inc(hidden_ready, 1)

                def output(pair, s, ago=0):
                    dve.wait_ge(y_stored[s], pair * 16 + (16 - 16 * ago))
                    dve.sem_inc(dve_passed, 1)
                    for m in range(2):
                        dve.wait_ge(down_filled, pair * 4 + (2 * s + m + 5 - 4 * ago))
                        nc.vector.tensor_tensor(ysb[s][:, m * 512:(m + 1) * 512], banks[4 + 2 * s + m][:, :],
                                                gtB[:, m * 512:(m + 1) * 512], ALU.mult).then_inc(y_taken, 1)

                wait_drained(dve, ("gt2", 1))
                for s in range(2):
                    turned(0, s)
                for s in range(2):
                    hidden(0, s)
                with dve.Fori(1, pairs) as pair:
                    for s in range(2):
                        turned(pair, s)
                        output(pair, s, 1)
                    for s in range(2):
                        hidden(pair, s)
                for s in range(2):
                    output(pairs, s, 1)
                dve.wait_ge(gates_ready, 1)
                for i in range(TT):
                    dve.wait_ge(choice_landed[i], 32)
                    for c, y in enumerate((tok[:, i, :], hT[:, 2 * i:2 * i + 2, :].rearrange("p a n -> p (a n)"))):
                        nc.vector.scalar_tensor_tensor(out=x[:, i, :], in0=y, scalar=gates[:, c * TT + i:c * TT + i + 1],
                                                       in1=x[:, i, :], op0=ALU.mult, op1=ALU.add).then_inc(combined, 1)
                        dve.wait_ge(combined, 2 * i + c + 1)
                    if i > 0:
                        norm_rows(i - 1, root_ready, TT + i, link, xhat_ready)
                norm_rows(TT - 1, root_ready, 2 * TT, link, xhat_ready)
                dve.wait_ge(small_landed, SMALLS * 16)
                scale1(scales_ready)
                dve.wait_ge(scales_ready, 2)
                dve.wait_ge(xhat_ready, TT)
                dve.sem_inc(layer_end, 1)
                dve.wait_ge(layer_go, l + 1)
            totals[dve_step] = step[0]
            dve.wait_ge(consts_landed, (CONSTS + 1) * 16)
            for i in range(TT):
                nc.vector.tensor_tensor(tok[:, i, :], tok[:, i, :], gtB[:, :], ALU.mult).then_inc(fin_rows, 1)

        @block.tensor
        def _(pe):
            def mm(dst, lhsT, rhs, first=True, last=True):
                return nc.tensor.matmul(dst, lhsT, rhs, start=first, stop=last)

            def features(name, rows, w, rhs, kt):
                wait_bank(pe, name)
                for k in range(kt):
                    last = mm(bank(name)[0:rows, :], w(k), rhs[:, k, :], k == 0, k == kt - 1)
                last.then_inc(psum_filled, 1)

            def project(name, n, at, rows):
                features(name, rows, lambda k: slot(n, CHUNKS[n][1])[:, k, at:at + rows], hT, KT)

            def turn(name, parts):
                wait_bank(pe, name)
                for dst, src, size in parts:
                    last = nc.tensor.transpose(dst, src, ident[0:size, 0:size])
                last.then_inc(psum_filled, 1)

            def turn_rows(name, k):
                turn(name, [(bank(name)[:, i * P:(i + 1) * P], tok[:, i, k * P:(k + 1) * P], P) for i in range(TT)])

            pe.wait_ge(consts_landed, CONSTS * 16)
            pe.wait_ge(consts_set, 3)
            pe.wait_ge(first_bada_landed, 16)
            nc.tensor.transpose(banks[7][:, 0:16], bada[0:16, :], ident[0:16, 0:16]).then_inc(first_turned, 1)
            pe.wait_ge(first_used, NEXT)
            for j in range(2 * NEXT):
                last = mm(banks[6][:, j:j + 1], first_acc[:, j // 2, (j % 2) * P:(j % 2 + 1) * P], ones[:, 0:1])
            last.then_inc(first_filled, 1)
            pe.wait_ge(first_mod, 1)
            pe.wait_ge(first_rows, TT)
            pe.wait_ge(padded, 8)
            pe.wait_ge(rows_landed, 6 * 16)
            pe.wait_ge(first_small_landed, SMALLS * 16)
            with pe.Fori(0, DEPTH) as l:
                def mod_sum(j):
                    pe.wait_ge(ada_used, j + 1)
                    wait_bank(pe, ("mod", j))
                    for n in range(2):
                        last = mm(bank(("mod", j))[:, n:n + 1], ada_acc[:, j % 2, n * P:(n + 1) * P], ones[:, 0:1])
                    last.then_inc(psum_filled, 1)

                turn("bias", [(bank("bias")[:, 0:48], bada[0:48, :], 48)])
                for k in range(KT):
                    turn_rows(("h1", k), k)
                wait_drained(pe, ("h1", KT - 1))
                wait_drained(pe, ("h1", KT - 2))
                for m in range(2):
                    project(("qi", m), 0, m * P, P)
                project("kiwi", 0, 256, 104)
                mod_sum(0)
                mod_sum(1)
                pe.wait_ge(win_landed[1], 16)
                project(("qD", 0), 1, 0, P)
                wait_drained(pe, "kiwi")
                turn("wiT", [(bank("wiT")[:, i * 8:(i + 1) * 8], kiwiT[0:8, i * P:(i + 1) * P], 8) for i in range(TT)])

                def host(name, n, at, i, first):
                    wait_bank(pe, name)
                    for k in range(KT):
                        if k % 2 == 0:
                            h = first + k // 2
                            r = slice(32 * (h % 4), 32 * (h % 4) + 32)
                            wait_bank(pe, ("idx", i, h))
                            mm(bank(("idx", i, h))[:, 0:P * (i + 1)], qi[r, h // 4, i * P:(i + 1) * P], ki[r, 0:P * (i + 1)])\
                                .then_inc(psum_filled, 1)
                        last = mm(bank(name)[:, :], slot(n, CHUNKS[n][1])[:, k, at:at + P], hT[:, k, :], k == 0, k == KT - 1)
                    last.then_inc(psum_filled, 1)

                host(("qD", 1), 1, P, 1, 0)
                mod_sum(2)
                mod_sum(3)
                host("kvD", 1, 256, 1, 4)
                pe.wait_ge(win_landed[2], 16)
                project(("cq", 0), 2, 0, P)
                wait_drained(pe, "kvD")
                turn("vDT", [(bank("vDT")[:, i * 64:(i + 1) * 64], vdT[0:64, i * P:(i + 1) * P], 64) for i in range(TT)])
                project(("cq", 1), 2, P, P)
                project("ckv", 2, 256, P)
                mod_sum(4)
                mod_sum(5)
                pe.wait_ge(win_landed[3], 16)
                host(("qA", 0), 3, 0, 2, 0)
                host(("qA", 1), 3, P, 2, 4)
                project(("kA", 0), 3, 256, P)
                pe.wait_ge(cq_squared, 3)
                wait_bank(pe, "ssq")
                for m in range(2):
                    last = mm(bank("ssq")[:, :], ones[:, :], sqT[:, m, :], m == 0, m == 1)
                last.then_inc(psum_filled, 1)
                wait_bank(pe, "ssk")
                mm(bank("ssk")[:, :], ones[:, :], sqT[:, 2, :]).then_inc(psum_filled, 1)
                pe.wait_ge(win_landed[4], 16)
                host(("kA", 1), 4, 0, 3, 0)
                for i in range(TT):
                    wait_bank(pe, ("vA", i))
                    for k in range(KT):
                        last = mm(bank(("vA", i))[:, 0:260], hT[:, k, i * P:(i + 1) * P], slot(4, 388)[:, k, 128:388],
                                  k == 0, k == KT - 1)
                    last.then_inc(psum_filled, 1)
                wait_drained(pe, ("vA", TT - 1))
                turn("afT", [(bank("afT")[0:4, i * P:(i + 1) * P], vA[:, i, 256:260], P) for i in range(TT)])
                pe.wait_ge(win_landed[5], 16)
                host(("qC", 0), 5, 0, 3, 4)
                mod_sum(6)
                mod_sum(7)
                project(("qC", 1), 5, P, P)
                project("kC", 5, 256, P)
                pe.wait_ge(win_landed[6], 16)
                wait_bank(pe, "vC")
                for i in range(TT):
                    for k in range(KT):
                        last = mm(bank("vC")[:, i * P:(i + 1) * P], hT[:, k, i * P:(i + 1) * P], slot(6, 128)[:, k, :],
                                  k == 0, k == KT - 1)
                last.then_inc(psum_filled, 1)
                pe.wait_ge(latents_ready, 1)
                for m in range(2):
                    features(("qBn", m), P, lambda k: wq_n[:, k, m * P:(m + 1) * P], cqT, 2)
                features("qBr", P, lambda k: wq_r[:, k, :], cqT, 2)
                features("qBs", P, lambda k: wq_s[:, k, :], cqT, 2)
                for m in range(2):
                    wait_bank(pe, ("kBn", m))
                    mm(bank(("kBn", m))[:, :], wk_n[:, m * P:(m + 1) * P], ckvT).then_inc(psum_filled, 1)
                for m in range(2):
                    wait_bank(pe, ("vB", m))
                    for j in range(2):
                        i = 2 * m + j
                        last = mm(bank(("vB", m))[:, j * 256:(j + 1) * 256], ckvT[:, i * P:(i + 1) * P], wk_v[:, :])
                    last.then_inc(psum_filled, 1)
                mod_sum(8)
                mod_sum(9)

                Q = {"A": qA, "B": qB, "C": qC, "D": qD}
                K = {"A": lambda h: kA[:, h, :], "B": lambda h: kB[:, h, :], "C": lambda h: kC[:, h // 2, :],
                     "D": lambda h: kD[:, :]}
                V = {"A": lambda h, t: vA[:, t, h * HD:(h + 1) * HD], "B": lambda h, t: vB[:, t, h * HD:(h + 1) * HD],
                     "C": lambda h, t: vC[:, t, (h // 2) * HD:(h // 2 + 1) * HD], "D": lambda h, t: vD[:, t, :]}

                def unit_scores(u):
                    g, i, h = UNITS[u]
                    k0, n = keys(g, i)
                    wait_bank(pe, ("S", u))
                    mm(bank(("S", u))[:, 0:n], Q[g][:, h, i * P:(i + 1) * P], K[g](h)[:, k0:k0 + n])\
                        .then_inc(psum_filled, 1)

                def unit_turn(u):
                    g, i, _ = UNITS[u]
                    pe.wait_ge(probs_ready, u + 1)
                    b = bank(("T", u))
                    turn(("T", u), [(b[:, t * P:(t + 1) * P], tring[:, u % 4, t * P:(t + 1) * P], P)
                                    for t in range(keys(g, i)[1] // P)])

                def unit_values(u):
                    g, i, h = UNITS[u]
                    k0, n = keys(g, i)
                    og = u // HEADS
                    if h == 0 and og >= 2:
                        pe.wait_ge(o_drained, og - 1)
                    wait_drained(pe, ("T", u))
                    for t in range(n // P):
                        last = mm(banks[6 + og % 2][:, h * HD:(h + 1) * HD], pring[:, u % 3, t * P:(t + 1) * P],
                                  V[g](h, k0 // P + t), t == 0, t == n // P - 1)
                    if h == HEADS - 1:
                        last.then_inc(o_filled, 1)

                pe.wait_ge(forget_landed, 8 * 16)
                pe.wait_ge(qrope_ready, 1)
                pe.wait_ge(krope_ready, 2 + HEADS)
                wait_drained(pe, ("vB", 1))
                for u in range(3):
                    unit_scores(u)
                for u in range(len(UNITS)):
                    unit_turn(u)
                    if u + 3 < len(UNITS):
                        unit_scores(u + 3)
                    if u in MOD_AT:
                        mod_sum(MOD_AT[u])
                    if u > 0:
                        unit_values(u - 1)
                unit_values(last_unit)
                pe.wait_ge(o_drained, len(UNITS) // HEADS)
                for k in range(KT):
                    turn_rows(("mT", k), k)

                def spread(name, n):
                    pe.wait_ge(diag_ready, n + 1)
                    for m in range(2):
                        wait_bank(pe, (name, m))
                        mm(bank((name, m))[:, :], ones[:, :], diags[n][:, m * 512:(m + 1) * 512]).then_inc(psum_filled, 1)

                def router(i):
                    wait_drained(pe, ("h2", i, 0))
                    wait_drained(pe, ("h2", i, 1))
                    wait_bank(pe, ("router", i))
                    for k in range(KT):
                        last = mm(bank(("router", i))[:, 0:NE], hT[:, k, i * P:(i + 1) * P], wr[:, k, :],
                                  k == 0, k == KT - 1)
                    last.then_inc(psum_filled, 1)

                def h2(i):
                    pe.wait_ge(rows2_ready, i + 1)
                    for half in range(2):
                        name = ("h2", i, half)
                        turn(name, [(bank(name)[:, k * P:(k + 1) * P], tok[:, i, (4 * half + k) * P:(4 * half + k + 1) * P], P)
                                    for k in range(4)])

                mod_sum(OWN - 1)
                wait_drained(pe, ("mT", KT - 1))
                wait_drained(pe, ("mT", KT - 2))
                pe.wait_ge(wout_landed, 16)
                for i in range(TT):
                    for m in range(2):
                        name = ("out", i, m)
                        wait_bank(pe, name)
                        for k in range(KT):
                            last = mm(bank(name)[:, :], hT[:, k, i * P:(i + 1) * P], wo[:, k, m * 512:(m + 1) * 512],
                                      k == 0, k == KT - 1)
                        last.then_inc(psum_filled, 1)
                        if m == 0 and i == 0:
                            spread("gt1", 0)
                        if m == 0 and i > 0:
                            mod_sum(OWN + 2 * i - 1)
                            if i > 1:
                                router(i - 2)
                    if i > 0:
                        h2(i - 1)
                    if i < TT - 1:
                        mod_sum(OWN + 2 * i)
                spread("gt2", 1)
                router(TT - 2)
                mod_sum(MODS - 2)
                mod_sum(MODS - 1)
                h2(TT - 1)
                router(TT - 1)
                pe.wait_ge(chosen, 1)
                wait_bank(pe, "pos")
                sel = rout[:, 7, :]
                mm(bank("pos")[:, 0:NE], before, sel[:, 0:NE])
                for j in range(TT):
                    last = mm(bank("pos")[:, (j + 1) * NE:(TT + 1) * NE].rearrange("p (i e) -> p i e", e=NE), ones[:, :],
                              sel[:, j * NE:(j + 1) * NE].unsqueeze(1).to_broadcast([P, TT - j, NE]), j == 0, j == TT - 1)
                    if j == 0:
                        mm(bank("pos")[:, NE:TT * NE], before, sel[:, NE:TT * NE], False, False)
                last.then_inc(psum_filled, 1)
                pe.wait_ge(onehots_ready, 1)
                wait_bank(pe, "inv")
                for n in range(8):
                    last = mm(bank("inv")[:, 0:MAX_TILES], in_slot[:, n, :], in_tile[:, n, :], n == 0, n == 7)
                last.then_inc(psum_filled, 1)
                pe.wait_ge(act_drained, count["act"])
                pe.wait_ge(dve_drained, count["dve"])
                pairs = pairs_of(pe)

                def turn_tile(pair, s):
                    pe.wait_ge(xg_landed[s], pair * 16 + 16)
                    pe.sem_inc(pe_passed, 1)
                    for half, taken in ((0, xt_act), (1, xt_dve)):
                        pe.wait_ge(taken, pair * 2 + (s + 2))
                        for k in range(4):
                            last = nc.tensor.transpose(banks[half][:, k * P:(k + 1) * P],
                                                       xg[s][:, (4 * half + k) * P:(4 * half + k + 1) * P], ident[:, :])
                        last.then_inc(xt_filled, 1)

                def gate_up(pair, s):
                    g, u, d = expert(s)
                    pe.wait_ge(xt_act, pair * 2 + (s + 3))
                    pe.wait_ge(xt_dve, pair * 2 + (s + 3))
                    pe.wait_ge(gu_landed[s], pair * 32 + 32)
                    for n in range(4):
                        w = (g, u)[n // 2]
                        for k in range(KT):
                            last = mm(banks[2 + s][:, n * P:(n + 1) * P], w[:, k, (n % 2) * P:(n % 2 + 1) * P],
                                      xgT[s][:, k * P:(k + 1) * P], k == 0, k == KT - 1)
                    last.then_inc(gu_filled, 1)

                def down(pair, s, ago=1):
                    g, u, d = expert(s)
                    pe.wait_ge(hidden_ready, pair * 2 + (s + 3 - 2 * ago))
                    pe.wait_ge(d_landed[s], pair * 16 + (16 - 16 * ago))
                    for m in range(2):
                        pe.wait_ge(y_taken, pair * 4 + (2 * s + m + 5 - 4 * ago))
                        for f in range(2):
                            last = mm(banks[4 + 2 * s + m][:, :], hid[s][:, f * P:(f + 1) * P],
                                      d[:, f, m * 512:(m + 1) * 512], f == 0, f == 1)
                        last.then_inc(down_filled, 1)

                for s in range(2):
                    turn_tile(0, s)
                for s in range(2):
                    gate_up(0, s)
                with pe.Fori(1, pairs) as pair:
                    for s in range(2):
                        turn_tile(pair, s)
                        down(pair, s)
                    for s in range(2):
                        gate_up(pair, s)
                for s in range(2):
                    down(pairs, s)
                pe.sem_inc(layer_end, 1)
                pe.wait_ge(layer_go, l + 1)

        @block.sync
        def _(sp):
            def flat_bias(l, first, last):
                return b_ada[bass.ds(l, 1)].rearrange("a (r n) -> (a r) n", n=P)[first:last, :]

            def layer(l, t):
                return t[bass.ds(l, 1)]

            def flat(l, t, pattern, **kw):
                return layer(l, t).rearrange(pattern, **kw)

            def load_columns(l, n, landed):
                columns, at = flat(l, w_in, "a (k p) n -> p (a k) n", p=P), 0
                for first, cols in INDEX_PARTS if n == 0 else [(CHUNK_AT[n], CHUNKS[n][1])]:
                    sp.dma_start(slot(n, CHUNKS[n][1])[:, :, at:at + cols], columns[:, :, first:first + cols],
                                 allow_slow_non_contiguous=cols < 64).then_inc(landed, 16)
                    at += cols

            def load_small(l, after, landed):
                sp.dma_start(bada[0:32, :], flat_bias(l, 2 * D // P, 48)).then_inc(landed, 16)
                sp.dma_start(bada[32:48, :], flat_bias(after, 0, 16)).then_inc(landed, 16)
                for dst, src in [(vecT[:, 0:8], flat(l, g_norm1, "a (k p) -> p (a k)", p=P)),
                                 (vecT[:, 8:16], flat(l, g_norm2, "a (k p) -> p (a k)", p=P)),
                                 (vecT[:, 16:18], flat(l, g_q_mla, "a (k p) -> p (a k)", p=P)),
                                 (vecT[:, 18:19], flat(l, g_kv_mla, "a (k p) -> p (a k)", p=P)),
                                 (bfg[0:4, :], flat(l, b_forget, "a h -> h a")),
                                 (sinkb, layer(l, sinks).partition_broadcast(P))]:
                    sp.dma_start(dst, src, allow_slow_non_contiguous=True).then_inc(landed, 16)
                wq = flat(l, w_q_up, "a (k p) (h e) -> p (a k) h e", p=P, h=HEADS)
                for k in range(2):
                    sp.dma_start(wq_n[:, k, :].rearrange("p (h e) -> p h e", h=HEADS),
                                 wq[:, k, :, 0:NOPE]).then_inc(landed, 16)
                    sp.dma_start(wq_r[:, k, :].rearrange("p (h e) -> p h e", h=HEADS),
                                 wq[:, k, :, NOPE:]).then_inc(landed, 16)
                    for a in range(2):
                        sp.dma_start(wq_s[:, k, :].rearrange("p (h b e) -> p h b e", h=HEADS, b=2)[:, :, a, :],
                                     wq[:, k, :, NOPE + 16 * (1 - a):NOPE + 16 * (2 - a)],
                                     allow_slow_non_contiguous=True).then_inc(landed, 16)
                wkv = flat(l, w_kv_up, "a p (h b e) -> p (a h) b e", h=HEADS, b=2)
                sp.dma_start(wk_n[:, :].rearrange("p (h e) -> p h e", h=HEADS), wkv[:, :, 0, :]).then_inc(landed, 16)
                sp.dma_start(wk_v[:, :].rearrange("p (h e) -> p h e", h=HEADS), wkv[:, :, 1, :]).then_inc(landed, 16)

            sp.dma_start(cT, c_in.rearrange("b (k p) -> p (b k)", p=P), allow_slow_non_contiguous=True).then_inc(c_landed, 16)

            def load_first_ada(j):
                wa0 = w_ada[0:1].rearrange("a (k p) n -> p (a k) n", p=P)
                sp.dma_start(first_slot(j), wa0[:, :, j * ADA:(j + 1) * ADA]).then_inc(first_ada_landed[j % 4], 16)

            load_first_ada(0)
            load_first_ada(1)
            for dst, src in [(x[:, :, :], x_in.rearrange("b (i p) d -> p (b i) d", p=P)),
                             (ident[:, :], k_ident), (route[:, :], k_route), (causal[:, :], k_causal), (window[:, :], k_window),
                             (wr[:, :, :], w_router.rearrange("(k p) e -> p k e", p=P)),
                             (brt, b_router.rearrange("(a e) -> a e", a=1).partition_broadcast(P))]:
                sp.dma_start(dst, src, allow_slow_non_contiguous=True).then_inc(consts_landed, 16)

            sp.dma_start(bada[0:16, :], flat_bias(0, 0, 16)).then_inc(first_bada_landed, 16)
            for j in range(2, NEXT):
                if j >= 4:
                    sp.wait_ge(first_used, j - 3)
                load_first_ada(j)
            sp.wait_ge(padded, 6)
            for dst, src in [(qC[64:66, :, :], k_rows[:, 0:4, :]), (kC[64:66, :, :], k_rows[:, 4:6, :]),
                             (qD[64:66, :, :], k_rows[:, 6:10, :]), (kD[64:66, :], k_rows[:, 10, :]),
                             (qA[65:66, :, :], k_rows[0:1, 11:15, :]), (kA[64:65, :, :], k_rows[0:1, 15:19, :])]:
                sp.dma_start(dst, src).then_inc(rows_landed, 16)
            sp.wait_ge(first_turned, 1)
            load_small(0, min(1, DEPTH - 1), first_small_landed)
            load_columns(0, 0, first_small_landed)
            sp.wait_ge(first_used, NEXT)
            sp.wait_ge(next_ready, 1)

            with sp.Fori(0, DEPTH) as l:
                after = sp.value_load(next_i[0:1, bass.ds(l, 1)], min_val=0, max_val=DEPTH - 1)

                def load_in(n):
                    wait_filled(sp, chunk_last_job[n - SLOTS])
                    load_columns(l, n, win_landed[n])

                def load_ada(j):
                    if j >= 2:
                        sp.wait_ge(ada_used, j - 1)
                    whose, at = (l, 2 * D + j * ADA) if j < OWN else (after, (j - OWN) * ADA)
                    sp.dma_start(ada_slot(j), w_ada[bass.ds(whose, 1)].rearrange("a (k p) n -> p (a k) n", p=P)[:, :, at:at + ADA])\
                        .then_inc(ada_landed[j % 2], 16)

                load_columns(l, 1, win_landed[1])
                for j in range(4):
                    load_ada(j)
                load_in(2)
                load_in(3)
                load_ada(4)
                load_ada(5)
                load_in(4)
                load_ada(6)
                load_ada(7)
                load_in(5)
                load_ada(8)
                load_ada(9)
                load_in(6)
                sp.wait_ge(relu_used, 3 * IDX_HEADS)
                sp.dma_start(cosT, k_cos).then_inc(rope_landed, 16)
                sp.dma_start(sinT, k_sin).then_inc(rope_landed, 16)
                sp.wait_ge(forget_ready, 2)
                for h in range(HEADS):
                    sp.dma_start(qA[64:65, h, :], fg[0][h:h + 1, :]).then_inc(forget_landed, 16)
                    sp.dma_start(kA[65:66, h, :], fg[1][h:h + 1, :]).then_inc(forget_landed, 16)
                wait_filled(sp, "vC")
                sp.dma_start(wo, flat(l, w_out, "a (k p) n -> p (a k) n", p=P)).then_inc(wout_landed, 16)
                for j in range(10, MODS):
                    load_ada(j)

                for n in range(OTHERS):
                    sp.dma_start(y_rows[(NE + n) * P:(NE + n + 1) * P, :], k_zero).then_inc(y_cleared, 16)

                def store_rows(i):
                    sp.wait_ge(rows2_ready, i + 1)
                    sp.dma_start(norm_rows2[i * P:(i + 1) * P, :], tok[:, i, :]).then_inc(rows2_stored, 16)

                for i in range(TT - 1):
                    store_rows(i)
                wait_filled(sp, ("out", TT - 1, 1))

                def load_gu(e, s):
                    for dst, w in zip(expert(s), (w_gate, w_up)):
                        sp.dma_start(dst, w[bass.ds(l, 1), bass.ds(e, 1)].rearrange("a e (k p) f -> p (a e k) f", p=P))\
                            .then_inc(gu_landed[s], 16)

                def load_d(e, s):
                    sp.dma_start(expert(s)[2], w_down[bass.ds(l, 1), bass.ds(e, 1)]
                                 .rearrange("a e (k p) f -> p (a e k) f", p=P)).then_inc(d_landed[s], 16)

                load_gu(0, 0)
                load_d(0, 0)
                store_rows(TT - 1)
                sp.wait_ge(ada_used, MODS)
                load_gu(1, 1)
                load_d(1, 1)
                pairs = pairs_of(sp)
                sp.wait_ge(y_cleared, 16 * OTHERS)

                def store(t, s):
                    sp.wait_ge(y_taken, t * 2 + 10)
                    sp.sem_inc(sp_passed, 1)
                    sp.dma_start(y_rows[bass.ds(t * P, P), :], ysb[s]).then_inc(y_stored[s], 16)

                with sp.Fori(1, pairs) as pair:
                    experts = [sp.value_load(expert_of[0:1, bass.ds(pair * 2 + s, 1)], min_val=0, max_val=NE - 1)
                               for s in range(2)]
                    for s in range(2):
                        sp.wait_ge(gu_filled, pair * 2 + (s - 1))
                        sp.sem_inc(sp_passed, 1)
                        load_gu(experts[s], s)
                    for s in range(2):
                        sp.wait_ge(down_filled, pair * 4 + (2 * s + 2))
                        sp.sem_inc(sp_passed, 1)
                        load_d(experts[s], s)
                        store(pair * 2 + (s - 2), s)
                second = sp.value_load(next_i[0:1, bass.ds(after, 1)], min_val=0, max_val=DEPTH - 1)
                load_small(after, second, small_landed)
                sp.wait_ge(gu_filled, pairs * 2)
                sp.sem_inc(sp_passed, 1)
                load_columns(after, 0, small_landed)
                for s in range(2):
                    store(pairs * 2 + (s - 2), s)

                for counter, last in pair_totals(pairs).items():
                    sp.wait_ge(counter, last)
                    sp.sem_inc(sp_passed, 1)
                sp.sem_inc(sp_passed, 1)
                for counter, last in totals.items():
                    sp.wait_ge(counter, last)
                sp.wait_ge(layer_end, (l + 1) * 4)
                sp.sem_inc(layer_passed, 1)
                sp.sem_clear(range(first_layer_sem.num, last_layer_sem.num + 1))
                sp.sem_inc(layer_go, 1)
            sp.dma_start(gtB[:, :], g_final.rearrange("(a n) -> a n", a=1).partition_broadcast(P)).then_inc(consts_landed, 16)
            for i in range(TT):
                sp.wait_ge(fin_rows, i + 1)
                sp.dma_start(out.rearrange("b (i p) d -> p (b i) d", p=P)[:, i, :], tok[:, i, :]).then_inc(stored, 16)
            sp.wait_ge(stored, 16 * TT)


_INS = ["x", "c", "w_ada", "b_ada", "g_norm1", "w_in", "b_forget", "g_q_mla", "w_q_up", "g_kv_mla", "w_kv_up",
        "sinks", "w_out", "g_norm2", "w_router", "b_router", "w_gate", "w_up", "w_down", "g_final"]


def kernel(**inputs):
    import concourse.bacc as _bacc
    from concourse.bass_utils import run_bass_kernel_spmd as _run

    nc = _bacc.Bacc("TRN2", target_bir_lowering=False, num_devices=1)
    arrays, args = {}, []
    given = {name: np.ascontiguousarray(inputs[name]) for name in _INS}
    given.update(constants())
    for name, a in given.items():
        arrays[f"in_{name}"] = a
        args.append(nc.dram_tensor(f"in_{name}", a.shape, mybir.dt.from_np(a.dtype), kind="ExternalInput").ap())
    args.append(nc.dram_tensor("out_0", (1, SEQ, D), F32, kind="ExternalOutput").ap())
    trunk(nc, *args)
    r = _run(nc, [arrays], core_ids=[0])
    return r.results[0]["out_0"]
```
